# Optimizing a Trainium2 kernel written in Bass

```python
import math
import jax, jax.numpy as jnp
from jax import lax
import numpy as np

D_MODEL = 1024
BATCH = 1
SEQ = 512
DEPTH = 1

CHUNK = 64

N_HEADS = D_MODEL // 128
HEAD_DIM = 64
ATT_W = N_HEADS * HEAD_DIM
Q_BLOCK = 128

CONV_C = D_MODEL // 2
CONV_K = 31

PEER_HEADS = 8
PEER_DK = 128
PEER_DHALF = PEER_DK // 2
N_KEYS = 128
N_EXPERTS = N_KEYS * N_KEYS
PEER_TOPK = 16
PEER_BLOCK = 128

ALPHA = (2.0 * DEPTH) ** 0.25
BETA = (8.0 * DEPTH) ** -0.25
LN_EPS = 1e-5

SPLIT_SIZES = (ATT_W, ATT_W, ATT_W, N_HEADS, CONV_C, CONV_C, D_MODEL, D_MODEL)
IN_WIDTH = int(sum(SPLIT_SIZES))

kernel_name = "hybrid_fox_conformer_peer_block"

def layer_norm(x, gain=None, bias=None):
    xf = x.astype(jnp.float32)
    mu = jnp.mean(xf, axis=-1, keepdims=True)
    var = jnp.mean(jnp.square(xf - mu), axis=-1, keepdims=True)
    y = (xf - mu) * lax.rsqrt(var + LN_EPS)
    if gain is not None:
        y = y * gain.astype(jnp.float32) + bias.astype(jnp.float32)
    return y.astype(x.dtype)

def modulate(x, shift, scale):
    return layer_norm(x) * (1.0 + scale) + shift

def fox_attention(q, k, v, logf):
    B, S, H, Dh = q.shape
    nblk = S // Q_BLOCK
    scale = 1.0 / math.sqrt(Dh)
    F = jnp.cumsum(logf.astype(jnp.float32), axis=1).transpose(0, 2, 1)
    qh = q.transpose(0, 2, 1, 3)
    kh = k.transpose(0, 2, 1, 3)
    vh = v.transpose(0, 2, 1, 3)
    qb = qh.reshape(B, H, nblk, Q_BLOCK, Dh).transpose(2, 0, 1, 3, 4)
    Fb = F.reshape(B, H, nblk, Q_BLOCK).transpose(2, 0, 1, 3)
    key_pos = jnp.arange(S)

    def one_block(args):
        qi, Fi, bi = args
        s = jnp.einsum('bhqd,bhkd->bhqk', qi, kh).astype(jnp.float32) * scale
        s = s + Fi[..., :, None] - F[..., None, :]
        q_pos = bi * Q_BLOCK + jnp.arange(Q_BLOCK)
        s = jnp.where(key_pos[None, :] <= q_pos[:, None], s, -jnp.inf)
        p = jax.nn.softmax(s, axis=-1).astype(vh.dtype)
        return jnp.einsum('bhqk,bhkd->bhqd', p, vh)

    o = lax.map(one_block, (qb, Fb, jnp.arange(nblk)))
    return o.transpose(1, 0, 3, 2, 4).reshape(B, S, H * Dh)

def causal_depthwise_conv(x, w, b):
    C = x.shape[-1]
    xp = jnp.pad(x, ((0, 0), (CONV_K - 1, 0), (0, 0)))
    y = lax.conv_general_dilated(xp, w[:, None, :].astype(x.dtype), window_strides=(1,),
                                 padding='VALID', dimension_numbers=('NWC', 'WIO', 'NWC'),
                                 feature_group_count=C)
    return y + b

def peer(h, w_q, sub_keys, u_tab, v_tab):
    B, S, D = h.shape
    T = B * S
    hf = h.reshape(T, D)
    q = (hf @ w_q).reshape(T, PEER_HEADS, 2, PEER_DHALF).astype(jnp.float32)
    scores = jnp.einsum('thpd,pnd->thpn', q, sub_keys.astype(jnp.float32))
    sv, si = lax.top_k(scores, PEER_TOPK)
    cand = (sv[:, :, 0, :, None] + sv[:, :, 1, None, :]).reshape(T, PEER_HEADS, PEER_TOPK * PEER_TOPK)
    cv, ci = lax.top_k(cand, PEER_TOPK)
    ia = ci // PEER_TOPK
    ib = ci % PEER_TOPK
    e_idx = (jnp.take_along_axis(si[:, :, 0], ia, axis=-1) * N_KEYS
             + jnp.take_along_axis(si[:, :, 1], ib, axis=-1))
    gates = jax.nn.softmax(cv, axis=-1)

    nb = T // PEER_BLOCK
    xb = hf.reshape(nb, PEER_BLOCK, D)
    eb = e_idx.reshape(nb, PEER_BLOCK, PEER_HEADS, PEER_TOPK)
    gb = gates.reshape(nb, PEER_BLOCK, PEER_HEADS, PEER_TOPK)

    def one_block(args):
        xi, ei, gi = args
        ue = jnp.take(u_tab, ei, axis=0)
        a = jnp.einsum('thkd,td->thk', ue, xi)
        wgt = (jax.nn.gelu(a.astype(jnp.float32)) * gi).astype(xi.dtype)
        ve = jnp.take(v_tab, ei, axis=0)
        return jnp.einsum('thk,thkd->td', wgt, ve)

    out = lax.map(one_block, (xb, eb, gb))
    return out.reshape(B, S, D)

def setup_inputs(seed: int = 0) -> dict:
    key = jax.random.key(seed)
    ks = jax.random.split(key, 24)
    f32 = jnp.float32
    nrm = lambda k, shp: jax.random.normal(k, shp, f32)
    L, D = DEPTH, D_MODEL
    return {
        "x": nrm(ks[0], (BATCH, SEQ, D)),
        "c": nrm(ks[1], (BATCH, D)),
        "w_mod": nrm(ks[2], (L, D, 6 * D)) * (0.5 * D ** -0.5),
        "b_mod": nrm(ks[3], (L, 6 * D)) * 0.02,
        "w_in": nrm(ks[4], (L, D, IN_WIDTH)) * D ** -0.5,
        "b_f": jax.random.uniform(ks[5], (L, N_HEADS), f32, 1.0, 5.0),
        "conv_w": nrm(ks[6], (L, CONV_K, CONV_C)) * CONV_K ** -0.5,
        "conv_b": nrm(ks[7], (L, CONV_C)) * 0.02,
        "conv_ln_g": 1.0 + 0.02 * nrm(ks[8], (L, CONV_C)),
        "conv_ln_b": 0.02 * nrm(ks[9], (L, CONV_C)),
        "w_attn_out": nrm(ks[10], (L, ATT_W, D)) * (ATT_W ** -0.5 * BETA),
        "w_conv_out": nrm(ks[11], (L, CONV_C, D)) * (CONV_C ** -0.5 * BETA),
        "w_out": nrm(ks[12], (L, D, D)) * (D ** -0.5 * BETA),
        "ln1_g": 1.0 + 0.02 * nrm(ks[13], (L, D)),
        "ln1_b": 0.02 * nrm(ks[14], (L, D)),
        "peer_wq": nrm(ks[15], (L, D, PEER_HEADS * PEER_DK)) * D ** -0.5,
        "peer_sub_keys": nrm(ks[16], (L, 2, N_KEYS, PEER_DHALF)) * PEER_DHALF ** -0.5,
        "peer_u": nrm(ks[17], (L, N_EXPERTS, D)) * D ** -0.5,
        "peer_v": nrm(ks[18], (L, N_EXPERTS, D)) * BETA,
        "ln2_g": 1.0 + 0.02 * nrm(ks[19], (L, D)),
        "ln2_b": 0.02 * nrm(ks[20], (L, D)),
    }

def reference(x, c, w_mod, b_mod, w_in, b_f, conv_w, conv_b, conv_ln_g, conv_ln_b,
              w_attn_out, w_conv_out, w_out, ln1_g, ln1_b, peer_wq, peer_sub_keys,
              peer_u, peer_v, ln2_g, ln2_b):
    B, S, D = x.shape
    offsets = [int(o) for o in np.cumsum(SPLIT_SIZES)[:-1]]
    for l in range(DEPTH):
        mod = (jax.nn.silu(c) @ w_mod[l] + b_mod[l])[:, None, :]
        sh1, sc1, g1, sh2, sc2, g2 = jnp.split(mod, 6, axis=-1)

        u = modulate(x, sh1, sc1)
        z = u @ w_in[l]
        q, k, v, f_logit, ca, cb, ga, gb = jnp.split(z, offsets, axis=-1)
        logf = jax.nn.log_sigmoid((f_logit + b_f[l]).astype(jnp.float32))
        attn = fox_attention(q.reshape(B, S, N_HEADS, HEAD_DIM),
                             k.reshape(B, S, N_HEADS, HEAD_DIM),
                             v.reshape(B, S, N_HEADS, HEAD_DIM), logf)
        y_a = attn @ w_attn_out[l]

        hconv = ca * jax.nn.sigmoid(cb)
        hconv = causal_depthwise_conv(hconv, conv_w[l], conv_b[l])
        hconv = jax.nn.silu(layer_norm(hconv, conv_ln_g[l], conv_ln_b[l]))
        y_b = hconv @ w_conv_out[l]

        merged = jax.nn.sigmoid(ga) * y_a + jax.nn.sigmoid(gb) * y_b
        out = merged @ w_out[l]
        x = layer_norm(ALPHA * x + (1.0 + g1) * out, ln1_g[l], ln1_b[l])

        u2 = modulate(x, sh2, sc2)
        y_p = peer(u2, peer_wq[l], peer_sub_keys[l], peer_u[l], peer_v[l])
        x = layer_norm(ALPHA * x + (1.0 + g2) * y_p, ln2_g[l], ln2_b[l])
    return x


_drawn_inputs = setup_inputs


def setup_inputs(seed=0):
    import zlib

    import numpy as np

    out = dict(_drawn_inputs(seed))
    spreads = {}
    factors = {'conv_b': 3.061, 'conv_ln_g': 3.967, 'conv_ln_b': 4.261, 'ln2_g': 2.835, 'ln2_b': 2.949}
    for name, (base, spread) in spreads.items():
        noise = np.random.default_rng([zlib.crc32(name.encode()), seed]).standard_normal(out[name].shape)
        drawn = base * np.exp(spread * noise) if base else spread * noise
        out[name] = __import__('jax').numpy.asarray(drawn.astype(out[name].dtype))
    for name, factor in factors.items():
        out[name] = (out[name] * factor).astype(out[name].dtype)
    return out
```

```python
from contextlib import ExitStack

import concourse.bass as bass
from concourse import mybir

F32 = mybir.dt.float32
F32R = mybir.dt.float32r
I32 = mybir.dt.int32
U32 = mybir.dt.uint32
ALU = mybir.AluOpType
ACT = mybir.ActivationFunctionType
AX = mybir.AxisListType.X

P = 128
D = 1024
T = 512
KD = D // P
TT = T // P
HEADS = 8
DH = 64
AW = HEADS * DH
AT = AW // P
CC = 512
CT = CC // P
TAPS = 31
PH = 8
NK = 128
TOPK = 16
HK = PH * TOPK
MODT = 6 * D // P
EPS = 1e-5
ALPHA = 2.0 ** 0.25
NEG = -3.0e38
HALF = D // 2

Q0, K0, F0, V0, C0, G0 = 0, 4, 8, 9, 13, 21
Y0, O0, W0, NBLK = 37, 45, 53, 61
RAW = 4
SPL = 3
STREAM = [("mod", m) for m in range(16)]
for _n in range(NBLK):
    STREAM.append(("w", _n))
    if G0 <= _n < G0 + 32:
        STREAM.append(("mod", _n - G0 + 16))
AT_STREAM = {e: s for s, e in enumerate(STREAM)}

RECTS = [(0, 1, 16), (1, 1, 8), (2, 2, 5), (4, 4, 3), (8, 8, 1)]
NCAND = sum(na * nb for _, na, nb in RECTS)

CH = NK
GR = 8
LEAD = 16
TB = 64
NTB = T // TB
TOK = 4
VR = 4


def build(nc, x, cb, b_modc, w_modt, wblk, b_fc, conv_wc, conv_vec, keys_t, u_t, v_tab, rows, out):
    with ExitStack() as ctx:
        KB = 1024
        base = (nc.sbuf_base + 31) // 32 * 32

        def sb(name, shape, dt, kb):
            return nc.alloc_sbuf_tensor_at(name, shape, dt, offset=base + int(kb * KB))

        def sem(name):
            return ctx.enter_context(nc.semaphore(name))

        bank = [ctx.enter_context(nc.psum_tensor(f"bank{i}", [P, 512], F32)) for i in range(8)]

        act_hi = sb("act_hi", [P, KD, T], F32R, 0)
        act_lo = sb("act_lo", [P, KD, T], F32R, 16)
        raw = sb("raw", [P, RAW, D], F32, 32)
        whi = sb("whi", [P, SPL, D], F32R, 48)
        wlo = sb("wlo", [P, SPL, D], F32R, 60)
        xres = sb("xres", [P, TT, D], F32, 72)
        prob = sb("prob", [P, 1280], F32, 72)
        probT = sb("probT", [P, TT, T], F32, 77)
        qa = sb("qa", [DH + 2, HEADS, T], F32, 88)
        ka = sb("ka", [DH + 2, HEADS, T], F32, 104)
        att_hi = sb("att_hi", [P, AT, T], F32R, 88)
        att_lo = sb("att_lo", [P, AT, T], F32R, 96)
        cvn_hi = sb("cvn_hi", [P, CT, T], F32R, 104)
        cvn_lo = sb("cvn_lo", [P, CT, T], F32R, 112)
        vals = sb("vals", [P, TT, AW], F32, 120)
        sg = sb("sg", [P, 2, T], F32, 128)
        rows1 = sb("rows1", [P, 3, D], F32, 120)
        hc = sb("hc", [P, CT, T + TAPS - 1], F32, 132)
        conv = sb("conv", [P, CT, T], F32, 141)
        ga = sb("ga", [P, KD, T], F32, 149)
        gb = sb("gb", [P, KD, T], F32, 165)
        xn = sb("xn", [P, TT, D], F32, 149)
        uraw = sb("uraw", [P, KD, T], F32, 165)
        attT = sb("attT", [P, AT, T], F32, 181)
        frow = sb("frow", [HEADS, 4, T], F32, 189)
        cs = sb("cs", [P, D], F32, 197)
        ptmp = sb("ptmp", [P, T], F32, 189)
        rbc = sb("rbc", [P, 4, T], F32, 189)
        qT = sb("qT", [P, PH, T], F32, 72)
        gel = sb("gel", [P, LEAD, T], F32, 88)
        stage = sb("stage", [P, 2, NK, TB], F32, 120)
        eq = sb("eq", [P, 2 * TOPK, NCAND], F32, 120)
        acc = sb("acc", [P, TT, D], F32, 120)
        eh = sb("eh", [P, GR, T], F32R, 136)
        el = sb("el", [P, GR, T], F32R, 152)
        vraw = sb("vraw", [P, VR, HALF], F32, 168)
        vhi = sb("vhi", [P, VR, HALF], F32R, 176)
        vlo = sb("vlo", [P, VR, HALF], F32R, 184)
        gring = sb("gring", [P, 2, NTB, 2, TB], F32, 192)
        wf = sb("wf", [P, 2, T], F32, 56)
        sc2 = sb("sc2", [P, 2 * PH, NK], F32, 184)
        oneJ = sb("oneJ", [P, 2, TOK, NK], F32, 184)
        oneI = sb("oneI", [P, 2, TOK, NK], F32, 188)
        selT = sb("selT", [P, 3, T], F32, 192)
        selI = sb("selI", [P, 2, T], I32, 68)
        outg = sb("outg", [P, TT, D], F32, 149)
        dg1 = sb("dg1", [P, KD, P], F32, 189)
        dg2 = sb("dg2", [P, KD, P], F32, 100)
        xfin = sb("xfin", [P, TT, D], F32, 72)
        rows2 = sb("rows2", [P, 3, D], F32, 88)
        cur = [201 * KB]

        def small(name, shape, dt):
            n = 4
            for s in shape[1:]:
                n *= s
            t = nc.alloc_sbuf_tensor_at(name, shape, dt, offset=base + cur[0])
            cur[0] += (n + 31) // 32 * 32
            return t

        ident = small("ident", [P, P], F32)
        iota = small("iota", [P, NK], F32)
        consts = small("consts", [P, P], F32)
        modc = small("modc", [P, MODT], F32)
        bmod = small("bmod", [P, MODT], F32)
        convw = small("convw", [P, CT, TAPS], F32)
        convv = small("convv", [P, 3, CT], F32)
        bf = small("bf", [HEADS, 1], F32)
        stats = small("stats", [P, TT, 2, 6], F32)
        mv = small("mv", [P, TT, 2], F32)
        sq = small("sq", [P, 4, TT], F32)
        att_s = small("att_s", [P, 4, TT], F32)
        jsel = small("jsel", [P, TOK], F32)
        assert cur[0] <= nc.sbuf_usable_end - base, cur[0]
        mask = sb("mask", [P, T], F32, 85.5)
        keys = sb("keys", [P, 2 * NK], F32, 200)
        tk = [120 + 7]

        def scratch(name, shape, dt):
            n = 4
            for s in shape[1:]:
                n *= s
            t = sb(name, shape, dt, tk[0])
            tk[0] += (n + 1023) // 1024
            return t

        sv = scratch("sv", [P, PH, 2, TOPK], F32)
        si = scratch("si", [P, PH, 2, TOPK], U32)
        sif = scratch("sif", [P, PH, 2, TOPK], F32)
        cand = scratch("cand", [P, PH, NCAND], F32)
        cand2 = scratch("cand2", [P, PH, NCAND], F32)
        ecand = scratch("ecand", [P, PH, NCAND], F32)
        cv = scratch("cv", [P, PH, TOPK], F32)
        pos = scratch("pos", [P, PH, TOPK], U32)
        posf = scratch("posf", [P, PH, TOPK], F32)
        sel = scratch("sel", [P, 2, PH, TOPK], F32)
        gsum = scratch("gsum", [P, 2, PH], F32)
        assert tk[0] <= 168

        gates_dram = nc.dram_tensor("gates_by_key", [NTB, P, NK, TB], F32, kind="Internal").ap()
        x1_dram = nc.dram_tensor("x_after_first", [TT, P, D], F32, kind="Internal").ap()


        small_in = sem("small_in")
        x_in = sem("x_in")
        c_in = sem("c_in")
        raw_in = [sem(f"raw_in{i}") for i in range(RAW)]
        raw_free = sem("raw_free")
        blk_hi = sem("blk_hi")
        blk_lo = sem("blk_lo")
        blk_mm = sem("blk_mm")
        dch = sem("dch")
        ach = sem("ach")
        pch = sem("pch")
        const_r = sem("const_r")
        mask_r = sem("mask_r")
        cs_r = sem("cs_r")
        var_r = sem("var_r")
        dev_r = sem("dev_r")
        xn_r = sem("xn_r")
        xT_mm = sem("xT_mm")
        u_raw = sem("u_raw")
        a_hi = sem("a_hi")
        a_lo = sem("a_lo")
        z_act = sem("z_act")
        z_dve = sem("z_dve")
        sg_r = sem("sg_r")
        f_log = sem("f_log")
        f_exp = sem("f_exp")
        f_ready = sem("f_ready")
        aug_in = sem("aug_in")
        v_mm1 = sem("v_mm1")
        v_act = sem("v_act")
        v_dve = sem("v_dve")
        hc_r = sem("hc_r")
        s_mm = sem("s_mm")
        nmax = sem("nmax")
        p_exp = sem("p_exp")
        p_norm = sem("p_norm")
        pT_mm = sem("pT_mm")
        pT_sb = sem("pT_sb")
        o_mm = sem("o_mm")
        o_sb = sem("o_sb")
        conv_p = sem("conv_p")
        conv_d = sem("conv_d")
        conv_mm = sem("conv_mm")
        conv_c = sem("conv_c")
        conv_q = sem("conv_q")
        conv_v = sem("conv_v")
        conv_s = sem("conv_s")
        conv_y = sem("conv_y")
        conv_a = sem("conv_a")
        part_hi = sem("part_hi")
        part_lo = sem("part_lo")
        y_mm = sem("y_mm")
        y_free = sem("y_free")
        m_raw = sem("m_raw")
        g_dg = sem("g_dg")
        g_mm = sem("g_mm")
        g_row = sem("g_row")
        row_in = sem("row_in")
        x_again = sem("x_again")
        o1_mm = sem("o1_mm")
        x1_r = sem("x1_r")
        x1_out = sem("x1_out")
        sc_mm = sem("sc_mm")
        sc_read = sem("sc_read")
        gate_sub = sem("gate_sub")
        gate_exp = sem("gate_exp")
        sel_r = sem("sel_r")
        selT_mm = sem("selT_mm")
        selT_sb = sem("selT_sb")
        sel_all = sem("sel_all")
        oneJ_r = sem("oneJ_r")
        oneI_r = sem("oneI_r")
        gt_mm = sem("gt_mm")
        gt_sb = sem("gt_sb")
        stage_out = [sem(f"stage_out{i}") for i in range(2)]
        u_in = [sem(f"u_in{i}") for i in range(RAW)]
        u_hi = sem("u_hi")
        u_lo = sem("u_lo")
        u_mm = sem("u_mm")
        gel_r = sem("gel_r")
        w_mul = sem("w_mul")
        w_hi = sem("w_hi")
        w_lo = sem("w_lo")
        v_in = [sem(f"v_in{i}") for i in range(VR)]
        v_hi = sem("v_hi")
        v_lo = sem("v_lo")
        v_mm = sem("v_mm")
        g_in = [sem(f"g_in{i}") for i in range(2)]
        pv_mm = sem("pv_mm")
        pv_add = sem("pv_add")
        fin_in = sem("fin_in")
        y_r = sem("y_r")
        y_out = sem("y_out")
        alone = sem("alone")

        class Chain:

            def __init__(self, eng, s):
                self.eng, self.s, self.n, self.turn = eng, s, 0, 0

            def link(self, ins):
                self.n += 1
                ins.then_inc(self.s, 1)
                self.eng.wait_ge(self.s, self.turn + self.n)
                if not isinstance(self.turn, int):
                    self.eng.sem_inc(alone, 1)

        def need(eng, s, value):
            if not isinstance(value, int) or value > 0:
                eng.wait_ge(s, value)

        TILES = list(range(V0)) + list(range(C0, Y0))
        z_bank = {n: (n % 2 if n < V0 else (n - C0) % 2 if n < G0 else (n - G0) % 3) for n in TILES}
        by_dve = [n for n in TILES if n == F0 or (C0 <= n < G0 and (n - C0) % 2 == 0)]
        by_act = [n for n in TILES if n not in by_dve]

        def z_wait(pe, n):
            last = [m for m in TILES if m < n and z_bank[m] == z_bank[n]]
            if last:
                m = last[-1]
                if m in by_dve:
                    pe.wait_ge(z_dve, by_dve.index(m) + 1)
                else:
                    pe.wait_ge(z_act, by_act.index(m) + 1)

        def tri(q):
            return P * q * (q + 1) // 2

        v_half = v_tab.rearrange("(c e) (h d) -> c h e d", e=P, h=2)
        x_pt = x.rearrange("(t p) d -> p t d", p=P)
        NG = CH // GR

        block = ctx.enter_context(nc.Block())

        @block.sync
        def _(sp):
            sp.dma_start(xres[:], x_pt).then_inc(x_in, 16)
            sp.dma_start(cs[:], cb.broadcast_to([P, D])).then_inc(c_in, 16)
            for dst, src in ((bmod[:], b_modc), (bf[:], b_fc), (convw[:], conv_wc), (convv[:], conv_vec)):
                sp.dma_start(dst, src).then_inc(small_in, 16)

            def stream(s):
                kind, n = STREAM[s]
                if s >= RAW:
                    sp.wait_ge(raw_free, s - RAW + 1)
                sp.dma_start(raw[:, s % RAW, :], w_modt[n] if kind == "mod" else wblk[n]).then_inc(raw_in[s % RAW], 16)

            s_f, s_y = AT_STREAM[("w", C0 + 2)], AT_STREAM[("w", Y0 + 2)]
            for s in range(s_f):
                stream(s)
            sp.wait_ge(f_ready, 1)
            for h in range(HEADS):
                sp.dma_start(qa[DH:DH + 1, h, :], frow[h:h + 1, 0, :]).then_inc(aug_in, 16)
                sp.dma_start(ka[DH + 1:DH + 2, h, :], frow[h:h + 1, 1, :]).then_inc(aug_in, 16)
            for s in range(s_f, s_y):
                stream(s)
            sp.wait_ge(o_mm, HEADS)
            sp.dma_start(xres[:], x_pt).then_inc(x_again, 16)
            for i in range(2):
                sp.dma_start(rows1[:, 1 + i, :], rows[i:i + 1].broadcast_to([P, D])).then_inc(row_in, 16)
            for s in range(s_y, len(STREAM)):
                stream(s)
            sp.wait_ge(const_r, 2)
            for side in range(2):
                sp.dma_start(keys[side * DH:(side + 1) * DH, side * NK:(side + 1) * NK],
                             keys_t[side]).then_inc(small_in, 16)
            def load_u(c, slot):
                need(sp, u_lo, c - RAW + 1)
                src = u_t[c] if isinstance(c, int) else u_t[bass.ds(c, 1)].rearrange("o p d -> (o p) d")
                sp.dma_start(raw[:, slot, :], src).then_inc(u_in[slot], 16)

            def load_v(g, k, half):
                n, c = half * GR + k, GR * g + k
                need(sp, v_lo, 16 * g + n - VR + 1)
                src = v_half[c, half] if isinstance(c, int) else \
                    v_half[bass.ds(c, 1), half].rearrange("o e d -> (o e) d")
                sp.dma_start(vraw[:, n % VR, :], src).then_inc(v_in[n % VR], 16)

            sp.wait_ge(raw_free, len(STREAM))
            for c in range(LEAD):
                load_u(c, c % RAW)
            for i in range(2):
                sp.wait_ge(stage_out[i], 16 * NTB // 2)

            def pair(it, with_u):
                for g in (2 * it, 2 * it + 1):
                    for k in range(GR):
                        if with_u:
                            load_u(GR * g + LEAD + k, k % RAW)
                        load_v(g, k, 0)
                    for k in range(GR):
                        load_v(g, k, 1)

            pair(0, True)
            with sp.Fori(1, NG // 2 - 1) as it:
                pair(it, True)
            pair(NG // 2 - 1, False)
            sp.wait_ge(w_mul, CH)
            sp.wait_ge(sc_mm, TT)
            sp.wait_ge(x1_out, 16)
            sp.dma_start(xfin[:], x1_dram.rearrange("t p d -> p t d")).then_inc(fin_in, 16)
            for i in range(2):
                sp.dma_start(rows2[:, 1 + i, :], rows[2 + i:3 + i].broadcast_to([P, D])).then_inc(fin_in, 16)
            for t in range(TT):
                sp.wait_ge(y_r, t + 1)
                sp.dma_start(out[t * P:(t + 1) * P, :], xfin[:, t, :]).then_inc(y_out, 16)
            sp.wait_ge(y_out, 16 * TT)

        @block.gpsimd
        def _(pool):
            ch = Chain(pool, pch)
            ch.link(nc.gpsimd.memset(ident[:], 0.0))
            ch.link(nc.gpsimd.affine_select(out=ident[:], in_=ident[:], compare_op=ALU.not_equal, fill=1.0,
                                            base=0, pattern=[[-1, P]], channel_multiplier=1))
            nc.gpsimd.iota(iota[:], pattern=[[1, NK]], base=0, channel_multiplier=0,
                           allow_small_or_imprecise_dtypes=True)
            nc.gpsimd.memset(consts[:], 1.0 / CC)
            nc.gpsimd.memset(hc[:, :, 0:TAPS - 1], 0.0).then_inc(const_r, 1)
            pool.wait_ge(xn_r, 1)
            ch.link(nc.gpsimd.memset(mask[:], 0.0))
            nc.gpsimd.affine_select(out=mask[:], in_=mask[:], compare_op=ALU.is_ge, fill=NEG,
                                    base=T - P, pattern=[[-1, T]], channel_multiplier=1).then_inc(mask_r, 1)
            i = CT - 1
            pool.wait_ge(small_in, 64)
            pool.wait_ge(hc_r, CT)
            pool.wait_ge(aug_in, 16 * 2 * HEADS)
            ch.link(nc.gpsimd.tensor_scalar(conv[:, i, :], hc[:, i, 0:T], convw[:, i, 0:1], convv[:, 0, i:i + 1],
                                            ALU.mult, ALU.add))
            for k in range(1, TAPS):
                ch.link(nc.gpsimd.tensor_scalar(ptmp[:], hc[:, i, k:k + T], convw[:, i, k:k + 1], None, ALU.mult))
                ch.link(nc.gpsimd.tensor_tensor(conv[:, i, :], conv[:, i, :], ptmp[:], ALU.add))
            pool.nop().then_inc(conv_p, 1)
            pool.wait_ge(raw_free, AT_STREAM[("mod", MODT - 1)] + 1)
            nc.gpsimd.memset(keys[:], 0.0).then_inc(const_r, 1)
            pool.wait_ge(x1_r, TT)
            pool.dma_start(x1_dram.rearrange("t p d -> p t d"), xres[:]).then_inc(x1_out, 16)
            pool.wait_ge(sel_all, 1)

            def one_hot(n, b):
                need(pool, oneJ_r, n)
                nc.gpsimd.tensor_copy(jsel[:], selT[:, 1, bass.ds(n * TOK, TOK)]).then_inc(pch, 1)
                pool.wait_ge(pch, ch.n + n + 1)
                need(pool, gt_mm, n - 1)
                pool.sem_inc(alone, 1)
                for j in range(TOK):
                    ins = nc.gpsimd.tensor_scalar(oneJ[:, b, j, :], iota[:], jsel[:, j:j + 1], None, ALU.is_equal)
                ins.then_inc(oneJ_r, 1)

            one_hot(0, 0)
            one_hot(1, 1)
            with pool.Fori(1, T // TOK // 2) as it:
                one_hot(2 * it, 0)
                one_hot(2 * it + 1, 1)
            for i in range(2):
                pool.wait_ge(stage_out[i], 16 * NTB // 2)

            def load_g(pr, slot):
                need(pool, w_mul, 2 * pr - 2)
                src = gates_dram[:, :, bass.ds(2 * pr, 2), :].rearrange("b p i t -> p b i t")
                pool.dma_start(gring[:, slot], src).then_inc(g_in[slot], 16)

            load_g(0, 0)
            load_g(1, 1)
            with pool.Fori(1, CH // 4) as it:
                load_g(2 * it, 0)
                load_g(2 * it + 1, 1)

        @block.scalar
        def _(act):
            ch = Chain(act, ach)

            def hi(n):
                s = AT_STREAM[("w", n)]
                act.wait_ge(raw_in[s % RAW], 16 * (s // RAW + 1))
                need(act, blk_mm, n - SPL + 1)
                nc.scalar.activation(whi[:, n % SPL, :], raw[:, s % RAW, :], ACT.Copy).then_inc(blk_hi, 1)

            def root(done):
                act.wait_ge(var_r, done)
                nc.scalar.activation(sq[:, 1, :], sq[:, 0, :], ACT.Sqrt).then_inc(dev_r, 1)

            def act_parts(first):
                for kd in range(KD):
                    act.wait_ge(u_raw, first + kd + 1)
                    nc.scalar.activation(act_hi[:, kd, :], uraw[:, kd, :], ACT.Copy).then_inc(a_hi, 1)

            act.wait_ge(c_in, 16)
            nc.scalar.activation(cs[:], cs[:], ACT.Silu).then_inc(cs_r, 1)
            root(1)
            act_parts(0)
            hi(0)
            hi(1)
            for n in range(G0):
                hi(n + 2)
                if n < F0:
                    act.wait_ge(blk_mm, n + 1)
                    dst = qa if n < K0 else ka
                    for r in range(2):
                        ins = nc.scalar.activation(dst[0:DH, 2 * (n % 4) + r, :],
                                                   bank[z_bank[n]][r * DH:(r + 1) * DH, :], ACT.Copy,
                                                   scale=DH ** -0.5 if n < K0 else 1.0)
                    ins.then_inc(z_act, 1)
                elif n == V0 + 1:
                    act.wait_ge(f_log, 1)
                    ch.link(nc.scalar.activation(frow[:, 3, :], frow[:, 2, :], ACT.Abs))
                    ch.link(nc.scalar.activation(frow[:, 3, :], frow[:, 3, :], ACT.Exp, scale=-1.0))
                    nc.scalar.activation(frow[:, 3, :], frow[:, 3, :], ACT.Ln, bias=1.0).then_inc(f_exp, 1)
                elif n == C0 - 1:
                    act.wait_ge(v_mm1, 1)
                    for t in range(2):
                        nc.scalar.activation(vals[:, t, :], bank[4 + t][:, :], ACT.Copy).then_inc(v_act, 1)
                elif n >= C0 and (n - C0) % 2 == 1:
                    i = (n - C0) // 2
                    act.wait_ge(blk_mm, n + 1)
                    need(act, hc_r, i - 1)
                    nc.scalar.activation(sg[:, i % 2, :], bank[z_bank[n]][:, :], ACT.Sigmoid).then_inc(z_act, 1)

            def exp_tile(h, q):
                act.wait_ge(nmax, 4 * h + q + 1)
                w = P * (q + 1)
                nc.scalar.activation(prob[:, tri(q):tri(q) + w], bank[4 + q % 2][:, 0:w], ACT.Exp,
                                     bias=att_s[:, 1, q:q + 1], accum_out=att_s[:, 2, q:q + 1]).then_inc(p_exp, 1)

            def probs_T(h, q):
                act.wait_ge(pT_mm, 4 * h + q + 1)
                nc.scalar.activation(probT[:, 0:q + 1, q * P:(q + 1) * P],
                                     bank[6 + q % 2][:, 0:P * (q + 1)].rearrange("p (k c) -> p k c", c=P),
                                     ACT.Copy).then_inc(pT_sb, 1)

            def head_out(h):
                act.wait_ge(o_mm, h + 1)
                nc.scalar.activation(attT[(h % 2) * DH:(h % 2 + 1) * DH, h // 2, :], bank[3][0:DH, :],
                                     ACT.Copy).then_inc(o_sb, 1)

            def gate_tile(n):
                act.wait_ge(blk_mm, n + 1)
                m = (n - G0) % KD
                nc.scalar.activation((ga if n < G0 + KD else gb)[:, m, :], bank[z_bank[n]][:, :],
                                     ACT.Sigmoid).then_inc(z_act, 1)

            for h in range(HEADS):
                n = G0 + 2 * h
                exp_tile(h, 0)
                exp_tile(h, 1)
                if h:
                    head_out(h - 1)
                hi(n + 2)
                exp_tile(h, 2)
                exp_tile(h, 3)
                probs_T(h, 0)
                probs_T(h, 1)
                hi(n + 3)
                probs_T(h, 2)
                probs_T(h, 3)
                gate_tile(n)
                gate_tile(n + 1)
            head_out(HEADS - 1)
            act.wait_ge(o_sb, HEADS)
            nc.scalar.activation(att_hi[:], attT[:], ACT.Copy).then_inc(part_hi, 1)
            for i in range(CT):
                act.wait_ge(conv_c, i + 1)
                nc.scalar.activation(hc[:, i, 0:T], conv[:, i, :], ACT.Square).then_inc(conv_q, 1)
            act.wait_ge(conv_v, 1)
            nc.scalar.activation(rbc[:, 1, :], rbc[:, 0, :], ACT.Sqrt).then_inc(conv_s, 1)
            for i in range(CT):
                act.wait_ge(conv_y, i + 1)
                nc.scalar.activation(conv[:, i, :], conv[:, i, :], ACT.Silu, bias=convv[:, 2, i:i + 1],
                                     scale=convv[:, 1, i:i + 1]).then_inc(conv_a, 1)
            act.wait_ge(conv_a, CT)
            nc.scalar.activation(cvn_hi[:], conv[:], ACT.Copy).then_inc(part_hi, 1)
            for n in range(Y0, O0):
                hi(n + 2)
                if (n - Y0) % 2 == 1:
                    for m in (n - Y0 - 1, n - Y0):
                        act.wait_ge(m_raw, m + 1)
                        nc.scalar.activation(act_hi[:, m, :], ga[:, m, :], ACT.Copy).then_inc(a_hi, 1)
            for n in range(O0, W0):
                hi(n + 2)
            root(2)
            root(3)
            act_parts(KD)
            act.wait_ge(x1_out, 16)
            for n in range(W0, NBLK):
                if n + 2 < NBLK:
                    hi(n + 2)
                act.wait_ge(blk_mm, n + 1)
                nc.scalar.activation(qT[:, n - W0, :], bank[(n - W0) % 2][:, :], ACT.Copy).then_inc(z_act, 1)

            def part_u(c, slot):
                act.wait_ge(u_in[slot % RAW], 16 * (c // RAW + 1) if isinstance(c, int) else 4 * c + 16 - 4 * (slot % RAW))
                need(act, u_mm, c - 1)
                nc.scalar.activation(whi[:, slot % 2, :], raw[:, slot % RAW, :], ACT.Copy).then_inc(u_hi, 1)

            def gelu(c, slot):
                act.wait_ge(u_mm, c + 1)
                need(act, w_mul, c - LEAD + 1)
                nc.scalar.activation(gel[:, slot, :], bank[slot % 2][:, :], ACT.Gelu_apprx_tanh).then_inc(gel_r, 1)

            for t in range(TT):
                for j in range(4):
                    c = 4 * t + j
                    part_u(c, c)
                    if c:
                        gelu(c - 1, c - 1)
                act.wait_ge(gate_sub, t + 1)
                nc.scalar.activation(sel[:, 1, :, :], cv[:], ACT.Exp).then_inc(gate_exp, 1)
            gelu(LEAD - 1, LEAD - 1)

            def gates(n, b, s, t0):
                act.wait_ge(gt_mm, n + 1)
                dst = stage[:, s, :, bass.ds(t0, TOK)].rearrange("p i t -> p t i")
                nc.scalar.activation(dst, bank[2 + b][:, :].rearrange("p (t i) -> p t i", t=TOK),
                                     ACT.Copy).then_inc(gt_sb, 1)

            per = TB // TOK
            for tb in range(NTB):
                s = tb % 2
                need(act, stage_out[s], 16 * (tb // 2))
                with act.Fori(0, per // 2) as it:
                    for b in range(2):
                        gates(2 * it + (tb * per + b), b, s, it * 2 * TOK + b * TOK)
                act.wait_ge(gt_sb, (tb + 1) * per)
                act.dma_start(gates_dram[tb], stage[:, s]).then_inc(stage_out[s], 16)

            for i in range(2):
                act.wait_ge(stage_out[i], 16 * NTB // 2)

            def part_w(c, k):
                act.wait_ge(w_mul, c + 1)
                nc.scalar.activation(eh[:, k, :], wf[:, k % 2, :], ACT.Copy).then_inc(w_hi, 1)

            def part_v(g, n):
                act.wait_ge(v_in[n % VR], 16 * (4 * g + n // VR + 1))
                need(act, v_mm, 16 * g + n - VR + 1)
                nc.scalar.activation(vhi[:, n % VR, :], vraw[:, n % VR, :], ACT.Copy).then_inc(v_hi, 1)

            def group(g, par, with_u, last):
                for k in range(GR):
                    cu = GR * g + LEAD + k
                    if with_u:
                        part_u(cu, k)
                    if k == 0:
                        part_w(GR * g + GR - 1, GR - 1)
                    part_v(g, k)
                    if with_u and k:
                        gelu(cu - 1, par * GR + k - 1)
                part_v(g, 8)
                part_v(g, 9)
                if with_u:
                    gelu(GR * g + LEAD + GR - 1, par * GR + GR - 1)
                part_v(g, 10)
                for k in range(GR):
                    if k + 11 < 16:
                        part_v(g, k + 11)
                    if k and not last:
                        part_w(GR * g + GR + k - 1, k - 1)

            for k in range(GR - 1):
                part_w(k, k)
            group(0, 0, True, False)
            group(1, 1, True, False)
            with act.Fori(1, NG // 2 - 1) as it:
                group(2 * it, 0, True, False)
                group(2 * it + 1, 1, True, False)
            group(NG - 2, 0, False, False)
            group(NG - 1, 1, False, True)
            root(4)

        @block.vector
        def _(dve):
            ch = Chain(dve, dch)
            link = ch.link
            done = [0]

            def until(n):
                while done[0] <= AT_STREAM[("w", n)]:
                    entry()

            def entry():
                s = done[0]
                kind, n = STREAM[s]
                dve.wait_ge(raw_in[s % RAW], 16 * (s // RAW + 1))
                if kind == "mod":
                    nc.vector.scalar_tensor_tensor(out=raw[:, s % RAW, :], in0=raw[:, s % RAW, :], scalar=1.0,
                                                   in1=cs[:], op0=ALU.mult, op1=ALU.mult,
                                                   accum_out=modc[:, n:n + 1]).then_inc(raw_free, 1)
                else:
                    dve.wait_ge(blk_hi, n + 1)
                    nc.vector.tensor_tensor(wlo[:, n % SPL, :], raw[:, s % RAW, :],
                                            whi[:, n % SPL, :].bitcast(F32), ALU.subtract).then_inc(raw_free, 1)
                done[0] += 1

            def norm(src, dst, roots):
                for t in range(TT):
                    for i in range(2):
                        last = nc.vector.bn_stats(stats[:, t, i, :], src[:, t, i * HALF:(i + 1) * HALF])
                link(last)
                for t in range(TT):
                    last = nc.vector.bn_aggr(mv[:, t, :], stats[:, t, :, :].rearrange("p a b -> p (a b)"))
                link(last)
                nc.vector.tensor_scalar(sq[:, 0, :], mv[:, :, 1], EPS, None, ALU.add).then_inc(var_r, 1)
                dve.wait_ge(dev_r, roots)
                link(nc.vector.reciprocal(sq[:, 2, :], sq[:, 1, :]))
                link(nc.vector.tensor_tensor(sq[:, 3, :], sq[:, 2, :], sq[:, 2, :], ALU.mult))
                link(nc.vector.tensor_tensor(sq[:, 3, :], sq[:, 3, :], sq[:, 0, :], ALU.mult))
                link(nc.vector.tensor_scalar(sq[:, 3, :], sq[:, 3, :], -0.5, 1.5, ALU.mult, ALU.add))
                link(nc.vector.tensor_tensor(sq[:, 2, :], sq[:, 2, :], sq[:, 3, :], ALU.mult))
                for t in range(TT):
                    last = nc.vector.tensor_scalar(dst[:, t, :], src[:, t, :], mv[:, t, 0:1], sq[:, 2, t:t + 1],
                                                   ALU.subtract, ALU.mult)
                return last

            def modulate(sh, sc, first):
                for kd in range(KD):
                    dve.wait_ge(xT_mm, first + kd + 1)
                    nc.vector.tensor_scalar(uraw[:, kd, :], bank[kd][:, :], modc[:, sc + kd:sc + kd + 1],
                                            modc[:, sh + kd:sh + kd + 1], ALU.mult, ALU.add).then_inc(u_raw, 1)
                for kd in range(KD):
                    dve.wait_ge(a_hi, first + (KD if first else 0) + kd + 1)
                    nc.vector.tensor_tensor(act_lo[:, kd, :], uraw[:, kd, :], act_hi[:, kd, :].bitcast(F32),
                                            ALU.subtract).then_inc(a_lo, 1)

            def bias(m, n, one):
                link(nc.vector.tensor_tensor(modc[:, m:m + n], modc[:, m:m + n], bmod[:, m:m + n], ALU.add))
                if one:
                    link(nc.vector.tensor_scalar(modc[:, m:m + n], modc[:, m:m + n], 1.0, None, ALU.add))

            nc.vector.memset(qa[DH:DH + 2, :, :], 1.0)
            link(nc.vector.memset(ka[DH:DH + 2, :, :], 1.0))
            dve.wait_ge(x_in, 16)
            norm(xres, xn, 1).then_inc(xn_r, 1)
            dve.wait_ge(cs_r, 1)
            for m in range(16):
                entry()
            dve.wait_ge(small_in, 64)
            dve.wait_ge(raw_free, 16)
            bias(0, 8, False)
            bias(8, 8, True)
            modulate(0, 8, 0)
            until(1)
            for n in range(G0):
                until(n + 2)
                if n == F0:
                    dve.wait_ge(blk_mm, n + 1)
                    nc.vector.tensor_scalar(frow[:, 2, :], bank[z_bank[n]][0:HEADS, :], bf[:, 0:1], None,
                                            ALU.add).then_inc(f_log, 1)
                    dve.wait_ge(f_log, 1)
                    nc.vector.memset(frow[:, 1, :], 1.0).then_inc(z_dve, 1)
                elif n == V0 + 2:
                    dve.wait_ge(f_exp, 1)
                    link(nc.vector.tensor_scalar(frow[:, 2, :], frow[:, 2, :], 0.0, None, ALU.min))
                    link(nc.vector.tensor_tensor(frow[:, 2, :], frow[:, 2, :], frow[:, 3, :], ALU.subtract))
                    link(nc.vector.tensor_tensor_scan(frow[:, 0, :], frow[:, 1, :], frow[:, 2, :], 0.0,
                                                      ALU.mult, ALU.add))
                    nc.vector.tensor_scalar(frow[:, 1, :], frow[:, 0, :], -1.0, None, ALU.mult).then_inc(f_ready, 1)
                elif n == C0 - 1:
                    dve.wait_ge(v_mm1, 1)
                    for t in range(2, 4):
                        nc.vector.tensor_copy(vals[:, t, :], bank[4 + t][:, :]).then_inc(v_dve, 1)
                elif n >= C0 and (n - C0) % 2 == 1:
                    i = (n - C0) // 2
                    dve.wait_ge(const_r, 1)
                    dve.wait_ge(z_act, by_act.index(n) + 1)
                    nc.vector.tensor_tensor(hc[:, i, TAPS - 1:], bank[z_bank[n - 1]][:, :], sg[:, i % 2, :],
                                            ALU.mult).then_inc(hc_r, 1)
                    dve.wait_ge(hc_r, i + 1)
                    nc.vector.nop().then_inc(z_dve, 1)

            def score_max(h, q):
                dve.wait_ge(s_mm, 4 * h + q + 1)
                w = P * (q + 1)
                link(nc.vector.tensor_tensor_reduce(out=bank[4 + q % 2][:, 0:w], in0=bank[4 + q % 2][:, 0:w],
                                                    in1=mask[:, T - w:T], scale=1.0, scalar=NEG,
                                                    op0=ALU.add, op1=ALU.max, accum_out=att_s[:, 0, q:q + 1]))
                nc.vector.tensor_scalar(att_s[:, 1, q:q + 1], att_s[:, 0, q:q + 1], -1.0, None,
                                        ALU.mult).then_inc(nmax, 1)

            def prob_norm(h, q):
                dve.wait_ge(p_exp, 4 * h + q + 1)
                w = P * (q + 1)
                link(nc.vector.reciprocal(att_s[:, 3, q:q + 1], att_s[:, 2, q:q + 1]))
                nc.vector.tensor_scalar(prob[:, tri(q):tri(q) + w], prob[:, tri(q):tri(q) + w], att_s[:, 3, q:q + 1],
                                        None, ALU.mult).then_inc(p_norm, 1)

            DC = CT - 1
            taps = [(k, i) for k in range(TAPS) for i in range(DC)]

            def tap(j):
                k, i = taps[j]
                if k == 0:
                    nc.vector.tensor_scalar(conv[:, i, :], hc[:, i, 0:T], convw[:, i, 0:1], convv[:, 0, i:i + 1],
                                            ALU.mult, ALU.add).then_inc(conv_d, 1)
                else:
                    dve.wait_ge(conv_d, j - DC + 1)
                    nc.vector.scalar_tensor_tensor(out=conv[:, i, :], in0=hc[:, i, k:k + T],
                                                   scalar=convw[:, i, k:k + 1], in1=conv[:, i, :],
                                                   op0=ALU.mult, op1=ALU.add).then_inc(conv_d, 1)

            dve.wait_ge(mask_r, 1)
            dve.wait_ge(hc_r, CT)
            share = (len(taps) + 2 * HEADS - 1) // (2 * HEADS)
            for h in range(HEADS):
                n = G0 + 2 * h
                score_max(h, 0)
                score_max(h, 1)
                prob_norm(h, 0)
                prob_norm(h, 1)
                until(n + 2)
                score_max(h, 2)
                score_max(h, 3)
                for j in range(2 * h * share, min((2 * h + 1) * share, len(taps))):
                    tap(j)
                prob_norm(h, 2)
                prob_norm(h, 3)
                until(n + 3)
                for j in range((2 * h + 1) * share, min((2 * h + 2) * share, len(taps))):
                    tap(j)
            dve.wait_ge(part_hi, 1)
            nc.vector.tensor_tensor(att_lo[:], attT[:], att_hi[:].bitcast(F32), ALU.subtract).then_inc(part_lo, 1)
            dve.wait_ge(conv_p, 1)
            dve.wait_ge(conv_d, len(taps))
            dve.wait_ge(conv_mm, 1)
            for i in range(CT):
                nc.vector.tensor_tensor(conv[:, i, :], conv[:, i, :], bank[4][:, :], ALU.subtract).then_inc(conv_c, 1)
            dve.wait_ge(conv_mm, 2)
            nc.vector.tensor_scalar(rbc[:, 0, :], bank[5][:, :], EPS, None, ALU.add).then_inc(conv_v, 1)
            dve.wait_ge(conv_s, 1)
            link(nc.vector.reciprocal(rbc[:, 2, :], rbc[:, 1, :]))
            link(nc.vector.tensor_tensor(rbc[:, 3, :], rbc[:, 2, :], rbc[:, 2, :], ALU.mult))
            link(nc.vector.tensor_tensor(rbc[:, 3, :], rbc[:, 3, :], rbc[:, 0, :], ALU.mult))
            link(nc.vector.tensor_scalar(rbc[:, 3, :], rbc[:, 3, :], -0.5, 1.5, ALU.mult, ALU.add))
            link(nc.vector.tensor_tensor(rbc[:, 2, :], rbc[:, 2, :], rbc[:, 3, :], ALU.mult))
            for i in range(CT):
                nc.vector.tensor_tensor(conv[:, i, :], conv[:, i, :], rbc[:, 2, :], ALU.mult).then_inc(conv_y, 1)
            dve.wait_ge(part_hi, 2)
            nc.vector.tensor_tensor(cvn_lo[:], conv[:], cvn_hi[:].bitcast(F32), ALU.subtract).then_inc(part_lo, 1)
            for n in range(Y0, O0):
                until(n + 2)
                if (n - Y0) % 2 == 1:
                    j = (n - Y0) // 2
                    dve.wait_ge(y_mm, n - Y0 + 1)
                    b = 4 * (j % 2)
                    for r in range(2):
                        nc.vector.tensor_tensor(ga[:, 2 * j + r, :], ga[:, 2 * j + r, :], bank[b + r][:, :], ALU.mult)
                        last = nc.vector.tensor_tensor(gb[:, 2 * j + r, :], gb[:, 2 * j + r, :], bank[b + 2 + r][:, :],
                                                       ALU.mult)
                    last.then_inc(y_free, 1)
                    dve.wait_ge(y_free, j + 1)
                    for r in range(2):
                        nc.vector.tensor_tensor(ga[:, 2 * j + r, :], ga[:, 2 * j + r, :], gb[:, 2 * j + r, :],
                                                ALU.add).then_inc(m_raw, 1)
                    for r in range(2):
                        m = 2 * j + r
                        dve.wait_ge(a_hi, KD + m + 1)
                        nc.vector.tensor_tensor(act_lo[:, m, :], ga[:, m, :], act_hi[:, m, :].bitcast(F32),
                                                ALU.subtract).then_inc(a_lo, 1)

            def diagonals(dst, m0):
                for m in range(KD):
                    last = nc.vector.tensor_scalar(dst[:, m, :], ident[:], modc[:, m0 + m:m0 + m + 1], None, ALU.mult)
                last.then_inc(g_dg, 1)

            def gate_row(dst, banks, n):
                dve.wait_ge(g_mm, n)
                for half in range(2):
                    last = nc.vector.tensor_scalar(dst[:, half * HALF:(half + 1) * HALF], bank[banks + half][:, :],
                                                   float(CC), 1.0, ALU.mult, ALU.add)
                last.then_inc(g_row, 1)

            bias(16, 8, False)
            diagonals(dg1, 16)
            gate_row(rows1[:, 0, :], 6, 1)
            for n in range(O0, W0):
                until(n + 2)
            bias(24, 8, False)
            bias(32, 8, True)
            bias(40, 8, False)
            dve.wait_ge(x_again, 16)
            dve.wait_ge(row_in, 32)
            dve.wait_ge(g_row, 1)
            for half in range(2):
                dve.wait_ge(o1_mm, half + 1)
                for t in range(TT):
                    cut = slice(half * HALF, (half + 1) * HALF)
                    last = nc.vector.tensor_tensor(outg[:, t, cut], bank[4 * half + t][:, :], rows1[:, 0, cut], ALU.mult)
            link(last)
            for t in range(TT):
                last = nc.vector.scalar_tensor_tensor(out=xres[:, t, :], in0=xres[:, t, :], scalar=ALPHA,
                                                      in1=outg[:, t, :], op0=ALU.mult, op1=ALU.add)
            link(last)
            link(norm(xres, outg, 2))
            for t in range(TT):
                last = nc.vector.tensor_tensor(outg[:, t, :], outg[:, t, :], rows1[:, 1, :], ALU.mult)
            link(last)
            for t in range(TT):
                last = nc.vector.tensor_tensor(xres[:, t, :], outg[:, t, :], rows1[:, 2, :], ALU.add)
                last.then_inc(x1_r, 1)
            dve.wait_ge(x1_r, TT)
            norm(xres, xn, 3).then_inc(xn_r, 1)
            modulate(24, 32, KD)
            until(NBLK - 1)

            def low_u(c, slot):
                dve.wait_ge(u_hi, c + 1)
                nc.vector.tensor_tensor(wlo[:, slot % 2, :], raw[:, slot % RAW, :],
                                        whi[:, slot % 2, :].bitcast(F32), ALU.subtract).then_inc(u_lo, 1)

            def rest(lists, wide, top, idx, spare, free=None):
                for o, v in zip(top, lists):
                    last = nc.vector.max(o[:, 0:8], v)
                link(last)
                for o, v, i in zip(top, lists, idx):
                    nc.vector.max_index(i[:, 0:8], o[:, 0:8], v)
                for o, v, w in zip(top, lists, spare):
                    last = nc.vector.match_replace(w, o[:, 0:8], v, NEG)
                link(last)
                if free is not None:
                    nc.vector.nop().then_inc(free, 1)
                for o, w in zip(top, spare):
                    last = nc.vector.max(o[:, 8:16], w)
                link(last)
                for o, w, i in zip(top, spare, idx):
                    last = nc.vector.max_index(i[:, 8:16], o[:, 8:16], w)
                link(last)

            both = [(h, s) for h in range(PH) for s in range(2)]

            def select(t):
                dve.wait_ge(sc_mm, t + 1)
                dve.sem_inc(alone, 1)
                rest([bank[4 + h // 2][:, (h % 2) * 256 + s * NK:(h % 2) * 256 + (s + 1) * NK] for h, s in both], NK,
                     [sv[:, h, s, :] for h, s in both], [si[:, h, s, :] for h, s in both],
                     [sc2[:, 2 * h + s, :] for h, s in both], sc_read)
                low_u(4 * t, 0)
                low_u(4 * t + 1, 1)
                link(nc.vector.tensor_copy(sif[:], si[:]))
                link(nc.vector.tensor_scalar(sif[:, :, 0, :], sif[:, :, 0, :], float(NK), None, ALU.mult))
                for src, dst in ((sv, cand), (sif, ecand)):
                    off = 0
                    for a, na, nb in RECTS:
                        shape = [P, PH, na, nb]
                        last = nc.vector.tensor_tensor(
                            dst[:, :, off:off + na * nb].rearrange("p h (a b) -> p h a b", b=nb),
                            src[:, :, 0, a:a + na].unsqueeze(3).broadcast_to(shape),
                            src[:, :, 1, 0:nb].unsqueeze(2).broadcast_to(shape), ALU.add)
                        off += na * nb
                link(last)
                heads = range(PH)
                rest([cand[:, h, :] for h in heads], NCAND, [cv[:, h, :] for h in heads],
                     [pos[:, h, :] for h in heads], [cand2[:, h, :] for h in heads])
                nc.vector.tensor_copy(posf[:], pos[:])
                link(nc.vector.tensor_copy(gsum[:, 1, :], cv[:, :, 0]))
                nc.vector.tensor_tensor(cv[:], cv[:], gsum[:, 1, :].unsqueeze(2).broadcast_to([P, PH, TOPK]),
                                        ALU.subtract).then_inc(gate_sub, 1)
                low_u(4 * t + 2, 2)
                low_u(4 * t + 3, 3)
                for h in range(0, PH, 2):
                    shape = [P, 2, TOPK, NCAND]
                    e3 = eq[:]
                    for r in range(2):
                        last = nc.vector.tensor_tensor(
                            e3[:, r * TOPK:(r + 1) * TOPK, :],
                            posf[:, h + r, :].unsqueeze(2).broadcast_to([P, TOPK, NCAND]),
                            iota[:, 0:NCAND].unsqueeze(1).broadcast_to([P, TOPK, NCAND]), ALU.is_equal)
                    link(last)
                    for r in range(2):
                        last = nc.vector.tensor_tensor(
                            e3[:, r * TOPK:(r + 1) * TOPK, :], e3[:, r * TOPK:(r + 1) * TOPK, :],
                            ecand[:, h + r, :].unsqueeze(1).broadcast_to([P, TOPK, NCAND]), ALU.mult)
                    link(last)
                    link(nc.vector.tensor_reduce(sel[:, 0, h:h + 2, :].rearrange("p h k -> p (h k)"), e3, AX, ALU.add))
                dve.wait_ge(gate_exp, t + 1)
                link(nc.vector.tensor_reduce(gsum[:, 0, :], sel[:, 1, :, :], AX, ALU.add))
                link(nc.vector.reciprocal(gsum[:, 1, :], gsum[:, 0, :]))
                nc.vector.tensor_tensor(sel[:, 1, :, :], sel[:, 1, :, :],
                                        gsum[:, 1, :].unsqueeze(2).broadcast_to([P, PH, TOPK]),
                                        ALU.mult).then_inc(sel_r, 1)
                dve.wait_ge(selT_mm, t + 1)
                nc.vector.tensor_copy(selT[:, 0, bass.ds(t * P, P)], bank[2][:, 0:P])
                link(nc.vector.tensor_copy(selT[:, 2, bass.ds(t * P, P)], bank[2][:, P:2 * P]))
                nc.vector.nop().then_inc(selT_sb, 1)

            n0 = ch.n
            select(0)
            per_tile = ch.n - n0
            with dve.Fori(1, TT) as it:
                ch.turn, ch.n = (it - 1) * per_tile, ch.n
                select(it)
            ch.turn = 0
            ch.n = n0 + TT * per_tile
            link(nc.vector.tensor_copy(selI[:, 0, :], selT[:, 0, :]))
            link(nc.vector.tensor_scalar(selI[:, 1, :], selI[:, 0, :], NK - 1, None, ALU.bitwise_and))
            link(nc.vector.tensor_scalar(selI[:, 0, :], selI[:, 0, :], NK.bit_length() - 1, None,
                                         ALU.logical_shift_right))
            nc.vector.tensor_copy(selT[:, 0, :], selI[:, 0, :])
            nc.vector.tensor_copy(selT[:, 1, :], selI[:, 1, :]).then_inc(sel_all, 1)
            dve.wait_ge(sel_all, 1)

            def one_hot(n, b):
                need(dve, gt_mm, n - 1)
                for j in range(TOK):
                    last = nc.vector.tensor_scalar(oneI[:, b, j, :], iota[:], selT[:, 0, bass.ds(n * TOK + j, 1)],
                                                   selT[:, 2, bass.ds(n * TOK + j, 1)], ALU.is_equal, ALU.mult)
                last.then_inc(oneI_r, 1)

            one_hot(0, 0)
            one_hot(1, 1)
            with dve.Fori(1, T // TOK // 2) as it:
                one_hot(2 * it, 0)
                one_hot(2 * it + 1, 1)

            def weigh(g, k, slot):
                c = GR * g + k
                dve.wait_ge(gel_r, c + 1)
                s = (k // 2) % 2
                dve.wait_ge(g_in[s], 16 * (2 * g + k // 4 + 1))
                need(dve, v_mm, 16 * g + k - 7)
                need(dve, w_lo, c - 1)
                nc.vector.tensor_tensor(wf[:, k % 2, :].rearrange("p (b t) -> p b t", t=TB),
                                        gel[:, slot, :].rearrange("p (b t) -> p b t", t=TB),
                                        gring[:, s, :, k % 2, :], ALU.mult).then_inc(w_mul, 1)

            def low_w(g, k):
                dve.wait_ge(w_hi, GR * g + k + 1)
                nc.vector.tensor_tensor(el[:, k, :], wf[:, k % 2, :], eh[:, k, :].bitcast(F32),
                                        ALU.subtract).then_inc(w_lo, 1)

            def low_v(g, n):
                dve.wait_ge(v_hi, 16 * g + n + 1)
                nc.vector.tensor_tensor(vlo[:, n % VR, :], vraw[:, n % VR, :], vhi[:, n % VR, :].bitcast(F32),
                                        ALU.subtract).then_inc(v_lo, 1)

            def add(g, half, first):
                for t in range(TT):
                    dve.wait_ge(pv_mm, 8 * g + 4 * half + t + 1)
                    need(dve, pv_add, 8 * g + 4 * half + t - 7)
                    dst = acc[:, t, half * HALF:(half + 1) * HALF]
                    if first:
                        nc.vector.tensor_copy(dst, bank[2 + t][:, :]).then_inc(pv_add, 1)
                    else:
                        nc.vector.tensor_tensor(dst, dst, bank[2 + t][:, :], ALU.add).then_inc(pv_add, 1)

            def group(g, par, with_u, first, last, last_row=False):
                for k in range(GR):
                    if with_u:
                        low_u(GR * g + LEAD + k, k)
                    if k == 0:
                        weigh(g, GR - 1, par * GR + GR - 1)
                        low_w(g, GR - 1)
                    low_v(g, k)
                    if k == 0 and first is not True:
                        add(g - 1, 1, first == "second")
                if last:
                    dve.wait_ge(w_mul, CH)
                    diagonals(dg2, 40)
                for n in range(8, 11):
                    low_v(g, n)
                add(g, 0, first is True)
                if last:
                    gate_row(rows2[:, 0, :], 0, 2)
                for k in range(GR):
                    if k + 11 < 16:
                        low_v(g, k + 11)
                    if k and not last:
                        weigh(g + 1, k - 1, (1 - par) * GR + k - 1)
                        low_w(g + 1, k - 1)

            for i in range(2):
                dve.wait_ge(stage_out[i], 16 * NTB // 2)
            for k in range(GR - 1):
                weigh(0, k, k)
                low_w(0, k)
            group(0, 0, True, True, False)
            group(1, 1, True, "second", False)
            with dve.Fori(1, NG // 2 - 1) as it:
                group(2 * it, 0, True, False, False)
                group(2 * it + 1, 1, True, False, False)
            group(NG - 2, 0, False, False, False)
            group(NG - 1, 1, False, False, True)
            add(NG - 1, 1, False)
            dve.wait_ge(fin_in, 48)
            dve.wait_ge(g_row, 2)
            dve.wait_ge(pv_add, 8 * NG)
            for t in range(TT):
                last = nc.vector.tensor_tensor(acc[:, t, :], acc[:, t, :], rows2[:, 0, :], ALU.mult)
            link(last)
            for t in range(TT):
                last = nc.vector.scalar_tensor_tensor(out=xfin[:, t, :], in0=xfin[:, t, :], scalar=ALPHA,
                                                      in1=acc[:, t, :], op0=ALU.mult, op1=ALU.add)
            link(last)
            link(norm(xfin, acc, 4))
            for t in range(TT):
                last = nc.vector.tensor_tensor(acc[:, t, :], acc[:, t, :], rows2[:, 1, :], ALU.mult)
            link(last)
            for t in range(TT):
                nc.vector.tensor_tensor(xfin[:, t, :], acc[:, t, :], rows2[:, 2, :], ALU.add).then_inc(y_r, 1)

        @block.tensor
        def _(pe):
            mm = nc.tensor.matmul

            def three(o, wh, wl, mh, ml, start, stop):
                mm(o, wh, mh, start=start, stop=False)
                mm(o, wh, ml, start=False, stop=False)
                return mm(o, wl, mh, start=False, stop=stop)

            def transposes(turn):
                pe.wait_ge(xn_r, turn)
                for kd in range(KD):
                    for t in range(TT):
                        last = nc.tensor.transpose(bank[kd][:, t * P:(t + 1) * P], xn[:, t, kd * P:(kd + 1) * P],
                                                   ident[:])
                    last.then_inc(xT_mm, 1)

            def low_ready(n):
                pe.wait_ge(raw_free, AT_STREAM[("w", n)] + 1)

            def tile(n, o):
                low_ready(n)
                for kd in range(KD):
                    w = slice(kd * P, (kd + 1) * P)
                    last = three(o, whi[:, n % SPL, w], wlo[:, n % SPL, w], act_hi[:, kd, :], act_lo[:, kd, :],
                                 kd == 0, kd == KD - 1)
                last.then_inc(blk_mm, 1)

            def rows_block(n, b, o0):
                low_ready(n)
                for kk in range(2):
                    kd = 2 * b + kk
                    w = slice(kk * HALF, (kk + 1) * HALF)
                    for t in range(TT):
                        c = slice(t * P, (t + 1) * P)
                        last = three(bank[o0 + t][:, :], act_hi[:, kd, c], act_lo[:, kd, c],
                                     whi[:, n % SPL, w], wlo[:, n % SPL, w], kd == 0, kd == KD - 1)
                last.then_inc(blk_mm, 1)
                return last

            pe.wait_ge(const_r, 1)
            transposes(1)
            pe.wait_ge(a_lo, KD)
            for n in range(G0):
                if V0 <= n < C0:
                    rows_block(n, n - V0, 4)
                    if n == C0 - 1:
                        pe.wait_ge(blk_mm, C0)
                        pe.nop().then_inc(v_mm1, 1)
                else:
                    z_wait(pe, n)
                    tile(n, bank[z_bank[n]][:, :])

            def scores(h, q):
                need(pe, p_exp, 4 * h + q - 1)
                w = P * (q + 1)
                mm(bank[4 + q % 2][:, 0:w], qa[:, h, q * P:(q + 1) * P], ka[:, h, 0:w],
                   start=True, stop=True).then_inc(s_mm, 1)

            def prob_T(h, q):
                pe.wait_ge(p_norm, 4 * h + q + 1)
                need(pe, pT_sb, 4 * h + q - 1)
                for k in range(q + 1):
                    last = nc.tensor.transpose(bank[6 + q % 2][:, k * P:(k + 1) * P],
                                               prob[:, tri(q) + k * P:tri(q) + (k + 1) * P], ident[:])
                last.then_inc(pT_mm, 1)

            def attend(h):
                pe.wait_ge(pT_sb, 4 * h + 4)
                need(pe, o_sb, h)
                for k in range(TT):
                    last = mm(bank[3][0:DH, k * P:T], vals[:, k, h * DH:(h + 1) * DH], probT[:, k, k * P:T],
                              start=(k == 0), stop=(k == TT - 1))
                last.then_inc(o_mm, 1)

            pe.wait_ge(aug_in, 16 * 2 * HEADS)
            pe.wait_ge(z_act, 8)
            pe.wait_ge(v_act, 2)
            pe.wait_ge(v_dve, 2)
            for h in range(HEADS):
                n = G0 + 2 * h
                scores(h, 0)
                scores(h, 1)
                if h:
                    attend(h - 1)
                z_wait(pe, n)
                tile(n, bank[z_bank[n]][:, :])
                scores(h, 2)
                scores(h, 3)
                prob_T(h, 0)
                prob_T(h, 1)
                z_wait(pe, n + 1)
                tile(n + 1, bank[z_bank[n + 1]][:, :])
                prob_T(h, 2)
                prob_T(h, 3)
            attend(HEADS - 1)
            pe.wait_ge(conv_p, 1)
            pe.wait_ge(conv_d, (CT - 1) * TAPS)
            for i in range(CT):
                last = mm(bank[4][:, :], consts[:], conv[:, i, :], start=(i == 0), stop=(i == CT - 1))
            last.then_inc(conv_mm, 1)
            for i in range(CT):
                pe.wait_ge(conv_q, i + 1)
                last = mm(bank[5][:, :], consts[:], hc[:, i, 0:T], start=(i == 0), stop=(i == CT - 1))
            last.then_inc(conv_mm, 1)
            pe.wait_ge(z_act, len(by_act))
            pe.wait_ge(o_sb, HEADS)
            pe.wait_ge(conv_v, 1)
            for n in range(Y0, O0):
                j, branch = (n - Y0) // 2, (n - Y0) % 2
                need(pe, y_free, j - 1)
                pe.wait_ge(part_lo, branch + 1)
                low_ready(n)
                src_hi, src_lo = (att_hi, att_lo) if branch == 0 else (cvn_hi, cvn_lo)
                for r in range(2):
                    for k in range(AT):
                        w = slice((r * AT + k) * P, (r * AT + k + 1) * P)
                        last = three(bank[4 * (j % 2) + 2 * branch + r][:, :], whi[:, n % SPL, w], wlo[:, n % SPL, w],
                                     src_hi[:, k, :], src_lo[:, k, :], k == 0, k == AT - 1)
                last.then_inc(blk_mm, 1)
                pe.wait_ge(blk_mm, n + 1)
                pe.nop().then_inc(y_mm, 1)

            def gate_row(dg, banks, n):
                pe.wait_ge(g_dg, n)
                for half in range(2):
                    last = mm(bank[banks + half][:, :], consts[:],
                              dg[:, 4 * half:4 * half + 4, :].rearrange("p m c -> p (m c)"), start=True, stop=True)
                last.then_inc(g_mm, 1)

            pe.wait_ge(y_free, 4)
            gate_row(dg1, 6, 1)
            pe.wait_ge(g_row, 1)
            pe.wait_ge(a_lo, 2 * KD)
            for half in range(2):
                for b in range(4):
                    rows_block(O0 + 4 * half + b, b, 4 * half)
                pe.wait_ge(blk_mm, O0 + 4 * half + 4)
                pe.nop().then_inc(o1_mm, 1)
            transposes(2)
            pe.wait_ge(a_lo, 3 * KD)
            for h in range(PH):
                need(pe, z_act, len(by_act) + h - 1 if h > 1 else 0)
                tile(W0 + h, bank[h % 2][:, :])
            pe.wait_ge(small_in, 96)
            pe.wait_ge(z_act, len(by_act) + PH)

            def first_product(c, slot):
                pe.wait_ge(u_lo, c + 1)
                need(pe, gel_r, c - 1)
                for kd in range(KD):
                    w = slice(kd * P, (kd + 1) * P)
                    last = three(bank[slot % 2][:, :], whi[:, slot % 2, w], wlo[:, slot % 2, w],
                                 act_hi[:, kd, :], act_lo[:, kd, :], kd == 0, kd == KD - 1)
                last.then_inc(u_mm, 1)

            def sel_T(t):
                pe.wait_ge(sel_r, t + 1)
                need(pe, selT_sb, t)
                for r in range(2):
                    last = nc.tensor.transpose(bank[2][:, r * P:(r + 1) * P],
                                               sel[:, r, :, :].rearrange("p h k -> p (h k)"), ident[:])
                last.then_inc(selT_mm, 1)

            for t in range(TT):
                need(pe, sc_read, t)
                for h in range(PH):
                    last = mm(bank[4 + h // 2][:, (h % 2) * 256:(h % 2 + 1) * 256], qT[:, h, t * P:(t + 1) * P],
                              keys[:], start=True, stop=True)
                last.then_inc(sc_mm, 1)
                for j in range(4):
                    first_product(4 * t + j, 4 * t + j)
                sel_T(t)
            pe.wait_ge(selT_sb, TT)

            def token_gates(n, b):
                pe.wait_ge(oneJ_r, n + 1)
                pe.wait_ge(oneI_r, n + 1)
                need(pe, gt_sb, n - 1)
                for j in range(TOK):
                    last = mm(bank[2 + b][:, j * NK:(j + 1) * NK], oneJ[:, b, j, :], oneI[:, b, j, :],
                              start=True, stop=True)
                last.then_inc(gt_mm, 1)

            token_gates(0, 0)
            token_gates(1, 1)
            with pe.Fori(1, T // TOK // 2) as it:
                token_gates(2 * it, 0)
                token_gates(2 * it + 1, 1)
            pe.wait_ge(gt_sb, T // TOK)

            def second_product(g, k, half):
                n = half * GR + k
                pe.wait_ge(v_lo, 16 * g + n + 1)
                pe.wait_ge(w_lo, GR * g + k + 1)
                for t in range(TT):
                    if k == 0:
                        need(pe, pv_add, 8 * g + 4 * half + t - 3)
                    c = slice(t * P, (t + 1) * P)
                    last = three(bank[2 + t][:, :], eh[:, k, c], el[:, k, c], vhi[:, n % VR, :], vlo[:, n % VR, :],
                                 k == 0, k == GR - 1)
                    if k == GR - 1 and t < TT - 1:
                        last.then_inc(pv_mm, 1)
                last.then_inc(v_mm, 1)
                if k == GR - 1:
                    pe.wait_ge(v_mm, 16 * g + n + 1)
                    pe.nop().then_inc(pv_mm, 1)

            def group(g, with_u, last=False):
                for k in range(GR):
                    if with_u:
                        first_product(GR * g + LEAD + k, k)
                    second_product(g, k, 0)
                if last:
                    gate_row(dg2, 0, 2)
                for k in range(GR):
                    second_product(g, k, 1)

            group(0, True)
            group(1, True)
            with pe.Fori(1, NG // 2 - 1) as it:
                group(2 * it, True)
                group(2 * it + 1, True)
            group(NG - 2, False)
            group(NG - 1, False, True)


def kernel(**inputs):
    import numpy as np
    import concourse.bacc as _bacc
    from concourse import mybir as _mybir
    from concourse.bass_utils import run_bass_kernel_spmd as _run

    a = {k: np.asarray(v) for k, v in inputs.items()}

    def tiles(w):
        return w.reshape(KD, P, -1, P).transpose(2, 1, 0, 3).reshape(-1, P, D)

    def branch(w):
        return w.reshape(AT, P, 4, 2, P).transpose(2, 1, 3, 0, 4).reshape(4, P, D)

    w_in = a["w_in"][0]
    o = [0, AW, 2 * AW, 3 * AW, 3 * AW + HEADS]
    ca, cbc = o[4], o[4] + CC
    gates = cbc + CC
    wv = w_in[:, o[2]:o[3]].reshape(4, 2, P, AW).transpose(0, 2, 1, 3).reshape(4, P, D)
    pairs = np.stack([tiles(w_in[:, ca:cbc]), tiles(w_in[:, cbc:gates])], 1).reshape(2 * CT, P, D)
    branches = np.stack([branch(a["w_attn_out"][0]), branch(a["w_conv_out"][0])], 1).reshape(8, P, D)
    w_out = a["w_out"][0].reshape(4, 2, P, 2, HALF).transpose(3, 0, 2, 1, 4).reshape(8, P, D)
    wblk = np.concatenate([
        tiles(w_in[:, o[0]:o[1]]), tiles(w_in[:, o[1]:o[2]]), tiles(w_in[:, o[3]:o[3] + P]), wv, pairs,
        tiles(w_in[:, gates:]), branches, w_out, tiles(a["peer_wq"][0])])
    arrays = {
        "x": a["x"][0],
        "cb": a["c"],
        "b_modc": a["b_mod"][0].reshape(MODT, P).T,
        "w_modt": a["w_mod"][0].T.reshape(MODT, P, D),
        "wblk": wblk,
        "b_fc": a["b_f"][0][:, None],
        "conv_wc": a["conv_w"][0].reshape(TAPS, CT, P).transpose(2, 1, 0),
        "conv_vec": np.stack([a["conv_b"][0], a["conv_ln_g"][0], a["conv_ln_b"][0]]).reshape(3, CT, P).transpose(2, 0, 1),
        "keys_t": a["peer_sub_keys"][0].transpose(0, 2, 1),
        "u_t": a["peer_u"][0].reshape(CH, P, KD, P).transpose(0, 3, 2, 1).reshape(CH, P, D),
        "v_tab": a["peer_v"][0],
        "rows": np.stack([a["ln1_g"][0], a["ln1_b"][0], a["ln2_g"][0], a["ln2_b"][0]]),
    }
    nc = _bacc.Bacc("TRN2", target_bir_lowering=False, num_devices=1)
    feeds, args = {}, []
    for name, arr in arrays.items():
        arr = np.ascontiguousarray(arr)
        feeds[f"in_{name}_dram"] = arr
        args.append(nc.dram_tensor(f"in_{name}_dram", arr.shape, _mybir.dt.from_np(arr.dtype), kind="ExternalInput").ap())
    args.append(nc.dram_tensor("out_0_dram", (T, D), F32, kind="ExternalOutput").ap())
    build(nc, *args)
    r = _run(nc, [feeds], core_ids=[0])
    return r.results[0]["out_0_dram"].reshape(1, T, D)
```

```python
from contextlib import ExitStack

import concourse.bass as bass
from concourse import mybir

F32 = mybir.dt.float32
F32R = mybir.dt.float32r
I32 = mybir.dt.int32
U32 = mybir.dt.uint32
ALU = mybir.AluOpType
ACT = mybir.ActivationFunctionType
AX = mybir.AxisListType.X

P = 128
D = 1024
T = 512
KD = D // P
TT = T // P
HEADS = 8
DH = 64
AW = HEADS * DH
AT = AW // P
CC = 512
CT = CC // P
TAPS = 31
PH = 8
NK = 128
TOPK = 16
HK = PH * TOPK
MODT = 6 * D // P
EPS = 1e-5
ALPHA = 2.0 ** 0.25
NEG = -3.0e38
HALF = D // 2

Q0, K0, F0, V0, C0, G0 = 0, 4, 8, 9, 13, 21
Y0, O0, W0, NBLK = 37, 45, 53, 61
RAW = 4
SPL = 3
STREAM = [("mod", m) for m in range(14)] + [("w", 0), ("mod", 14), ("mod", 15)]
for _n in range(NBLK):
    if _n:
        STREAM.append(("w", _n))
    if G0 <= _n < G0 + 32:
        STREAM.append(("mod", _n - G0 + 16))
AT_STREAM = {e: s for s, e in enumerate(STREAM)}

RECTS = [(0, 1, 16), (1, 1, 8), (2, 2, 5), (4, 4, 3), (8, 8, 1)]
NCAND = sum(na * nb for _, na, nb in RECTS)

CH = NK
GR = 8
LEAD = 16
TB = 64
NTB = T // TB
TOK = 4
NBT = P // TOK
OH = 4
PRE_T, PRE_G, FILL = 12, 4, 8
PER = PRE_T + PRE_G
PRE = TT * PER + FILL
PS = 8
VR = 4


def build(nc, x, cb, b_modc, w_modt, wblk, b_fc, conv_wc, conv_vec, keys_t, u_t, v_tab, rows, out):
    with ExitStack() as ctx:
        KB = 1024
        base = (nc.sbuf_base + 31) // 32 * 32

        def sb(name, shape, dt, kb):
            return nc.alloc_sbuf_tensor_at(name, shape, dt, offset=base + int(kb * KB))

        def sem(name):
            return ctx.enter_context(nc.semaphore(name))

        bank = [ctx.enter_context(nc.psum_tensor(f"bank{i}", [P, 512], F32)) for i in range(8)]

        act_hi = sb("act_hi", [P, KD, T], F32R, 0)
        act_lo = sb("act_lo", [P, KD, T], F32R, 16)
        raw = sb("raw", [P, RAW, D], F32, 32)
        whi = sb("whi", [P, SPL, D], F32R, 48)
        wlo = sb("wlo", [P, SPL, D], F32R, 60)
        xres = sb("xres", [P, TT, D], F32, 72)
        prob = sb("prob", [P, 1280], F32, 72)
        probT = sb("probT", [P, TT, T], F32, 77)
        qa = sb("qa", [DH + 2, HEADS, T], F32, 88)
        ka = sb("ka", [DH + 2, HEADS, T], F32, 104)
        att_hi = sb("att_hi", [P, AT, T], F32R, 88)
        att_lo = sb("att_lo", [P, AT, T], F32R, 96)
        cvn_hi = sb("cvn_hi", [P, CT, T], F32R, 104)
        cvn_lo = sb("cvn_lo", [P, CT, T], F32R, 112)
        vals = sb("vals", [P, TT, AW], F32, 120)
        sg = sb("sg", [P, 2, T], F32, 128)
        rows1 = sb("rows1", [P, 3, D], F32, 120)
        hc = sb("hc", [P, CT, T + TAPS - 1], F32, 132)
        conv = sb("conv", [P, CT, T], F32, 141)
        ga = sb("ga", [P, KD, T], F32, 149)
        gb = sb("gb", [P, KD, T], F32, 165)
        xn = sb("xn", [P, TT, D], F32, 149)
        uraw = sb("uraw", [P, KD, T], F32, 165)
        attT = sb("attT", [P, AT, T], F32, 181)
        frow = sb("frow", [HEADS, 4, T], F32, 189)
        cs = sb("cs", [P, D], F32, 197)
        ptmp = sb("ptmp", [P, T], F32, 189)
        rbc = sb("rbc", [P, 4, T], F32, 189)
        qT = sb("qT", [P, PH, T], F32, 72)
        gelz = sb("gelz", [P, PS, T], F32, 88)
        gel = sb("gel", [P, LEAD, T], F32, 88)
        gback = sb("gback", [P, 4, 2, T], F32, 72)
        stage = sb("stage", [P, 2, NK, TB], F32, 120)
        eq = sb("eq", [P, 2, TOPK, NCAND], F32, 192)
        acc = sb("acc", [P, TT, D], F32, 120)
        eh = sb("eh", [P, GR, T], F32R, 136)
        el = sb("el", [P, GR, T], F32R, 152)
        vraw = sb("vraw", [P, VR, HALF], F32, 168)
        vhi = sb("vhi", [P, VR, HALF], F32R, 176)
        vlo = sb("vlo", [P, VR, HALF], F32R, 184)
        gring = sb("gring", [P, 2, NTB, 2, TB], F32, 192)
        wf = sb("wf", [P, 2, T], F32, 56)
        sc2 = sb("sc2", [P, 2 * PH, NK], F32, 112)
        one = [sb(f"one{i}", [P, 2, TOK, NK], F32, kb) for i, kb in enumerate((184, 188, 112, 116))]
        selT = sb("selT", [P, 3, P], F32, 199)
        outg = sb("outg", [P, TT, D], F32, 149)
        dg1 = sb("dg1", [P, KD, P], F32, 189)
        dg2 = sb("dg2", [P, KD, P], F32, 100)
        xfin = sb("xfin", [P, TT, D], F32, 72)
        rows2 = sb("rows2", [P, 3, D], F32, 88)
        cur = [201 * KB]

        def small(name, shape, dt):
            n = 4
            for s in shape[1:]:
                n *= s
            t = nc.alloc_sbuf_tensor_at(name, shape, dt, offset=base + cur[0])
            cur[0] += (n + 31) // 32 * 32
            return t

        ident = small("ident", [P, P], F32)
        iota = small("iota", [P, NK], F32)
        consts = small("consts", [P, P], F32)
        modc = small("modc", [P, MODT], F32)
        bmod = small("bmod", [P, MODT], F32)
        convw = small("convw", [P, CT, TAPS], F32)
        convv = small("convv", [P, 3, CT], F32)
        bf = small("bf", [HEADS, 1], F32)
        stats = small("stats", [P, TT, 2, 6], F32)
        mv = small("mv", [P, TT, 2], F32)
        sq = small("sq", [P, 4, TT], F32)
        att_s = small("att_s", [P, 4, TT], F32)
        assert cur[0] <= nc.sbuf_usable_end - base, cur[0]
        mask = sb("mask", [P, T], F32, 85.5)
        keys = sb("keys", [P, 2 * NK], F32, 104)
        sv = sb("sv", [P, PH, 2, TOPK], F32, 57)
        si = sb("si", [P, PH, 2, TOPK], U32, 58)
        sif = sb("sif", [P, PH, 2, TOPK], F32, 59)
        cv = sb("cv", [P, PH, TOPK], F32, 68)
        pos = sb("pos", [P, PH, TOPK], U32, 68.5)
        posf = sb("posf", [P, PH, TOPK], F32, 69)
        sel = sb("sel", [P, 2, PH, TOPK], F32, 69.5)
        gsum = sb("gsum", [P, 2, PH], F32, 70.5)
        selI = sb("selI", [P, 2, P], I32, 71)
        cand = sb("cand", [P, PH, NCAND], F32, 184)
        cand2 = sb("cand2", [P, PH, NCAND], F32, 186)
        ecand = sb("ecand", [P, PH, NCAND], F32, 188)

        gates_dram = nc.dram_tensor("gates_by_key", [NTB, P, NK, TB], F32, kind="Internal").ap()
        gel_dram = nc.dram_tensor("gelu_ahead", [PRE // 4, P, 4, T], F32, kind="Internal").ap()
        x1_dram = nc.dram_tensor("x_after_first", [TT, P, D], F32, kind="Internal").ap()


        small_in = sem("small_in")
        x_in = sem("x_in")
        c_in = sem("c_in")
        raw_in = [sem(f"raw_in{i}") for i in range(RAW)]
        raw_free = sem("raw_free")
        blk_hi = sem("blk_hi")
        blk_lo = sem("blk_lo")
        blk_mm = sem("blk_mm")
        dch = sem("dch")
        ach = sem("ach")
        pch = sem("pch")
        const_r = sem("const_r")
        mask_r = sem("mask_r")
        cs_r = sem("cs_r")
        var_r = sem("var_r")
        dev_r = sem("dev_r")
        xn_r = sem("xn_r")
        xT_mm = sem("xT_mm")
        u_raw = sem("u_raw")
        a_hi = sem("a_hi")
        a_lo = sem("a_lo")
        z_act = sem("z_act")
        z_dve = sem("z_dve")
        sg_r = sem("sg_r")
        f_log = sem("f_log")
        f_exp = sem("f_exp")
        f_ready = sem("f_ready")
        aug_in = sem("aug_in")
        v_mm1 = sem("v_mm1")
        v_act = sem("v_act")
        v_dve = sem("v_dve")
        hc_r = sem("hc_r")
        s_mm = sem("s_mm")
        nmax = sem("nmax")
        p_exp = sem("p_exp")
        p_norm = sem("p_norm")
        pT_mm = sem("pT_mm")
        pT_sb = sem("pT_sb")
        o_mm = sem("o_mm")
        o_sb = sem("o_sb")
        conv_p = sem("conv_p")
        conv_d = sem("conv_d")
        conv_mm = sem("conv_mm")
        conv_c = sem("conv_c")
        conv_q = sem("conv_q")
        conv_v = sem("conv_v")
        conv_s = sem("conv_s")
        conv_y = sem("conv_y")
        conv_a = sem("conv_a")
        part_hi = sem("part_hi")
        part_lo = sem("part_lo")
        y_mm = sem("y_mm")
        y_free = sem("y_free")
        m_raw = sem("m_raw")
        g_dg = sem("g_dg")
        g_mm = sem("g_mm")
        g_row = sem("g_row")
        row_in = sem("row_in")
        x_again = sem("x_again")
        o1_mm = sem("o1_mm")
        x1_r = sem("x1_r")
        x1_out = sem("x1_out")
        sc_mm = sem("sc_mm")
        sc_read = sem("sc_read")
        gate_sub = sem("gate_sub")
        gate_exp = sem("gate_exp")
        sel_r = sem("sel_r")
        selT_mm = sem("selT_mm")
        selT_sb = sem("selT_sb")
        eq_r = sem("eq_r")
        eqm_r = sem("eqm_r")
        one_r = sem("one_r")
        onem_r = sem("onem_r")
        gt_mm = sem("gt_mm")
        gt_sb = sem("gt_sb")
        stage_out = [sem(f"stage_out{i}") for i in range(2)]
        gel_out = sem("gel_out")
        back_in = [sem(f"back_in{i}") for i in range(4)]
        u_in = [sem(f"u_in{i}") for i in range(RAW)]
        u_hi = sem("u_hi")
        u_lo = sem("u_lo")
        u_mm = sem("u_mm")
        gel_r = sem("gel_r")
        w_mul = sem("w_mul")
        w_hi = sem("w_hi")
        w_lo = sem("w_lo")
        v_in = [sem(f"v_in{i}") for i in range(VR)]
        v_hi = sem("v_hi")
        v_lo = sem("v_lo")
        v_mm = sem("v_mm")
        g_in = [sem(f"g_in{i}") for i in range(2)]
        pv_mm = sem("pv_mm")
        pv_add = sem("pv_add")
        fin_in = sem("fin_in")
        y_r = sem("y_r")
        y_out = sem("y_out")
        alone = sem("alone")

        class Chain:

            def __init__(self, eng, s):
                self.eng, self.s, self.n, self.turn = eng, s, 0, 0

            def link(self, ins):
                self.n += 1
                ins.then_inc(self.s, 1)
                self.eng.wait_ge(self.s, self.turn + self.n)
                if not isinstance(self.turn, int):
                    self.eng.sem_inc(alone, 1)

        def need(eng, s, value):
            if not isinstance(value, int) or value > 0:
                eng.wait_ge(s, value)

        TILES = list(range(V0)) + list(range(C0, Y0))
        z_bank = {n: (n % 2 if n < V0 else (n - C0) % 2 if n < G0 else (n - G0) % 3) for n in TILES}
        by_dve = [n for n in TILES if n == F0 or (C0 <= n < G0 and (n - C0) % 2 == 0)]
        by_act = [n for n in TILES if n not in by_dve]

        def z_wait(pe, n):
            last = [m for m in TILES if m < n and z_bank[m] == z_bank[n]]
            if last:
                m = last[-1]
                if m in by_dve:
                    pe.wait_ge(z_dve, by_dve.index(m) + 1)
                else:
                    pe.wait_ge(z_act, by_act.index(m) + 1)

        def tri(q):
            return P * q * (q + 1) // 2

        v_half = v_tab.rearrange("(c e) (h d) -> c h e d", e=P, h=2)
        x_pt = x.rearrange("(t p) d -> p t d", p=P)
        NG = CH // GR
        FIRST = (PRE // GR + 2) // 2 * 2

        block = ctx.enter_context(nc.Block())

        @block.sync
        def _(sp):
            sp.dma_start(cs[:], cb.broadcast_to([P, D])).then_inc(c_in, 16)
            for s in range(RAW):
                sp.dma_start(raw[:, s, :], w_modt[s]).then_inc(raw_in[s], 16)
            sp.dma_start(xres[:], x_pt).then_inc(x_in, 16)
            for dst, src in ((bmod[:], b_modc), (bf[:], b_fc), (convw[:], conv_wc), (convv[:], conv_vec)):
                sp.dma_start(dst, src).then_inc(small_in, 16)

            def stream(s):
                kind, n = STREAM[s]
                if s >= RAW:
                    sp.wait_ge(raw_free, s - RAW + 1)
                sp.dma_start(raw[:, s % RAW, :], w_modt[n] if kind == "mod" else wblk[n]).then_inc(raw_in[s % RAW], 16)

            s_f, s_y = AT_STREAM[("w", C0 + 2)], AT_STREAM[("w", Y0 + 2)]
            for s in range(RAW, s_f):
                stream(s)
            sp.wait_ge(f_ready, 1)
            for h in range(HEADS):
                sp.dma_start(qa[DH:DH + 1, h, :], frow[h:h + 1, 0, :]).then_inc(aug_in, 16)
                sp.dma_start(ka[DH + 1:DH + 2, h, :], frow[h:h + 1, 1, :]).then_inc(aug_in, 16)
            for s in range(s_f, s_y):
                stream(s)
            sp.wait_ge(o_mm, HEADS)
            sp.dma_start(xres[:], x_pt).then_inc(x_again, 16)
            for i in range(2):
                sp.dma_start(rows1[:, 1 + i, :], rows[i:i + 1].broadcast_to([P, D])).then_inc(row_in, 16)
            for s in range(s_y, len(STREAM)):
                stream(s)
            sp.wait_ge(const_r, 2)
            for side in range(2):
                sp.dma_start(keys[side * DH:(side + 1) * DH, side * NK:(side + 1) * NK],
                             keys_t[side]).then_inc(small_in, 16)
            def load_u(c, slot):
                need(sp, u_lo, c - RAW + 1)
                src = u_t[c] if isinstance(c, int) else u_t[bass.ds(c, 1)].rearrange("o p d -> (o p) d")
                sp.dma_start(raw[:, slot, :], src).then_inc(u_in[slot], 16)

            def load_v(g, k, half):
                n, c = half * GR + k, GR * g + k
                need(sp, v_lo, 16 * g + n - VR + 1)
                src = v_half[c, half] if isinstance(c, int) else \
                    v_half[bass.ds(c, 1), half].rearrange("o e d -> (o e) d")
                sp.dma_start(vraw[:, n % VR, :], src).then_inc(v_in[n % VR], 16)

            sp.wait_ge(raw_free, len(STREAM))
            def store_gel(m, slot):
                sp.wait_ge(gel_out, 16 * m + 16)
                sp.wait_ge(gel_r, 4 * m + 4)
                dst = gel_dram[m] if isinstance(m, int) else \
                    gel_dram[bass.ds(m, 1)].rearrange("o p c t -> (o p) c t")
                sp.dma_start(dst, gelz[:, 4 * slot:4 * slot + 4, :]).then_inc(gel_out, 16)

            sp.sem_inc(gel_out, 16)
            for c in range(PRE_T):
                load_u(c, c % RAW)
                if c % 4 == 3 and c > 3:
                    store_gel(c // 4 - 1, c // 4 - 1)
            with sp.Fori(0, TT - 1) as it:
                for i in range(PER // 4):
                    for j in range(4):
                        load_u(PER * it + (PRE_T + 4 * i + j), j)
                    store_gel(PER // 4 * it + (PRE_T // 4 + i - 1), (PRE_T // 4 + i - 1) % (PS // 4))
            for c in range(PRE - FILL - PRE_G, PRE):
                load_u(c, c % RAW)
                if c % 4 == 3:
                    store_gel(c // 4 - 1, (c // 4 - 1) % (PS // 4))
            for i in range(2):
                sp.wait_ge(stage_out[i], 16 * (NTB // 2 + 1))
            for k in range(VR):
                load_v(0, k, 0)
            store_gel(PRE // 4 - 1, (PRE // 4 - 1) % (PS // 4))

            def group(g, with_u):
                for k in range(GR):
                    if with_u:
                        load_u(GR * g + LEAD + k, k % RAW)
                    if not isinstance(g, int) or g > 0 or k >= VR:
                        load_v(g, k, 0)
                for k in range(GR):
                    load_v(g, k, 1)

            for g in range(FIRST):
                group(g, GR * g + LEAD >= PRE)
            with sp.Fori(FIRST // 2, NG // 2 - 1) as it:
                group(2 * it, True)
                group(2 * it + 1, True)
            group(NG - 2, False)
            group(NG - 1, False)
            sp.wait_ge(w_mul, CH)
            sp.wait_ge(x1_out, 16)
            sp.dma_start(xfin[:], x1_dram.rearrange("t p d -> p t d")).then_inc(fin_in, 16)
            for i in range(2):
                sp.dma_start(rows2[:, 1 + i, :], rows[2 + i:3 + i].broadcast_to([P, D])).then_inc(fin_in, 16)
            for t in range(TT):
                sp.wait_ge(y_r, t + 1)
                sp.dma_start(out[t * P:(t + 1) * P, :], xfin[:, t, :]).then_inc(y_out, 16)
            sp.wait_ge(y_out, 16 * TT)

        @block.gpsimd
        def _(pool):
            ch = Chain(pool, pch)
            ch.link(nc.gpsimd.memset(ident[:], 0.0))
            ch.link(nc.gpsimd.affine_select(out=ident[:], in_=ident[:], compare_op=ALU.not_equal, fill=1.0,
                                            base=0, pattern=[[-1, P]], channel_multiplier=1))
            nc.gpsimd.iota(iota[:], pattern=[[1, NK]], base=0, channel_multiplier=0,
                           allow_small_or_imprecise_dtypes=True)
            nc.gpsimd.memset(consts[:], 1.0 / CC)
            ch.link(nc.gpsimd.memset(hc[:, :, 0:TAPS - 1], 0.0))
            ch.link(nc.gpsimd.memset(qa[DH:DH + 2, :, :], 1.0))
            nc.gpsimd.memset(ka[DH:DH + 2, :, :], 1.0).then_inc(const_r, 1)
            pool.wait_ge(const_r, 1)
            pool.wait_ge(xn_r, 1)
            ch.link(nc.gpsimd.memset(mask[:], 0.0))
            nc.gpsimd.affine_select(out=mask[:], in_=mask[:], compare_op=ALU.is_ge, fill=NEG,
                                    base=T - P, pattern=[[-1, T]], channel_multiplier=1).then_inc(mask_r, 1)
            i = CT - 1
            pool.wait_ge(small_in, 64)
            pool.wait_ge(hc_r, CT)
            pool.wait_ge(aug_in, 16 * 2 * HEADS)
            ch.link(nc.gpsimd.tensor_scalar(conv[:, i, :], hc[:, i, 0:T], convw[:, i, 0:1], convv[:, 0, i:i + 1],
                                            ALU.mult, ALU.add))
            for k in range(1, TAPS):
                ch.link(nc.gpsimd.tensor_scalar(ptmp[:], hc[:, i, k:k + T], convw[:, i, k:k + 1], None, ALU.mult))
                ch.link(nc.gpsimd.tensor_tensor(conv[:, i, :], conv[:, i, :], ptmp[:], ALU.add))
            pool.nop().then_inc(conv_p, 1)
            pool.wait_ge(blk_mm, O0)
            nc.gpsimd.memset(keys[:], 0.0).then_inc(const_r, 1)
            pool.wait_ge(x1_r, TT)
            pool.dma_start(x1_dram.rearrange("t p d -> p t d"), xres[:]).then_inc(x1_out, 16)

            def by_expert(t):
                for h in range(PH):
                    pool.wait_ge(eq_r, 8 * t + (h + 1))
                    nc.gpsimd.tensor_tensor(eq[:, h % 2], eq[:, h % 2],
                                            ecand[:, h, :].unsqueeze(1).broadcast_to([P, TOPK, NCAND]),
                                            ALU.mult).then_inc(eqm_r, 1)

            def by_gate(t):
                for b in range(NBT):
                    pool.wait_ge(one_r, NBT * t + (b + 1))
                    row = one[b % OH][:, 1]
                    nc.gpsimd.tensor_tensor(row, row,
                                            selT[:, 2, b * TOK:(b + 1) * TOK].unsqueeze(2).broadcast_to([P, TOK, NK]),
                                            ALU.mult).then_inc(onem_r, 1)

            by_expert(0)
            with pool.Fori(0, TT - 1) as it:
                by_expert(it + 1)
                by_gate(it)
            by_gate(TT - 1)
            for i in range(2):
                pool.wait_ge(stage_out[i], 16 * (NTB // 2 + 1))

            def load_g(pr, slot):
                need(pool, w_mul, 2 * pr - 2)
                src = gates_dram[:, :, bass.ds(2 * pr, 2), :].rearrange("b p i t -> p b i t")
                pool.dma_start(gring[:, slot], src).then_inc(g_in[slot], 16)

            for pr in range(PRE // 2):
                load_g(pr, pr % 2)
                pool.wait_ge(gel_out, 16 * (pr // 2 + 2))
                pool.dma_start(gback[:, pr % 4], gel_dram[pr // 2, :, 2 * (pr % 2):2 * (pr % 2) + 2, :]
                               ).then_inc(back_in[pr % 4], 16)
            with pool.Fori(PRE // 4, CH // 4) as it:
                load_g(2 * it, 0)
                load_g(2 * it + 1, 1)

        @block.scalar
        def _(act):
            ch = Chain(act, ach)

            def hi(n):
                s = AT_STREAM[("w", n)]
                act.wait_ge(raw_in[s % RAW], 16 * (s // RAW + 1))
                need(act, blk_mm, n - SPL + 1)
                nc.scalar.activation(whi[:, n % SPL, :], raw[:, s % RAW, :], ACT.Copy).then_inc(blk_hi, 1)

            def root(done):
                act.wait_ge(var_r, done)
                nc.scalar.activation(sq[:, 1, :], sq[:, 0, :], ACT.Sqrt).then_inc(dev_r, 1)

            def act_parts(first):
                for kd in range(KD):
                    act.wait_ge(u_raw, first + kd + 1)
                    nc.scalar.activation(act_hi[:, kd, :], uraw[:, kd, :], ACT.Copy).then_inc(a_hi, 1)

            act.wait_ge(c_in, 16)
            nc.scalar.activation(cs[:], cs[:], ACT.Silu).then_inc(cs_r, 1)
            root(1)
            hi(0)
            act_parts(0)
            hi(1)
            for n in range(G0):
                hi(n + 2)
                if n < F0:
                    act.wait_ge(blk_mm, n + 1)
                    dst = qa if n < K0 else ka
                    for r in range(2):
                        ins = nc.scalar.activation(dst[0:DH, 2 * (n % 4) + r, :],
                                                   bank[z_bank[n]][r * DH:(r + 1) * DH, :], ACT.Copy,
                                                   scale=DH ** -0.5 if n < K0 else 1.0)
                    ins.then_inc(z_act, 1)
                elif n == V0 + 1:
                    act.wait_ge(f_log, 1)
                    ch.link(nc.scalar.activation(frow[:, 3, :], frow[:, 2, :], ACT.Abs))
                    ch.link(nc.scalar.activation(frow[:, 3, :], frow[:, 3, :], ACT.Exp, scale=-1.0))
                    nc.scalar.activation(frow[:, 3, :], frow[:, 3, :], ACT.Ln, bias=1.0).then_inc(f_exp, 1)
                elif n == C0 - 1:
                    act.wait_ge(v_mm1, 1)
                    for t in range(2):
                        nc.scalar.activation(vals[:, t, :], bank[4 + t][:, :], ACT.Copy).then_inc(v_act, 1)
                elif n >= C0 and (n - C0) % 2 == 1:
                    i = (n - C0) // 2
                    act.wait_ge(blk_mm, n + 1)
                    need(act, hc_r, i - 1)
                    nc.scalar.activation(sg[:, i % 2, :], bank[z_bank[n]][:, :], ACT.Sigmoid).then_inc(z_act, 1)

            def exp_tile(h, q):
                act.wait_ge(nmax, 4 * h + q + 1)
                w = P * (q + 1)
                nc.scalar.activation(prob[:, tri(q):tri(q) + w], bank[4 + q % 2][:, 0:w], ACT.Exp,
                                     bias=att_s[:, 1, q:q + 1], accum_out=att_s[:, 2, q:q + 1]).then_inc(p_exp, 1)

            def probs_T(h, q):
                act.wait_ge(pT_mm, 4 * h + q + 1)
                nc.scalar.activation(probT[:, 0:q + 1, q * P:(q + 1) * P],
                                     bank[6 + q % 2][:, 0:P * (q + 1)].rearrange("p (k c) -> p k c", c=P),
                                     ACT.Copy).then_inc(pT_sb, 1)

            def head_out(h):
                act.wait_ge(o_mm, h + 1)
                nc.scalar.activation(attT[(h % 2) * DH:(h % 2 + 1) * DH, h // 2, :], bank[3][0:DH, :],
                                     ACT.Copy).then_inc(o_sb, 1)

            def gate_tile(n):
                act.wait_ge(blk_mm, n + 1)
                m = (n - G0) % KD
                nc.scalar.activation((ga if n < G0 + KD else gb)[:, m, :], bank[z_bank[n]][:, :],
                                     ACT.Sigmoid).then_inc(z_act, 1)

            for h in range(HEADS):
                n = G0 + 2 * h
                exp_tile(h, 0)
                exp_tile(h, 1)
                if h:
                    head_out(h - 1)
                hi(n + 2)
                exp_tile(h, 2)
                exp_tile(h, 3)
                probs_T(h, 0)
                probs_T(h, 1)
                hi(n + 3)
                probs_T(h, 2)
                probs_T(h, 3)
                gate_tile(n)
                gate_tile(n + 1)
            head_out(HEADS - 1)
            act.wait_ge(o_sb, HEADS)
            nc.scalar.activation(att_hi[:], attT[:], ACT.Copy).then_inc(part_hi, 1)
            for i in range(CT):
                act.wait_ge(conv_c, i + 1)
                nc.scalar.activation(hc[:, i, 0:T], conv[:, i, :], ACT.Square).then_inc(conv_q, 1)
            act.wait_ge(conv_v, 1)
            nc.scalar.activation(rbc[:, 1, :], rbc[:, 0, :], ACT.Sqrt).then_inc(conv_s, 1)
            for i in range(CT):
                act.wait_ge(conv_y, i + 1)
                nc.scalar.activation(conv[:, i, :], conv[:, i, :], ACT.Silu, bias=convv[:, 2, i:i + 1],
                                     scale=convv[:, 1, i:i + 1]).then_inc(conv_a, 1)
            act.wait_ge(conv_a, CT)
            nc.scalar.activation(cvn_hi[:], conv[:], ACT.Copy).then_inc(part_hi, 1)
            for n in range(Y0, O0):
                hi(n + 2)
                if (n - Y0) % 2 == 1:
                    for m in (n - Y0 - 1, n - Y0):
                        act.wait_ge(m_raw, m + 1)
                        nc.scalar.activation(act_hi[:, m, :], ga[:, m, :], ACT.Copy).then_inc(a_hi, 1)
            for n in range(O0, W0):
                hi(n + 2)
            root(2)
            root(3)
            act_parts(KD)
            act.wait_ge(x1_out, 16)
            for n in range(W0, NBLK):
                if n + 2 < NBLK:
                    hi(n + 2)
                act.wait_ge(blk_mm, n + 1)
                nc.scalar.activation(qT[:, n - W0, :], bank[(n - W0) % 2][:, :], ACT.Copy).then_inc(z_act, 1)

            def part_u(c, slot):
                act.wait_ge(u_in[slot % RAW], 16 * (c // RAW + 1) if isinstance(c, int) else 4 * c + 16 - 4 * (slot % RAW))
                need(act, u_mm, c - 1)
                nc.scalar.activation(whi[:, slot % 2, :], raw[:, slot % RAW, :], ACT.Copy).then_inc(u_hi, 1)

            def gelu(c, slot, buf=gel):
                act.wait_ge(u_mm, c + 1)
                if buf is gel:
                    act.wait_ge(w_mul, c - LEAD + 1)
                nc.scalar.activation(buf[:, slot, :], bank[slot % 2][:, :], ACT.Gelu_apprx_tanh).then_inc(gel_r, 1)

            def ahead(c, p, last=False):
                if not isinstance(c, int) or c:
                    if (p - 1) % 4 == 0:
                        act.wait_ge(gel_out, 4 * (c - 1) if not isinstance(c, int) else max(16, 4 * (c - 1)))
                    gelu(c - 1, (p - 1) % PS, gelz)
                if not last:
                    part_u(c + 1, (p + 1) % PS)

            def gates(t, b):
                s, t0 = b // (TB // TOK), b % (TB // TOK) * TOK
                if t0 == 0:
                    act.wait_ge(stage_out[s], 16 * t + 16)
                act.wait_ge(gt_mm, NBT * t + (b + 1 + OH))
                nc.scalar.activation(stage[:, s, :, t0:t0 + TOK].rearrange("p i t -> p t i"),
                                     bank[2 + b % 2][:, :].rearrange("p (t i) -> p t i", t=TOK),
                                     ACT.Copy).then_inc(gt_sb, 1)
                if t0 == TB - TOK:
                    act.wait_ge(gt_sb, NBT * t + (b + 1 + 2))
                    dst = gates_dram[2 * t + s] if isinstance(t, int) else \
                        gates_dram[bass.ds(2 * t + s, 1)].rearrange("o p i t -> (o p) i t")
                    act.dma_start(dst, stage[:, s]).then_inc(stage_out[s], 16)

            def selecting(t, c0, p0):
                for j in range(PRE_T):
                    ahead(c0 + j, p0 + j)
                    if j == 8:
                        act.wait_ge(gate_sub, t + 1)
                        nc.scalar.activation(sel[:, 1, :, :], cv[:], ACT.Exp).then_inc(gate_exp, 1)

            def laying(t, c0, p0):
                for b in range(NBT):
                    if b % 8 == 1:
                        ahead(c0 + b // 8, p0 + b // 8)
                    gates(t, b)

            act.sem_inc(gt_sb, 2)
            for i in range(2):
                act.sem_inc(stage_out[i], 16)
            part_u(0, 0)
            selecting(0, 0, 0)
            with act.Fori(0, TT - 1) as it:
                selecting(it + 1, PER * it + PRE_T, PRE_T)
                laying(it, PER * it + 2 * PRE_T, 2 * PRE_T)
            laying(TT - 1, PRE - FILL - PRE_G, PRE - FILL - PRE_G)

            def part_w(c, k):
                act.wait_ge(w_mul, c + 1)
                nc.scalar.activation(eh[:, k, :], wf[:, k % 2, :], ACT.Copy).then_inc(w_hi, 1)

            def part_v(g, n):
                act.wait_ge(v_in[n % VR], 16 * (4 * g + n // VR + 1))
                need(act, v_mm, 16 * g + n - VR + 1)
                nc.scalar.activation(vhi[:, n % VR, :], vraw[:, n % VR, :], ACT.Copy).then_inc(v_hi, 1)

            for j in range(FILL):
                ahead(PRE - FILL + j, PRE - FILL + j, j == FILL - 1)
                if j >= 4:
                    if j == 4:
                        for i in range(2):
                            act.wait_ge(stage_out[i], 16 * (NTB // 2 + 1))
                    part_w(j - 4, j - 4)
            gelu(PRE - 1, (PRE - 1) % PS, gelz)

            def group(g, par, with_u, last):
                for k in range(GR):
                    cu = GR * g + LEAD + k
                    if with_u:
                        part_u(cu, k)
                    if k == 0:
                        part_w(GR * g + GR - 1, GR - 1)
                    part_v(g, k)
                    if with_u and k:
                        gelu(cu - 1, par * GR + k - 1)
                part_v(g, 8)
                part_v(g, 9)
                if with_u:
                    gelu(GR * g + LEAD + GR - 1, par * GR + GR - 1)
                part_v(g, 10)
                for k in range(GR):
                    if k + 11 < 16:
                        part_v(g, k + 11)
                    if k and not last:
                        part_w(GR * g + GR + k - 1, k - 1)

            for k in range(4, GR - 1):
                part_w(k, k)
            for g in range(FIRST):
                group(g, g % 2, GR * g + LEAD >= PRE, False)
            with act.Fori(FIRST // 2, NG // 2 - 1) as it:
                group(2 * it, 0, True, False)
                group(2 * it + 1, 1, True, False)
            group(NG - 2, 0, False, False)
            group(NG - 1, 1, False, True)
            root(4)

        @block.vector
        def _(dve):
            ch = Chain(dve, dch)
            link = ch.link
            done = [0]

            def until(n):
                while done[0] <= AT_STREAM[("w", n)]:
                    entry()

            def entry():
                s = done[0]
                kind, n = STREAM[s]
                dve.wait_ge(raw_in[s % RAW], 16 * (s // RAW + 1))
                if kind == "mod":
                    nc.vector.scalar_tensor_tensor(out=raw[:, s % RAW, :], in0=raw[:, s % RAW, :], scalar=1.0,
                                                   in1=cs[:], op0=ALU.mult, op1=ALU.mult,
                                                   accum_out=modc[:, n:n + 1]).then_inc(raw_free, 1)
                else:
                    dve.wait_ge(blk_hi, n + 1)
                    nc.vector.tensor_tensor(wlo[:, n % SPL, :], raw[:, s % RAW, :],
                                            whi[:, n % SPL, :].bitcast(F32), ALU.subtract).then_inc(raw_free, 1)
                done[0] += 1

            def norm(src, dst, roots, between=lambda: None):
                for t in range(TT):
                    for i in range(2):
                        last = nc.vector.bn_stats(stats[:, t, i, :], src[:, t, i * HALF:(i + 1) * HALF])
                    if t < TT - 1:
                        between()
                link(last)
                between()
                for t in range(TT):
                    last = nc.vector.bn_aggr(mv[:, t, :], stats[:, t, :, :].rearrange("p a b -> p (a b)"))
                link(last)
                nc.vector.tensor_scalar(sq[:, 0, :], mv[:, :, 1], EPS, None, ALU.add).then_inc(var_r, 1)
                between()
                dve.wait_ge(dev_r, roots)
                link(nc.vector.reciprocal(sq[:, 2, :], sq[:, 1, :]))
                link(nc.vector.tensor_tensor(sq[:, 3, :], sq[:, 2, :], sq[:, 2, :], ALU.mult))
                link(nc.vector.tensor_tensor(sq[:, 3, :], sq[:, 3, :], sq[:, 0, :], ALU.mult))
                link(nc.vector.tensor_scalar(sq[:, 3, :], sq[:, 3, :], -0.5, 1.5, ALU.mult, ALU.add))
                link(nc.vector.tensor_tensor(sq[:, 2, :], sq[:, 2, :], sq[:, 3, :], ALU.mult))
                for t in range(TT):
                    last = nc.vector.tensor_scalar(dst[:, t, :], src[:, t, :], mv[:, t, 0:1], sq[:, 2, t:t + 1],
                                                   ALU.subtract, ALU.mult)
                    if t < TT - 1:
                        between()
                return last

            def modulate(sh, sc, first):
                for kd in range(KD + 2):
                    if kd < KD:
                        dve.wait_ge(xT_mm, first + kd + 1)
                        nc.vector.tensor_scalar(uraw[:, kd, :], bank[kd][:, :], modc[:, sc + kd:sc + kd + 1],
                                                modc[:, sh + kd:sh + kd + 1], ALU.mult, ALU.add).then_inc(u_raw, 1)
                    if kd > 1:
                        dve.wait_ge(a_hi, first + (KD if first else 0) + kd - 1)
                        nc.vector.tensor_tensor(act_lo[:, kd - 2, :], uraw[:, kd - 2, :],
                                                act_hi[:, kd - 2, :].bitcast(F32), ALU.subtract).then_inc(a_lo, 1)

            def bias(m, n, one):
                link(nc.vector.tensor_tensor(modc[:, m:m + n], modc[:, m:m + n], bmod[:, m:m + n], ALU.add))
                if one:
                    link(nc.vector.tensor_scalar(modc[:, m:m + n], modc[:, m:m + n], 1.0, None, ALU.add))

            dve.wait_ge(cs_r, 1)
            for m in range(RAW):
                entry()
            dve.wait_ge(x_in, 16)
            norm(xres, xn, 1, entry).then_inc(xn_r, 1)
            while done[0] <= AT_STREAM[("mod", 15)]:
                entry()
            dve.wait_ge(small_in, 64)
            dve.wait_ge(raw_free, AT_STREAM[("mod", 15)] + 1)
            bias(0, 8, False)
            bias(8, 8, True)
            modulate(0, 8, 0)
            until(1)
            for n in range(G0):
                until(n + 2)
                if n == F0:
                    dve.wait_ge(blk_mm, n + 1)
                    nc.vector.tensor_scalar(frow[:, 2, :], bank[z_bank[n]][0:HEADS, :], bf[:, 0:1], None,
                                            ALU.add).then_inc(f_log, 1)
                    dve.wait_ge(f_log, 1)
                    nc.vector.memset(frow[:, 1, :], 1.0).then_inc(z_dve, 1)
                elif n == V0 + 2:
                    dve.wait_ge(f_exp, 1)
                    link(nc.vector.tensor_scalar(frow[:, 2, :], frow[:, 2, :], 0.0, None, ALU.min))
                    link(nc.vector.tensor_tensor(frow[:, 2, :], frow[:, 2, :], frow[:, 3, :], ALU.subtract))
                    link(nc.vector.tensor_tensor_scan(frow[:, 0, :], frow[:, 1, :], frow[:, 2, :], 0.0,
                                                      ALU.mult, ALU.add))
                    nc.vector.tensor_scalar(frow[:, 1, :], frow[:, 0, :], -1.0, None, ALU.mult).then_inc(f_ready, 1)
                elif n == C0 - 1:
                    dve.wait_ge(v_mm1, 1)
                    for t in range(2, 4):
                        nc.vector.tensor_copy(vals[:, t, :], bank[4 + t][:, :]).then_inc(v_dve, 1)
                elif n >= C0 and (n - C0) % 2 == 1:
                    i = (n - C0) // 2
                    dve.wait_ge(const_r, 1)
                    dve.wait_ge(z_act, by_act.index(n) + 1)
                    nc.vector.tensor_tensor(hc[:, i, TAPS - 1:], bank[z_bank[n - 1]][:, :], sg[:, i % 2, :],
                                            ALU.mult).then_inc(hc_r, 1)
                    dve.wait_ge(hc_r, i + 1)
                    nc.vector.nop().then_inc(z_dve, 1)

            def score_max(h, q):
                dve.wait_ge(s_mm, 4 * h + q + 1)
                w = P * (q + 1)
                link(nc.vector.tensor_tensor_reduce(out=bank[4 + q % 2][:, 0:w], in0=bank[4 + q % 2][:, 0:w],
                                                    in1=mask[:, T - w:T], scale=1.0, scalar=NEG,
                                                    op0=ALU.add, op1=ALU.max, accum_out=att_s[:, 0, q:q + 1]))
                nc.vector.tensor_scalar(att_s[:, 1, q:q + 1], att_s[:, 0, q:q + 1], -1.0, None,
                                        ALU.mult).then_inc(nmax, 1)

            def prob_norm(h, q):
                dve.wait_ge(p_exp, 4 * h + q + 1)
                w = P * (q + 1)
                link(nc.vector.reciprocal(att_s[:, 3, q:q + 1], att_s[:, 2, q:q + 1]))
                nc.vector.tensor_scalar(prob[:, tri(q):tri(q) + w], prob[:, tri(q):tri(q) + w], att_s[:, 3, q:q + 1],
                                        None, ALU.mult).then_inc(p_norm, 1)

            DC = CT - 1
            taps = [(k, i) for k in range(TAPS) for i in range(DC)]

            def tap(j):
                k, i = taps[j]
                if k == 0:
                    nc.vector.tensor_scalar(conv[:, i, :], hc[:, i, 0:T], convw[:, i, 0:1], convv[:, 0, i:i + 1],
                                            ALU.mult, ALU.add).then_inc(conv_d, 1)
                else:
                    dve.wait_ge(conv_d, j - DC + 1)
                    nc.vector.scalar_tensor_tensor(out=conv[:, i, :], in0=hc[:, i, k:k + T],
                                                   scalar=convw[:, i, k:k + 1], in1=conv[:, i, :],
                                                   op0=ALU.mult, op1=ALU.add).then_inc(conv_d, 1)

            dve.wait_ge(mask_r, 1)
            dve.wait_ge(hc_r, CT)
            share = (len(taps) + 2 * HEADS - 1) // (2 * HEADS)
            for h in range(HEADS):
                n = G0 + 2 * h
                score_max(h, 0)
                score_max(h, 1)
                prob_norm(h, 0)
                prob_norm(h, 1)
                until(n + 2)
                score_max(h, 2)
                score_max(h, 3)
                for j in range(2 * h * share, min((2 * h + 1) * share, len(taps))):
                    tap(j)
                prob_norm(h, 2)
                prob_norm(h, 3)
                until(n + 3)
                for j in range((2 * h + 1) * share, min((2 * h + 2) * share, len(taps))):
                    tap(j)
            dve.wait_ge(part_hi, 1)
            nc.vector.tensor_tensor(att_lo[:], attT[:], att_hi[:].bitcast(F32), ALU.subtract).then_inc(part_lo, 1)
            dve.wait_ge(conv_p, 1)
            dve.wait_ge(conv_d, len(taps))
            dve.wait_ge(conv_mm, 1)
            for i in range(CT):
                nc.vector.tensor_tensor(conv[:, i, :], conv[:, i, :], bank[4][:, :], ALU.subtract).then_inc(conv_c, 1)
            dve.wait_ge(conv_mm, 2)
            nc.vector.tensor_scalar(rbc[:, 0, :], bank[5][:, :], EPS, None, ALU.add).then_inc(conv_v, 1)
            dve.wait_ge(conv_s, 1)
            link(nc.vector.reciprocal(rbc[:, 2, :], rbc[:, 1, :]))
            link(nc.vector.tensor_tensor(rbc[:, 3, :], rbc[:, 2, :], rbc[:, 2, :], ALU.mult))
            link(nc.vector.tensor_tensor(rbc[:, 3, :], rbc[:, 3, :], rbc[:, 0, :], ALU.mult))
            link(nc.vector.tensor_scalar(rbc[:, 3, :], rbc[:, 3, :], -0.5, 1.5, ALU.mult, ALU.add))
            link(nc.vector.tensor_tensor(rbc[:, 2, :], rbc[:, 2, :], rbc[:, 3, :], ALU.mult))
            for i in range(CT):
                nc.vector.tensor_tensor(conv[:, i, :], conv[:, i, :], rbc[:, 2, :], ALU.mult).then_inc(conv_y, 1)
            dve.wait_ge(part_hi, 2)
            nc.vector.tensor_tensor(cvn_lo[:], conv[:], cvn_hi[:].bitcast(F32), ALU.subtract).then_inc(part_lo, 1)
            for n in range(Y0, O0):
                until(n + 2)
                if (n - Y0) % 2 == 1:
                    j = (n - Y0) // 2
                    dve.wait_ge(y_mm, n - Y0 + 1)
                    b = 4 * (j % 2)
                    for r in range(2):
                        nc.vector.tensor_tensor(ga[:, 2 * j + r, :], ga[:, 2 * j + r, :], bank[b + r][:, :], ALU.mult)
                        last = nc.vector.tensor_tensor(gb[:, 2 * j + r, :], gb[:, 2 * j + r, :], bank[b + 2 + r][:, :],
                                                       ALU.mult)
                    last.then_inc(y_free, 1)
                    dve.wait_ge(y_free, j + 1)
                    for r in range(2):
                        nc.vector.tensor_tensor(ga[:, 2 * j + r, :], ga[:, 2 * j + r, :], gb[:, 2 * j + r, :],
                                                ALU.add).then_inc(m_raw, 1)
                    for r in range(2):
                        m = 2 * j + r
                        dve.wait_ge(a_hi, KD + m + 1)
                        nc.vector.tensor_tensor(act_lo[:, m, :], ga[:, m, :], act_hi[:, m, :].bitcast(F32),
                                                ALU.subtract).then_inc(a_lo, 1)

            def diagonals(dst, m0):
                for m in range(KD):
                    last = nc.vector.tensor_scalar(dst[:, m, :], ident[:], modc[:, m0 + m:m0 + m + 1], None, ALU.mult)
                last.then_inc(g_dg, 1)

            def gate_row(dst, banks, n):
                dve.wait_ge(g_mm, n)
                for half in range(2):
                    last = nc.vector.tensor_scalar(dst[:, half * HALF:(half + 1) * HALF], bank[banks + half][:, :],
                                                   float(CC), 1.0, ALU.mult, ALU.add)
                last.then_inc(g_row, 1)

            bias(16, 8, False)
            diagonals(dg1, 16)
            gate_row(rows1[:, 0, :], 6, 1)
            for n in range(O0, W0):
                until(n + 2)
            bias(24, 8, False)
            bias(32, 8, True)
            bias(40, 8, False)
            dve.wait_ge(x_again, 16)
            dve.wait_ge(row_in, 32)
            dve.wait_ge(g_row, 1)
            for half in range(2):
                dve.wait_ge(o1_mm, half + 1)
                for t in range(TT):
                    cut = slice(half * HALF, (half + 1) * HALF)
                    last = nc.vector.tensor_tensor(outg[:, t, cut], bank[4 * half + t][:, :], rows1[:, 0, cut], ALU.mult)
            link(last)
            for t in range(TT):
                last = nc.vector.scalar_tensor_tensor(out=xres[:, t, :], in0=xres[:, t, :], scalar=ALPHA,
                                                      in1=outg[:, t, :], op0=ALU.mult, op1=ALU.add)
            link(last)
            link(norm(xres, outg, 2))
            for t in range(TT):
                last = nc.vector.tensor_tensor(outg[:, t, :], outg[:, t, :], rows1[:, 1, :], ALU.mult)
            link(last)
            for t in range(TT):
                last = nc.vector.tensor_tensor(xres[:, t, :], outg[:, t, :], rows1[:, 2, :], ALU.add)
                last.then_inc(x1_r, 1)
            dve.wait_ge(x1_r, TT)
            norm(xres, xn, 3).then_inc(xn_r, 1)
            modulate(24, 32, KD)
            until(NBLK - 1)

            def low_u(c, slot):
                dve.wait_ge(u_hi, c + 1)
                nc.vector.tensor_tensor(wlo[:, slot % 2, :], raw[:, slot % RAW, :],
                                        whi[:, slot % 2, :].bitcast(F32), ALU.subtract).then_inc(u_lo, 1)

            def best(lists, top, idx, spare, between, free=None):
                for o, v in zip(top, lists):
                    last = nc.vector.max(o[:, 0:8], v)
                link(last)
                between()
                for o, v, i in zip(top, lists, idx):
                    nc.vector.max_index(i[:, 0:8], o[:, 0:8], v)
                between()
                for o, v, w in zip(top, lists, spare):
                    last = nc.vector.match_replace(w, o[:, 0:8], v, NEG)
                link(last)
                if free is not None:
                    nc.vector.nop().then_inc(free, 1)
                between()
                for o, w in zip(top, spare):
                    last = nc.vector.max(o[:, 8:16], w)
                link(last)
                for o, w, i in zip(top, spare, idx):
                    last = nc.vector.max_index(i[:, 8:16], o[:, 8:16], w)
                link(last)

            both = [(h, s) for h in range(PH) for s in range(2)]
            heads = range(PH)

            def select(t, c0, p0):
                split = [0]

                def ahead():
                    if split[0] < PRE_T:
                        split[0] += 1
                        low_u(c0 + split[0], (p0 + split[0]) % PS)

                ahead()
                dve.wait_ge(sc_mm, t + 1)
                dve.sem_inc(alone, 1)
                best([bank[4 + h // 2][:, (h % 2) * 256 + s * NK:(h % 2) * 256 + (s + 1) * NK] for h, s in both],
                     [sv[:, h, s, :] for h, s in both], [si[:, h, s, :] for h, s in both],
                     [sc2[:, 2 * h + s, :] for h, s in both], ahead, sc_read)
                ahead()
                link(nc.vector.tensor_copy(sif[:], si[:]))
                link(nc.vector.tensor_scalar(sif[:, :, 0, :], sif[:, :, 0, :], float(NK), None, ALU.mult))
                for src, dst in ((sv, cand), (sif, ecand)):
                    off = 0
                    for a, na, nb in RECTS:
                        shape = [P, PH, na, nb]
                        last = nc.vector.tensor_tensor(
                            dst[:, :, off:off + na * nb].rearrange("p h (a b) -> p h a b", b=nb),
                            src[:, :, 0, a:a + na].unsqueeze(3).broadcast_to(shape),
                            src[:, :, 1, 0:nb].unsqueeze(2).broadcast_to(shape), ALU.add)
                        off += na * nb
                link(last)
                best([cand[:, h, :] for h in heads], [cv[:, h, :] for h in heads],
                     [pos[:, h, :] for h in heads], [cand2[:, h, :] for h in heads],
                     lambda: split[0] < 6 and ahead())
                ahead()
                nc.vector.tensor_copy(posf[:], pos[:])
                link(nc.vector.tensor_copy(gsum[:, 1, :], cv[:, :, 0]))
                nc.vector.tensor_tensor(cv[:], cv[:], gsum[:, 1, :].unsqueeze(2).broadcast_to([P, PH, TOPK]),
                                        ALU.subtract).then_inc(gate_sub, 1)

                def compare(h):
                    shape = [P, TOPK, NCAND]
                    nc.vector.tensor_tensor(eq[:, h % 2], posf[:, h, :].unsqueeze(2).broadcast_to(shape),
                                            iota[:, 0:NCAND].unsqueeze(1).broadcast_to(shape),
                                            ALU.is_equal).then_inc(eq_r, 1)

                compare(0)
                compare(1)
                for h in heads:
                    if h % 2 == 1:
                        ahead()
                    dve.wait_ge(eqm_r, 8 * t + (h + 1))
                    link(nc.vector.tensor_reduce(sel[:, 0, h, :], eq[:, h % 2], AX, ALU.add))
                    if h + 2 < PH:
                        compare(h + 2)
                dve.wait_ge(gate_exp, t + 1)
                link(nc.vector.tensor_reduce(gsum[:, 0, :], sel[:, 1, :, :], AX, ALU.add))
                link(nc.vector.reciprocal(gsum[:, 1, :], gsum[:, 0, :]))
                nc.vector.tensor_tensor(sel[:, 1, :, :], sel[:, 1, :, :],
                                        gsum[:, 1, :].unsqueeze(2).broadcast_to([P, PH, TOPK]),
                                        ALU.mult).then_inc(sel_r, 1)
                while split[0] < PRE_T:
                    ahead()

            def transposed(t):
                dve.wait_ge(selT_mm, t + 1)
                nc.vector.tensor_copy(selT[:, 2, :], bank[2][:, P:2 * P])
                link(nc.vector.tensor_copy(selI[:, 0, :], bank[2][:, 0:P]))
                link(nc.vector.tensor_scalar(selI[:, 1, :], selI[:, 0, :], NK - 1, None, ALU.bitwise_and))
                link(nc.vector.tensor_scalar(selI[:, 0, :], selI[:, 0, :], NK.bit_length() - 1, None,
                                             ALU.logical_shift_right))
                link(nc.vector.tensor_copy(selT[:, 0:2, :], selI[:]))
                nc.vector.nop().then_inc(selT_sb, 1)

            def one_hots(t, c0, p0):
                for b in range(NBT):
                    if b % 8 == 6:
                        low_u(c0 + (b // 8 + 1), (p0 + b // 8 + 1) % PS)
                    dve.wait_ge(gt_mm, NBT * t + (b + 1))
                    row = one[b % OH]
                    shape = [P, TOK, NK]
                    for r in range(2):
                        ins = nc.vector.tensor_tensor(
                            row[:, r], iota[:].unsqueeze(1).broadcast_to(shape),
                            selT[:, 1 - r, b * TOK:(b + 1) * TOK].unsqueeze(2).broadcast_to(shape), ALU.is_equal)
                    ins.then_inc(one_r, 1)

            low_u(0, 0)
            n0 = ch.n
            select(0, 0, 0)
            transposed(0)
            per = ch.n - n0
            with dve.Fori(0, TT - 1) as it:
                ch.turn = it * per
                select(it + 1, PER * it + PRE_T, PRE_T)
                one_hots(it, PER * it + 2 * PRE_T, 2 * PRE_T)
                dve.wait_ge(onem_r, NBT * it + NBT)
                transposed(it + 1)
            ch.turn = 0
            ch.n = n0 + TT * per
            one_hots(TT - 1, PRE - FILL - PRE_G, PRE - FILL - PRE_G)

            def weigh(g, k, slot):
                c = GR * g + k
                if isinstance(c, int) and c < PRE:
                    dve.wait_ge(back_in[c // 2 % 4], 16 * (c // 8 + 1))
                    src = gback[:, c // 2 % 4, c % 2, :]
                else:
                    dve.wait_ge(gel_r, c + 1)
                    src = gel[:, slot, :]
                s = (k // 2) % 2
                dve.wait_ge(g_in[s], 16 * (2 * g + k // 4 + 1))
                need(dve, v_mm, 16 * g + k - 7)
                need(dve, w_lo, c - 1)
                nc.vector.tensor_tensor(wf[:, k % 2, :].rearrange("p (b t) -> p b t", t=TB),
                                        src.rearrange("p (b t) -> p b t", t=TB),
                                        gring[:, s, :, k % 2, :], ALU.mult).then_inc(w_mul, 1)

            def low_w(g, k):
                dve.wait_ge(w_hi, GR * g + k + 1)
                nc.vector.tensor_tensor(el[:, k, :], wf[:, k % 2, :], eh[:, k, :].bitcast(F32),
                                        ALU.subtract).then_inc(w_lo, 1)

            def low_v(g, n):
                dve.wait_ge(v_hi, 16 * g + n + 1)
                nc.vector.tensor_tensor(vlo[:, n % VR, :], vraw[:, n % VR, :], vhi[:, n % VR, :].bitcast(F32),
                                        ALU.subtract).then_inc(v_lo, 1)

            def add(g, half, first):
                for t in range(TT):
                    dve.wait_ge(pv_mm, 8 * g + 4 * half + t + 1)
                    need(dve, pv_add, 8 * g + 4 * half + t - 7)
                    dst = acc[:, t, half * HALF:(half + 1) * HALF]
                    if first:
                        nc.vector.tensor_copy(dst, bank[2 + t][:, :]).then_inc(pv_add, 1)
                    else:
                        nc.vector.tensor_tensor(dst, dst, bank[2 + t][:, :], ALU.add).then_inc(pv_add, 1)

            def group(g, par, with_u, first, last, last_row=False):
                for k in range(GR):
                    if with_u:
                        low_u(GR * g + LEAD + k, k)
                    if k == 0:
                        weigh(g, GR - 1, par * GR + GR - 1)
                        low_w(g, GR - 1)
                    low_v(g, k)
                    if k == 0 and first is not True:
                        add(g - 1, 1, first == "second")
                if last:
                    dve.wait_ge(w_mul, CH)
                    diagonals(dg2, 40)
                for n in range(8, 11):
                    low_v(g, n)
                add(g, 0, first is True)
                if last:
                    gate_row(rows2[:, 0, :], 0, 2)
                for k in range(GR):
                    if k + 11 < 16:
                        low_v(g, k + 11)
                    if k and not last:
                        weigh(g + 1, k - 1, (1 - par) * GR + k - 1)
                        low_w(g + 1, k - 1)

            for j in range(FILL):
                if j < FILL - 1:
                    low_u(PRE - FILL + j + 1, (PRE - FILL + j + 1) % PS)
                if j == 4:
                    for i in range(2):
                        dve.wait_ge(stage_out[i], 16 * (NTB // 2 + 1))
                if j >= 4:
                    weigh(0, j - 4, j - 4)
                    low_w(0, j - 4)
            for k in range(4, GR - 1):
                weigh(0, k, k)
                low_w(0, k)
            for g in range(FIRST):
                group(g, g % 2, GR * g + LEAD >= PRE, (True, "second", False)[min(g, 2)], False)
            with dve.Fori(FIRST // 2, NG // 2 - 1) as it:
                group(2 * it, 0, True, False, False)
                group(2 * it + 1, 1, True, False, False)
            group(NG - 2, 0, False, False, False)
            group(NG - 1, 1, False, False, True)
            add(NG - 1, 1, False)
            dve.wait_ge(fin_in, 48)
            dve.wait_ge(g_row, 2)
            dve.wait_ge(pv_add, 8 * NG)
            for t in range(TT):
                last = nc.vector.tensor_tensor(acc[:, t, :], acc[:, t, :], rows2[:, 0, :], ALU.mult)
            link(last)
            for t in range(TT):
                last = nc.vector.scalar_tensor_tensor(out=xfin[:, t, :], in0=xfin[:, t, :], scalar=ALPHA,
                                                      in1=acc[:, t, :], op0=ALU.mult, op1=ALU.add)
            link(last)
            link(norm(xfin, acc, 4))
            for t in range(TT):
                last = nc.vector.tensor_tensor(acc[:, t, :], acc[:, t, :], rows2[:, 1, :], ALU.mult)
            link(last)
            for t in range(TT):
                nc.vector.tensor_tensor(xfin[:, t, :], acc[:, t, :], rows2[:, 2, :], ALU.add).then_inc(y_r, 1)

        @block.tensor
        def _(pe):
            mm = nc.tensor.matmul

            def three(o, wh, wl, mh, ml, start, stop):
                mm(o, wh, mh, start=start, stop=False)
                mm(o, wh, ml, start=False, stop=False)
                return mm(o, wl, mh, start=False, stop=stop)

            def transposes(turn):
                pe.wait_ge(xn_r, turn)
                for kd in range(KD):
                    for t in range(TT):
                        last = nc.tensor.transpose(bank[kd][:, t * P:(t + 1) * P], xn[:, t, kd * P:(kd + 1) * P],
                                                   ident[:])
                    last.then_inc(xT_mm, 1)

            def low_ready(n):
                pe.wait_ge(raw_free, AT_STREAM[("w", n)] + 1)

            def tile(n, o, parts=None):
                low_ready(n)
                for kd in range(KD):
                    if parts is not None:
                        pe.wait_ge(a_lo, parts + kd + 1)
                    w = slice(kd * P, (kd + 1) * P)
                    last = three(o, whi[:, n % SPL, w], wlo[:, n % SPL, w], act_hi[:, kd, :], act_lo[:, kd, :],
                                 kd == 0, kd == KD - 1)
                last.then_inc(blk_mm, 1)

            def rows_block(n, b, o0):
                low_ready(n)
                for kk in range(2):
                    kd = 2 * b + kk
                    w = slice(kk * HALF, (kk + 1) * HALF)
                    for t in range(TT):
                        c = slice(t * P, (t + 1) * P)
                        last = three(bank[o0 + t][:, :], act_hi[:, kd, c], act_lo[:, kd, c],
                                     whi[:, n % SPL, w], wlo[:, n % SPL, w], kd == 0, kd == KD - 1)
                last.then_inc(blk_mm, 1)
                return last

            pe.wait_ge(const_r, 1)
            transposes(1)
            for n in range(G0):
                if V0 <= n < C0:
                    rows_block(n, n - V0, 4)
                    if n == C0 - 1:
                        pe.wait_ge(blk_mm, C0)
                        pe.nop().then_inc(v_mm1, 1)
                else:
                    z_wait(pe, n)
                    if n == 0:
                        pe.wait_ge(u_raw, 1)
                    if n == 1:
                        pe.wait_ge(u_raw, 2)
                    tile(n, bank[z_bank[n]][:, :], 0 if n == 0 else None)

            def scores(h, q):
                need(pe, p_exp, 4 * h + q - 1)
                w = P * (q + 1)
                mm(bank[4 + q % 2][:, 0:w], qa[:, h, q * P:(q + 1) * P], ka[:, h, 0:w],
                   start=True, stop=True).then_inc(s_mm, 1)

            def prob_T(h, q):
                pe.wait_ge(p_norm, 4 * h + q + 1)
                need(pe, pT_sb, 4 * h + q - 1)
                for k in range(q + 1):
                    last = nc.tensor.transpose(bank[6 + q % 2][:, k * P:(k + 1) * P],
                                               prob[:, tri(q) + k * P:tri(q) + (k + 1) * P], ident[:])
                last.then_inc(pT_mm, 1)

            def attend(h):
                pe.wait_ge(pT_sb, 4 * h + 4)
                need(pe, o_sb, h)
                for k in range(TT):
                    last = mm(bank[3][0:DH, k * P:T], vals[:, k, h * DH:(h + 1) * DH], probT[:, k, k * P:T],
                              start=(k == 0), stop=(k == TT - 1))
                last.then_inc(o_mm, 1)

            pe.wait_ge(aug_in, 16 * 2 * HEADS)
            pe.wait_ge(z_act, 8)
            pe.wait_ge(v_act, 2)
            pe.wait_ge(v_dve, 2)
            for h in range(HEADS):
                n = G0 + 2 * h
                scores(h, 0)
                scores(h, 1)
                if h:
                    attend(h - 1)
                z_wait(pe, n)
                tile(n, bank[z_bank[n]][:, :])
                scores(h, 2)
                scores(h, 3)
                prob_T(h, 0)
                prob_T(h, 1)
                z_wait(pe, n + 1)
                tile(n + 1, bank[z_bank[n + 1]][:, :])
                prob_T(h, 2)
                prob_T(h, 3)
            attend(HEADS - 1)
            pe.wait_ge(conv_p, 1)
            pe.wait_ge(conv_d, (CT - 1) * TAPS)
            for i in range(CT):
                last = mm(bank[4][:, :], consts[:], conv[:, i, :], start=(i == 0), stop=(i == CT - 1))
            last.then_inc(conv_mm, 1)
            for i in range(CT):
                pe.wait_ge(conv_q, i + 1)
                last = mm(bank[5][:, :], consts[:], hc[:, i, 0:T], start=(i == 0), stop=(i == CT - 1))
            last.then_inc(conv_mm, 1)
            pe.wait_ge(z_act, len(by_act))
            pe.wait_ge(o_sb, HEADS)
            pe.wait_ge(conv_v, 1)
            for n in range(Y0, O0):
                j, branch = (n - Y0) // 2, (n - Y0) % 2
                need(pe, y_free, j - 1)
                pe.wait_ge(part_lo, branch + 1)
                low_ready(n)
                src_hi, src_lo = (att_hi, att_lo) if branch == 0 else (cvn_hi, cvn_lo)
                for r in range(2):
                    for k in range(AT):
                        w = slice((r * AT + k) * P, (r * AT + k + 1) * P)
                        last = three(bank[4 * (j % 2) + 2 * branch + r][:, :], whi[:, n % SPL, w], wlo[:, n % SPL, w],
                                     src_hi[:, k, :], src_lo[:, k, :], k == 0, k == AT - 1)
                last.then_inc(blk_mm, 1)
                pe.wait_ge(blk_mm, n + 1)
                pe.nop().then_inc(y_mm, 1)

            def gate_row(dg, banks, n):
                pe.wait_ge(g_dg, n)
                for half in range(2):
                    last = mm(bank[banks + half][:, :], consts[:],
                              dg[:, 4 * half:4 * half + 4, :].rearrange("p m c -> p (m c)"), start=True, stop=True)
                last.then_inc(g_mm, 1)

            pe.wait_ge(y_free, 4)
            gate_row(dg1, 6, 1)
            pe.wait_ge(g_row, 1)
            pe.wait_ge(a_lo, 2 * KD)
            for half in range(2):
                for b in range(4):
                    rows_block(O0 + 4 * half + b, b, 4 * half)
                pe.wait_ge(blk_mm, O0 + 4 * half + 4)
                pe.nop().then_inc(o1_mm, 1)
            transposes(2)
            for h in range(PH):
                need(pe, z_act, len(by_act) + h - 1 if h > 1 else 0)
                if h < 2:
                    pe.wait_ge(u_raw, KD + h + 1)
                tile(W0 + h, bank[h % 2][:, :], 2 * KD if h == 0 else None)
            pe.wait_ge(small_in, 96)
            pe.wait_ge(z_act, len(by_act) + PH)

            def first_product(c, slot, kds=range(KD)):
                if kds[0] == 0:
                    pe.wait_ge(u_lo, c + 1)
                    need(pe, gel_r, c - 1)
                for kd in kds:
                    w = slice(kd * P, (kd + 1) * P)
                    last = three(bank[slot % 2][:, :], whi[:, slot % 2, w], wlo[:, slot % 2, w],
                                 act_hi[:, kd, :], act_lo[:, kd, :], kd == 0, kd == KD - 1)
                if kds[-1] == KD - 1:
                    last.then_inc(u_mm, 1)

            def retrieval_scores(t):
                need(pe, sc_read, t)
                for h in range(PH):
                    last = mm(bank[4 + h // 2][:, (h % 2) * 256:(h % 2 + 1) * 256], qT[:, h, t * P:(t + 1) * P],
                              keys[:], start=True, stop=True)
                last.then_inc(sc_mm, 1)

            def sel_T(t):
                pe.wait_ge(sel_r, t + 1)
                pe.wait_ge(gt_sb, NBT * t + 2)
                for r in range(2):
                    last = nc.tensor.transpose(bank[2][:, r * P:(r + 1) * P],
                                               sel[:, r, :, :].rearrange("p h k -> p (h k)"), ident[:])
                last.then_inc(selT_mm, 1)

            def token_gates(t, b):
                n = NBT * t + b
                pe.wait_ge(onem_r, n + 1)
                pe.wait_ge(gt_sb, n + 1)
                if b == 0:
                    pe.wait_ge(selT_sb, t + 1)
                row = one[b % OH]
                for j in range(TOK):
                    last = mm(bank[2 + b % 2][:, j * NK:(j + 1) * NK], row[:, 0, j, :], row[:, 1, j, :],
                              start=True, stop=True)
                last.then_inc(gt_mm, 1)

            def selecting(t, c0, p0):
                for j in range(PRE_T):
                    first_product(c0 + j, (p0 + j) % PS)
                    if j == PRE_T // 2 - 1 and t + 1 < TT:
                        retrieval_scores(t + 1)

            def laying(t, c0, p0):
                for b in range(NBT):
                    token_gates(t, b)
                    if b % 2 == 1:
                        first_product(c0 + b // 8, (p0 + b // 8) % PS, range(b % 8 - 1, b % 8 + 1))

            pe.sem_inc(gt_mm, OH)
            retrieval_scores(0)
            selecting(0, 0, 0)
            sel_T(0)
            for t in range(TT - 1):
                c0 = PRE_T + PER * t
                selecting(t + 1, c0, c0)
                laying(t, c0 + PRE_T, c0 + PRE_T)
                sel_T(t + 1)
            laying(TT - 1, PRE - FILL - PRE_G, PRE - FILL - PRE_G)
            for c in range(PRE - FILL, PRE):
                first_product(c, c % PS)
            pe.wait_ge(gt_sb, T // TOK + 2)

            def second_product(g, k, half):
                n = half * GR + k
                pe.wait_ge(v_lo, 16 * g + n + 1)
                pe.wait_ge(w_lo, GR * g + k + 1)
                for t in range(TT):
                    if k == 0:
                        need(pe, pv_add, 8 * g + 4 * half + t - 3)
                    c = slice(t * P, (t + 1) * P)
                    last = three(bank[2 + t][:, :], eh[:, k, c], el[:, k, c], vhi[:, n % VR, :], vlo[:, n % VR, :],
                                 k == 0, k == GR - 1)
                    if k == GR - 1 and t < TT - 1:
                        last.then_inc(pv_mm, 1)
                last.then_inc(v_mm, 1)
                if k == GR - 1:
                    pe.wait_ge(v_mm, 16 * g + n + 1)
                    pe.nop().then_inc(pv_mm, 1)

            def group(g, with_u, last=False):
                for k in range(GR):
                    if with_u:
                        first_product(GR * g + LEAD + k, k)
                    second_product(g, k, 0)
                if last:
                    gate_row(dg2, 0, 2)
                for k in range(GR):
                    second_product(g, k, 1)

            for g in range(FIRST):
                group(g, GR * g + LEAD >= PRE)
            with pe.Fori(FIRST // 2, NG // 2 - 1) as it:
                group(2 * it, True)
                group(2 * it + 1, True)
            group(NG - 2, False)
            group(NG - 1, False, True)


def kernel(**inputs):
    import numpy as np
    import concourse.bacc as _bacc
    from concourse import mybir as _mybir
    from concourse.bass_utils import run_bass_kernel_spmd as _run

    a = {k: np.asarray(v) for k, v in inputs.items()}

    def tiles(w):
        return w.reshape(KD, P, -1, P).transpose(2, 1, 0, 3).reshape(-1, P, D)

    def branch(w):
        return w.reshape(AT, P, 4, 2, P).transpose(2, 1, 3, 0, 4).reshape(4, P, D)

    w_in = a["w_in"][0]
    o = [0, AW, 2 * AW, 3 * AW, 3 * AW + HEADS]
    ca, cbc = o[4], o[4] + CC
    gates = cbc + CC
    wv = w_in[:, o[2]:o[3]].reshape(4, 2, P, AW).transpose(0, 2, 1, 3).reshape(4, P, D)
    pairs = np.stack([tiles(w_in[:, ca:cbc]), tiles(w_in[:, cbc:gates])], 1).reshape(2 * CT, P, D)
    branches = np.stack([branch(a["w_attn_out"][0]), branch(a["w_conv_out"][0])], 1).reshape(8, P, D)
    w_out = a["w_out"][0].reshape(4, 2, P, 2, HALF).transpose(3, 0, 2, 1, 4).reshape(8, P, D)
    wblk = np.concatenate([
        tiles(w_in[:, o[0]:o[1]]), tiles(w_in[:, o[1]:o[2]]), tiles(w_in[:, o[3]:o[3] + P]), wv, pairs,
        tiles(w_in[:, gates:]), branches, w_out, tiles(a["peer_wq"][0])])
    arrays = {
        "x": a["x"][0],
        "cb": a["c"],
        "b_modc": a["b_mod"][0].reshape(MODT, P).T,
        "w_modt": a["w_mod"][0].T.reshape(MODT, P, D),
        "wblk": wblk,
        "b_fc": a["b_f"][0][:, None],
        "conv_wc": a["conv_w"][0].reshape(TAPS, CT, P).transpose(2, 1, 0),
        "conv_vec": np.stack([a["conv_b"][0], a["conv_ln_g"][0], a["conv_ln_b"][0]]).reshape(3, CT, P).transpose(2, 0, 1),
        "keys_t": a["peer_sub_keys"][0].transpose(0, 2, 1),
        "u_t": a["peer_u"][0].reshape(CH, P, KD, P).transpose(0, 3, 2, 1).reshape(CH, P, D),
        "v_tab": a["peer_v"][0],
        "rows": np.stack([a["ln1_g"][0], a["ln1_b"][0], a["ln2_g"][0], a["ln2_b"][0]]),
    }
    nc = _bacc.Bacc("TRN2", target_bir_lowering=False, num_devices=1)
    feeds, args = {}, []
    for name, arr in arrays.items():
        arr = np.ascontiguousarray(arr)
        feeds[f"in_{name}_dram"] = arr
        args.append(nc.dram_tensor(f"in_{name}_dram", arr.shape, _mybir.dt.from_np(arr.dtype), kind="ExternalInput").ap())
    args.append(nc.dram_tensor("out_0_dram", (T, D), F32, kind="ExternalOutput").ap())
    build(nc, *args)
    r = _run(nc, [feeds], core_ids=[0])
    return r.results[0]["out_0_dram"].reshape(1, T, D)
```

```python
from contextlib import ExitStack

import concourse.bass as bass
from concourse import mybir

F32 = mybir.dt.float32
F32R = mybir.dt.float32r
I32 = mybir.dt.int32
U32 = mybir.dt.uint32
ALU = mybir.AluOpType
ACT = mybir.ActivationFunctionType
AX = mybir.AxisListType.X

P = 128
D = 1024
T = 512
KD = D // P
TT = T // P
HEADS = 8
DH = 64
AW = HEADS * DH
AT = AW // P
CC = 512
CT = CC // P
TAPS = 31
PH = 8
NK = 128
TOPK = 16
MODT = 6 * D // P
EPS = 1e-5
ALPHA = 2.0 ** 0.25
NEG = -3.0e38
HALF = D // 2

Q0, K0, F0, V0, C0, G0 = 0, 4, 8, 9, 13, 21
Y0, O0, W0, NBLK = 37, 45, 53, 61
RAW = 4
SPL = 3
STREAM = [("mod", 0), ("mod", 8), ("mod", 1), ("mod", 9), ("w", 0), ("mod", 2), ("w", 1), ("mod", 10), ("w", 2)]
for _m in range(3, 8):
    STREAM += [("mod", _m), ("mod", _m + 8)]
for _n in range(3, NBLK):
    STREAM.append(("w", _n))
    if G0 <= _n < G0 + 32:
        STREAM.append(("mod", _n - G0 + 16))
AT_STREAM = {e: s for s, e in enumerate(STREAM)}

RECTS = [(0, 1, 16), (1, 1, 8), (2, 2, 5), (4, 4, 3), (8, 8, 1)]
NCAND = sum(na * nb for _, na, nb in RECTS)

CH = NK
GR = 8
LEAD = 16
TB = 64
NTB = T // TB
TOK = 4
NBT = P // TOK
OH = 4
PRE_T, PRE_G, FILL = 12, 4, 8
PER = PRE_T + PRE_G
PRE = TT * PER + FILL
PS = 8
VR = 4


def build(nc, x, cb, b_modc, w_modt, wblk, b_fc, conv_wc, conv_vec, keys_t, u_t, v_tab, rows, out):
    with ExitStack() as ctx:
        KB = 1024
        base = (nc.sbuf_base + 31) // 32 * 32

        def sb(name, shape, dt, kb):
            return nc.alloc_sbuf_tensor_at(name, shape, dt, offset=base + int(kb * KB))

        def sem(name):
            return ctx.enter_context(nc.semaphore(name))

        bank = [ctx.enter_context(nc.psum_tensor(f"bank{i}", [P, 512], F32)) for i in range(8)]

        act_hi = sb("act_hi", [P, KD, T], F32R, 0)
        act_lo = sb("act_lo", [P, KD, T], F32R, 16)
        raw = sb("raw", [P, RAW, D], F32, 32)
        whi = sb("whi", [P, SPL, D], F32R, 48)
        wlo = sb("wlo", [P, SPL, D], F32R, 60)
        whi0 = sb("whi0", [P, D], F32R, 141)
        wlo0 = sb("wlo0", [P, D], F32R, 145)
        xres = sb("xres", [P, TT, D], F32, 72)
        prob = sb("prob", [P, 1280], F32, 72)
        probT = sb("probT", [P, TT, T], F32, 77)
        qa = sb("qa", [DH + 2, HEADS, T], F32, 88)
        ka = sb("ka", [DH + 2, HEADS, T], F32, 104)
        att_hi = sb("att_hi", [P, AT, T], F32R, 88)
        att_lo = sb("att_lo", [P, AT, T], F32R, 96)
        cvn_hi = sb("cvn_hi", [P, CT, T], F32R, 104)
        cvn_lo = sb("cvn_lo", [P, CT, T], F32R, 112)
        vals = sb("vals", [P, TT, AW], F32, 120)
        sg = sb("sg", [P, 2, T], F32, 128)
        rows1 = sb("rows1", [P, 3, D], F32, 120)
        hc = sb("hc", [P, CT, T + TAPS - 1], F32, 132)
        conv = sb("conv", [P, CT, T], F32, 141)
        ga = sb("ga", [P, KD, T], F32, 149)
        gb = sb("gb", [P, KD, T], F32, 165)
        xn = sb("xn", [P, TT, D], F32, 149)
        uraw = sb("uraw", [P, KD, T], F32, 165)
        attT = sb("attT", [P, AT, T], F32, 181)
        frow = sb("frow", [HEADS, 4, T], F32, 189)
        cs = sb("cs", [P, D], F32, 197)
        ptmp = sb("ptmp", [P, T], F32, 189)
        rbc = sb("rbc", [P, 4, T], F32, 189)
        qT = sb("qT", [P, PH, T], F32, 72)
        gelz = sb("gelz", [P, PS, T], F32, 88)
        gel = sb("gel", [P, LEAD, T], F32, 88)
        gback = sb("gback", [P, 4, 2, T], F32, 72)
        stage = sb("stage", [P, 2, NK, TB], F32, 120)
        eq = sb("eq", [P, 2, TOPK, NCAND], F32, 192)
        acc = sb("acc", [P, TT, D], F32, 120)
        eh = sb("eh", [P, GR, T], F32R, 136)
        el = sb("el", [P, GR, T], F32R, 152)
        vraw = sb("vraw", [P, VR, HALF], F32, 168)
        vhi = sb("vhi", [P, VR, HALF], F32R, 176)
        vlo = sb("vlo", [P, VR, HALF], F32R, 184)
        vhi2 = sb("vhi2", [P, VR, HALF], F32R, 104)
        vlo2 = sb("vlo2", [P, VR, HALF], F32R, 112)
        gring = sb("gring", [P, 2, NTB, 2, TB], F32, 192)
        wf = sb("wf", [P, 2, T], F32, 56)
        sc2 = sb("sc2", [P, 2 * PH, NK], F32, 112)
        one = [sb(f"one{i}", [P, 2, TOK, NK], F32, kb) for i, kb in enumerate((184, 188, 112, 116))]
        selT = sb("selT", [P, 3, P], F32, 199)
        outg = sb("outg", [P, TT, D], F32, 149)
        dg1 = sb("dg1", [P, KD, P], F32, 189)
        dg2 = sb("dg2", [P, KD, P], F32, 100)
        xfin = sb("xfin", [P, TT, D], F32, 72)
        rows2 = sb("rows2", [P, 3, D], F32, 88)
        cur = [201 * KB]

        def small(name, shape, dt):
            n = 4
            for s in shape[1:]:
                n *= s
            t = nc.alloc_sbuf_tensor_at(name, shape, dt, offset=base + cur[0])
            cur[0] += (n + 31) // 32 * 32
            return t

        ident = small("ident", [P, P], F32)
        iota = small("iota", [P, NK], F32)
        consts = small("consts", [P, P], F32)
        modc = small("modc", [P, MODT], F32)
        bmod = small("bmod", [P, MODT], F32)
        convw = small("convw", [P, CT, TAPS], F32)
        convv = small("convv", [P, 3, CT], F32)
        bf = small("bf", [HEADS, 1], F32)
        stats = small("stats", [P, TT, 2, 6], F32)
        mv = small("mv", [P, TT, 2], F32)
        sq = small("sq", [P, 4, TT], F32)
        att_s = small("att_s", [P, 4, TT], F32)
        assert cur[0] <= nc.sbuf_usable_end - base, cur[0]
        mask = sb("mask", [P, T], F32, 85.5)
        keys = sb("keys", [P, 2 * NK], F32, 104)
        sv = sb("sv", [P, PH, 2, TOPK], F32, 57)
        si = sb("si", [P, PH, 2, TOPK], U32, 58)
        sif = sb("sif", [P, PH, 2, TOPK], F32, 59)
        cv = sb("cv", [P, PH, TOPK], F32, 68)
        pos = sb("pos", [P, PH, TOPK], U32, 68.5)
        posf = sb("posf", [P, PH, TOPK], F32, 69)
        sel = sb("sel", [P, 2, PH, TOPK], F32, 69.5)
        gsum = sb("gsum", [P, 2, PH], F32, 70.5)
        selI = sb("selI", [P, 2, P], I32, 71)
        cand = sb("cand", [P, PH, NCAND], F32, 184)
        cand2 = sb("cand2", [P, PH, NCAND], F32, 186)
        ecand = sb("ecand", [P, PH, NCAND], F32, 188)

        gates_dram = nc.dram_tensor("gates_by_key", [NTB, P, NK, TB], F32, kind="Internal").ap()
        gel_dram = nc.dram_tensor("gelu_ahead", [PRE // 4, P, 4, T], F32, kind="Internal").ap()
        x1_dram = nc.dram_tensor("x_after_first", [TT, P, D], F32, kind="Internal").ap()

        small_in = sem("small_in")
        x_in = [sem(f"x_in{t}") for t in range(TT)]
        c_in = sem("c_in")
        raw_in = [sem(f"raw_in{i}") for i in range(RAW)]
        raw_free = sem("raw_free")
        blk_hi = sem("blk_hi")
        blk_mm = sem("blk_mm")
        dch = sem("dch")
        ach = sem("ach")
        pch = sem("pch")
        const_r = sem("const_r")
        mask_r = sem("mask_r")
        cs_r = sem("cs_r")
        var_r = sem("var_r")
        dev_r = sem("dev_r")
        xn_r = sem("xn_r")
        xT_mm = sem("xT_mm")
        mod_r = sem("mod_r")
        u_raw = sem("u_raw")
        a_hi = sem("a_hi")
        a_lo = sem("a_lo")
        z_act = sem("z_act")
        z_dve = sem("z_dve")
        f_log = sem("f_log")
        f_exp = sem("f_exp")
        f_ready = sem("f_ready")
        aug_in = sem("aug_in")
        v_mm1 = sem("v_mm1")
        v_act = sem("v_act")
        v_dve = sem("v_dve")
        hc_r = sem("hc_r")
        s_mm = sem("s_mm")
        nmax = sem("nmax")
        p_exp = sem("p_exp")
        p_norm = sem("p_norm")
        pT_mm = sem("pT_mm")
        pT_sb = sem("pT_sb")
        o_mm = sem("o_mm")
        o_sb = sem("o_sb")
        scale_r = sem("scale_r")
        xa_r = sem("xa_r")
        x1_p = sem("x1_p")
        y_p = sem("y_p")
        conv_p = sem("conv_p")
        conv_d = sem("conv_d")
        conv_mm = sem("conv_mm")
        conv_c = sem("conv_c")
        conv_q = sem("conv_q")
        conv_v = sem("conv_v")
        conv_s = sem("conv_s")
        conv_y = sem("conv_y")
        conv_a = sem("conv_a")
        part_hi = sem("part_hi")
        part_lo = sem("part_lo")
        y_free = sem("y_free")
        m_raw = sem("m_raw")
        g_dg = sem("g_dg")
        g_mm = sem("g_mm")
        g_row = sem("g_row")
        row_in = sem("row_in")
        x_again = sem("x_again")
        x1_in = sem("x1_in")
        o1_mm = sem("o1_mm")
        x1_r = sem("x1_r")
        x1_out = sem("x1_out")
        sc_mm = sem("sc_mm")
        sc_read = sem("sc_read")
        gate_sub = sem("gate_sub")
        gate_exp = sem("gate_exp")
        sel_r = sem("sel_r")
        selT_mm = sem("selT_mm")
        selT_sb = sem("selT_sb")
        eq_r = sem("eq_r")
        eqm_r = sem("eqm_r")
        one_r = sem("one_r")
        onem_r = sem("onem_r")
        gt_mm = sem("gt_mm")
        gt_sb = sem("gt_sb")
        stage_out = [sem(f"stage_out{i}") for i in range(2)]
        gel_out = sem("gel_out")
        back_in = [sem(f"back_in{i}") for i in range(4)]
        u_in = [sem(f"u_in{i}") for i in range(RAW)]
        u_hi = sem("u_hi")
        u_lo = sem("u_lo")
        u_mm = sem("u_mm")
        gel_r = sem("gel_r")
        w_mul = sem("w_mul")
        w_hi = sem("w_hi")
        w_lo = sem("w_lo")
        v_in = [sem(f"v_in{i}") for i in range(VR)]
        v_hi = sem("v_hi")
        v_lo = sem("v_lo")
        v_mm = sem("v_mm")
        g_in = [sem(f"g_in{i}") for i in range(2)]
        pv_mm = sem("pv_mm")
        pv_add = sem("pv_add")
        fin_in = sem("fin_in")
        y_r = sem("y_r")
        y_out = sem("y_out")
        alone = sem("alone")

        class Chain:

            def __init__(self, eng, s):
                self.eng, self.s, self.n, self.turn = eng, s, 0, 0

            def link(self, ins):
                self.n += 1
                ins.then_inc(self.s, 1)
                self.eng.wait_ge(self.s, self.turn + self.n)
                if not isinstance(self.turn, int):
                    self.eng.sem_inc(alone, 1)

        def need(eng, s, value):
            if not isinstance(value, int) or value > 0:
                eng.wait_ge(s, value)

        def v_slot(n, last):
            if last and 8 <= n < 12:
                return vhi2[:, n - 8, :], vlo2[:, n - 8, :]
            return vhi[:, n % VR, :], vlo[:, n % VR, :]

        def v_before(n, last):
            if last and n >= 8:
                return n - 8 if n >= 12 else None
            return n - VR

        def w_parts(n):
            return (whi0, wlo0) if n == 0 else (whi[:, n % SPL, :], wlo[:, n % SPL, :])

        Y_BANK = (0, 2, 6, 4)

        TILES = list(range(V0)) + list(range(C0, Y0))
        z_bank = {n: (n % 3 if n < V0 else (n - C0) % 4 if n < G0 else (n - G0) % 3) for n in TILES}
        by_dve = [n for n in TILES if n == F0 or (C0 <= n < G0 and (n - C0) % 2 == 0)]
        by_act = [n for n in TILES if n not in by_dve]

        def z_wait(pe, n):
            last = [m for m in TILES if m < n and z_bank[m] == z_bank[n]]
            if last:
                m = last[-1]
                if m in by_dve:
                    pe.wait_ge(z_dve, by_dve.index(m) + 1)
                else:
                    pe.wait_ge(z_act, by_act.index(m) + 1)

        def tri(q):
            return P * q * (q + 1) // 2

        v_half = v_tab.rearrange("(c e) (h d) -> c h e d", e=P, h=2)
        NG = CH // GR
        FIRST = PRE // GR
        LOOP = (NG - 3 - FIRST) // 2
        assert GR * FIRST == PRE and FIRST + 2 * LOOP == NG - 3 and FIRST % 2 == 1

        def u_beside(g):
            return PRE <= GR * g + LEAD < CH


        block = ctx.enter_context(nc.Block())

        @block.sync
        def _(sp):
            sp.dma_start(cs[:], cb.broadcast_to([P, D])).then_inc(c_in, 16)
            for s in range(RAW):
                sp.dma_start(raw[:, s, :], w_modt[STREAM[s][1]]).then_inc(raw_in[s], 16)
                sp.dma_start(xres[:, s, :], x[s * P:(s + 1) * P, :]).then_inc(x_in[s], 16)
            for dst, src in ((bmod[:], b_modc), (bf[:], b_fc), (convw[:], conv_wc), (convv[:], conv_vec)):
                sp.dma_start(dst, src).then_inc(small_in, 16)

            def stream(s):
                kind, n = STREAM[s]
                if s >= RAW:
                    sp.wait_ge(raw_free, s - RAW + 1)
                sp.dma_start(raw[:, s % RAW, :], w_modt[n] if kind == "mod" else wblk[n]).then_inc(raw_in[s % RAW], 16)

            s_f = AT_STREAM[("w", C0 + 2)]
            for s in range(RAW, s_f):
                stream(s)
            sp.wait_ge(f_ready, 1)
            for h in range(HEADS):
                sp.dma_start(qa[DH:DH + 1, h, :], frow[h:h + 1, 0, :]).then_inc(aug_in, 16)
                sp.dma_start(ka[DH + 1:DH + 2, h, :], frow[h:h + 1, 1, :]).then_inc(aug_in, 16)
            for s in range(s_f, len(STREAM)):
                stream(s)
            sp.wait_ge(const_r, 2)
            for side in range(2):
                sp.dma_start(keys[side * DH:(side + 1) * DH, side * NK:(side + 1) * NK],
                             keys_t[side]).then_inc(small_in, 16)
            def load_u(c, slot):
                need(sp, u_lo, c - RAW + 1)
                src = u_t[c] if isinstance(c, int) else u_t[bass.ds(c, 1)].rearrange("o p d -> (o p) d")
                sp.dma_start(raw[:, slot, :], src).then_inc(u_in[slot], 16)

            def load_v(g, k, half):
                n, c = half * GR + k, GR * g + k
                need(sp, v_lo, 16 * g + n - VR + 1)
                src = v_half[c, half] if isinstance(c, int) else \
                    v_half[bass.ds(c, 1), half].rearrange("o e d -> (o e) d")
                sp.dma_start(vraw[:, n % VR, :], src).then_inc(v_in[n % VR], 16)

            sp.wait_ge(raw_free, len(STREAM))

            def store_gel(m, slot):
                sp.wait_ge(gel_out, 16 * m + 16)
                sp.wait_ge(gel_r, 4 * m + 4)
                dst = gel_dram[m] if isinstance(m, int) else \
                    gel_dram[bass.ds(m, 1)].rearrange("o p c t -> (o p) c t")
                sp.dma_start(dst, gelz[:, 4 * slot:4 * slot + 4, :]).then_inc(gel_out, 16)

            sp.sem_inc(gel_out, 16)
            for c in range(PRE_T):
                load_u(c, c % RAW)
                if c % 4 == 3 and c > 3:
                    store_gel(c // 4 - 1, c // 4 - 1)
            with sp.Fori(0, TT - 1) as it:
                for i in range(PER // 4):
                    for j in range(4):
                        load_u(PER * it + (PRE_T + 4 * i + j), j)
                    store_gel(PER // 4 * it + (PRE_T // 4 + i - 1), (PRE_T // 4 + i - 1) % (PS // 4))
            for c in range(PRE - FILL - PRE_G, PRE):
                load_u(c, c % RAW)
                if c % 4 == 3:
                    store_gel(c // 4 - 1, (c // 4 - 1) % (PS // 4))
            for i in range(2):
                sp.wait_ge(stage_out[i], 16 * (NTB // 2 + 1))
            for k in range(VR):
                load_v(0, k, 0)
            store_gel(PRE // 4 - 1, (PRE // 4 - 1) % (PS // 4))

            def group(g, with_u):
                for k in range(GR):
                    if with_u:
                        load_u(GR * g + LEAD + k, k % RAW)
                    if not isinstance(g, int) or g > 0 or k >= VR:
                        load_v(g, k, 0)
                for k in range(GR):
                    load_v(g, k, 1)

            for g in range(FIRST):
                group(g, u_beside(g))
            with sp.Fori(0, LOOP) as it:
                group(2 * it + FIRST, True)
                group(2 * it + (FIRST + 1), True)
            group(NG - 3, True)
            sp.wait_ge(x1_out, 16)
            sp.dma_start(xfin[:], x1_dram.rearrange("t p d -> p t d")).then_inc(x1_in, 16)
            group(NG - 2, False)
            for k in range(GR):
                load_v(NG - 1, k, 0)
            sp.wait_ge(w_mul, CH)
            for i in range(2):
                sp.dma_start(rows2[:, 1 + i, :], rows[2 + i:3 + i].broadcast_to([P, D])).then_inc(fin_in, 16)
            for k in range(GR):
                load_v(NG - 1, k, 1)
            for t in range(TT):
                if t < 3:
                    sp.wait_ge(y_p, t + 1)
                    sp.dma_start(out[t * P:(t + 1) * P, :], xfin[:, t, :]).then_inc(y_out, 16)
                else:
                    for half in range(2):
                        sp.wait_ge(y_r, half + 1)
                        cut = slice(half * HALF, (half + 1) * HALF)
                        sp.dma_start(out[t * P:(t + 1) * P, cut], xfin[:, t, cut]).then_inc(y_out, 16)
            sp.wait_ge(y_out, 16 * (TT + 1))

        @block.gpsimd
        def _(pool):
            ch = Chain(pool, pch)
            ch.link(nc.gpsimd.memset(ident[:], 0.0))
            ch.link(nc.gpsimd.affine_select(out=ident[:], in_=ident[:], compare_op=ALU.not_equal, fill=1.0,
                                            base=0, pattern=[[-1, P]], channel_multiplier=1))
            nc.gpsimd.iota(iota[:], pattern=[[1, NK]], base=0, channel_multiplier=0,
                           allow_small_or_imprecise_dtypes=True)
            nc.gpsimd.memset(consts[:], 1.0 / CC)
            ch.link(nc.gpsimd.memset(hc[:, :, 0:TAPS - 1], 0.0))
            ch.link(nc.gpsimd.memset(qa[DH:DH + 2, :, :], 1.0))
            nc.gpsimd.memset(ka[DH:DH + 2, :, :], 1.0).then_inc(const_r, 1)
            pool.wait_ge(const_r, 1)
            pool.wait_ge(xa_r, 2)
            ch.link(nc.gpsimd.memset(mask[:], 0.0))
            nc.gpsimd.affine_select(out=mask[:], in_=mask[:], compare_op=ALU.is_ge, fill=NEG,
                                    base=T - P, pattern=[[-1, T]], channel_multiplier=1).then_inc(mask_r, 1)
            i = CT - 1
            pool.wait_ge(small_in, 64)
            pool.wait_ge(hc_r, CT)
            pool.wait_ge(aug_in, 16 * 2 * HEADS)
            ch.link(nc.gpsimd.tensor_scalar(conv[:, i, :], hc[:, i, 0:T], convw[:, i, 0:1], convv[:, 0, i:i + 1],
                                            ALU.mult, ALU.add))
            for k in range(1, TAPS):
                ch.link(nc.gpsimd.tensor_scalar(ptmp[:], hc[:, i, k:k + T], convw[:, i, k:k + 1], None, ALU.mult))
                ch.link(nc.gpsimd.tensor_tensor(conv[:, i, :], conv[:, i, :], ptmp[:], ALU.add))
            pool.nop().then_inc(conv_p, 1)
            pool.wait_ge(o_mm, HEADS)
            for t in range(TT):
                pool.dma_start(xres[:, t, :], x[t * P:(t + 1) * P, :]).then_inc(x_again, 16)
            for i in range(2):
                pool.dma_start(rows1[:, 1 + i, :], rows[i:i + 1].broadcast_to([P, D])).then_inc(row_in, 16)
            pool.wait_ge(blk_mm, O0)
            nc.gpsimd.memset(keys[:], 0.0).then_inc(const_r, 1)
            def gain_bias(dst, src, rows_of, t):
                ch.link(nc.gpsimd.tensor_tensor(src[:, t, :], src[:, t, :], rows_of[:, 1, :], ALU.mult))
                return nc.gpsimd.tensor_tensor(dst[:, t, :], src[:, t, :], rows_of[:, 2, :], ALU.add)

            pool.wait_ge(row_in, 32)
            for i, t in enumerate((3, 2)):
                pool.wait_ge(xa_r, 3 + i)
                gain_bias(xres, outg, rows1, t).then_inc(x1_p, 1)
            pool.wait_ge(x1_p, 2)
            pool.wait_ge(x1_r, 2)
            pool.dma_start(x1_dram.rearrange("t p d -> p t d"), xres[:]).then_inc(x1_out, 16)

            def by_expert(t):
                for h in range(PH):
                    pool.wait_ge(eq_r, 8 * t + (h + 1))
                    nc.gpsimd.tensor_tensor(eq[:, h % 2], eq[:, h % 2],
                                            ecand[:, h, :].unsqueeze(1).broadcast_to([P, TOPK, NCAND]),
                                            ALU.mult).then_inc(eqm_r, 1)

            def by_gate(t):
                for b in range(NBT):
                    pool.wait_ge(one_r, NBT * t + (b + 1))
                    row = one[b % OH][:, 1]
                    nc.gpsimd.tensor_tensor(row, row,
                                            selT[:, 2, b * TOK:(b + 1) * TOK].unsqueeze(2).broadcast_to([P, TOK, NK]),
                                            ALU.mult).then_inc(onem_r, 1)

            by_expert(0)
            with pool.Fori(0, TT - 1) as it:
                by_expert(it + 1)
                by_gate(it)
            by_gate(TT - 1)
            for i in range(2):
                pool.wait_ge(stage_out[i], 16 * (NTB // 2 + 1))

            def load_g(pr, slot):
                need(pool, w_mul, 2 * pr - 2)
                src = gates_dram[:, :, bass.ds(2 * pr, 2), :].rearrange("b p i t -> p b i t")
                pool.dma_start(gring[:, slot], src).then_inc(g_in[slot], 16)

            for pr in range(PRE // 2):
                load_g(pr, pr % 2)
                pool.wait_ge(gel_out, 16 * (pr // 2 + 2))
                pool.dma_start(gback[:, pr % 4], gel_dram[pr // 2, :, 2 * (pr % 2):2 * (pr % 2) + 2, :]
                               ).then_inc(back_in[pr % 4], 16)
            with pool.Fori(PRE // 4, CH // 4) as it:
                load_g(2 * it, 0)
                load_g(2 * it + 1, 1)
            pool.wait_ge(fin_in, 32)
            for t in range(3):
                pool.wait_ge(xa_r, 6 + t + 1)
                nc.gpsimd.tensor_tensor(xfin[:, t, :], acc[:, t, :], rows2[:, 2, :], ALU.add).then_inc(y_p, 1)

        @block.scalar
        def _(act):
            ch = Chain(act, ach)

            def hi(n):
                s = AT_STREAM[("w", n)]
                act.wait_ge(raw_in[s % RAW], 16 * (s // RAW + 1))
                need(act, blk_mm, n - SPL + 1 if n > SPL else 0)
                nc.scalar.activation(w_parts(n)[0][:, :], raw[:, s % RAW, :], ACT.Copy).then_inc(blk_hi, 1)

            def root(done, ts=slice(0, TT)):
                act.wait_ge(var_r, done)
                nc.scalar.activation(sq[:, 1, ts], sq[:, 0, ts], ACT.Sqrt).then_inc(dev_r, 1)

            def modulated(sh, sc, first, biased):
                for kd in range(KD):
                    act.wait_ge(mod_r, biased + (kd if first == 0 else 0) + 1)
                    act.wait_ge(xT_mm, first + kd + 1)
                    nc.scalar.activation(uraw[:, kd, :], bank[kd][:, :], ACT.Identity,
                                         scale=modc[:, sc + kd:sc + kd + 1],
                                         bias=modc[:, sh + kd:sh + kd + 1]).then_inc(u_raw, 1)
                    act.wait_ge(u_raw, first + kd + 1)
                    nc.scalar.activation(act_hi[:, kd, :], uraw[:, kd, :], ACT.Copy).then_inc(a_hi, 1)

            def scaled(dst, src, t):
                return nc.scalar.activation(dst[:, t, :], src[:, t, :], ACT.Identity, scale=sq[:, 2, t:t + 1],
                                            bias=sq[:, 3, t:t + 1])

            act.wait_ge(c_in, 16)
            nc.scalar.activation(cs[:], cs[:], ACT.Silu).then_inc(cs_r, 1)
            hi(0)
            root(1)
            act.wait_ge(scale_r, 1)
            for t in (2, 3):
                scaled(xn, xres, t).then_inc(xa_r, 1)
            hi(1)
            hi(2)
            modulated(0, 8, 0, 0)
            hi(3)
            for n in range(G0):
                if n > 1:
                    hi(n + 2)
                if n < F0:
                    act.wait_ge(blk_mm, n + 1)
                    dst = qa if n < K0 else ka
                    for r in range(2):
                        ins = nc.scalar.activation(dst[0:DH, 2 * (n % 4) + r, :],
                                                   bank[z_bank[n]][r * DH:(r + 1) * DH, :], ACT.Copy,
                                                   scale=DH ** -0.5 if n < K0 else 1.0)
                    ins.then_inc(z_act, 1)
                elif n == V0 + 1:
                    act.wait_ge(f_log, 1)
                    ch.link(nc.scalar.activation(frow[:, 3, :], frow[:, 2, :], ACT.Abs))
                    ch.link(nc.scalar.activation(frow[:, 3, :], frow[:, 3, :], ACT.Exp, scale=-1.0))
                    nc.scalar.activation(frow[:, 3, :], frow[:, 3, :], ACT.Ln, bias=1.0).then_inc(f_exp, 1)
                elif n == C0 - 1:
                    act.wait_ge(v_mm1, 1)
                    for t in range(2):
                        nc.scalar.activation(vals[:, t, :], bank[4 + t][:, :], ACT.Copy).then_inc(v_act, 1)
                elif n >= C0 and (n - C0) % 2 == 1:
                    i = (n - C0) // 2
                    act.wait_ge(blk_mm, n + 1)
                    need(act, hc_r, i - 1)
                    nc.scalar.activation(sg[:, i % 2, :], bank[z_bank[n]][:, :], ACT.Sigmoid).then_inc(z_act, 1)

            def exp_tile(h, q):
                act.wait_ge(nmax, 4 * h + q + 1)
                w = P * (q + 1)
                nc.scalar.activation(prob[:, tri(q):tri(q) + w], bank[4 + q % 2][:, 0:w], ACT.Exp,
                                     bias=att_s[:, 1, q:q + 1], accum_out=att_s[:, 2, q:q + 1]).then_inc(p_exp, 1)

            def probs_T(h, q):
                act.wait_ge(pT_mm, 4 * h + q + 1)
                nc.scalar.activation(probT[:, 0:q + 1, q * P:(q + 1) * P],
                                     bank[6 + q % 2][:, 0:P * (q + 1)].rearrange("p (k c) -> p k c", c=P),
                                     ACT.Copy).then_inc(pT_sb, 1)

            def head_out(h):
                act.wait_ge(o_mm, h + 1)
                nc.scalar.activation(attT[(h % 2) * DH:(h % 2 + 1) * DH, h // 2, :], bank[3][0:DH, :],
                                     ACT.Copy).then_inc(o_sb, 1)

            def gate_tile(n):
                act.wait_ge(blk_mm, n + 1)
                m = (n - G0) % KD
                nc.scalar.activation((ga if n < G0 + KD else gb)[:, m, :], bank[z_bank[n]][:, :],
                                     ACT.Sigmoid).then_inc(z_act, 1)

            def att_part(i):
                act.wait_ge(o_sb, 2 * i + 2)
                nc.scalar.activation(att_hi[:, i, :], attT[:, i, :], ACT.Copy).then_inc(part_hi, 1)

            for h in range(HEADS):
                n = G0 + 2 * h
                exp_tile(h, 0)
                exp_tile(h, 1)
                if h:
                    head_out(h - 1)
                if h > 4:
                    att_part(h - 5)
                hi(n + 2)
                exp_tile(h, 2)
                exp_tile(h, 3)
                probs_T(h, 0)
                probs_T(h, 1)
                hi(n + 3)
                probs_T(h, 2)
                probs_T(h, 3)
                gate_tile(n)
                gate_tile(n + 1)
            head_out(HEADS - 1)
            att_part(AT - 1)
            hi(Y0 + 2)
            for i in range(CT):
                act.wait_ge(conv_c, i + 1)
                nc.scalar.activation(hc[:, i, 0:T], conv[:, i, :], ACT.Square).then_inc(conv_q, 1)
            hi(Y0 + 3)
            act.wait_ge(conv_v, 1)
            ch.link(nc.scalar.activation(rbc[:, 1, :], rbc[:, 0, :], ACT.Ln))
            nc.scalar.activation(rbc[:, 2, :], rbc[:, 1, :], ACT.Exp, scale=-0.5).then_inc(conv_s, 1)
            hi(Y0 + 4)
            for i in range(CT):
                act.wait_ge(conv_y, i + 1)
                nc.scalar.activation(conv[:, i, :], conv[:, i, :], ACT.Silu, bias=convv[:, 2, i:i + 1],
                                     scale=convv[:, 1, i:i + 1]).then_inc(conv_a, 1)
                act.wait_ge(conv_a, i + 1)
                nc.scalar.activation(cvn_hi[:, i, :], conv[:, i, :], ACT.Copy).then_inc(part_hi, 1)
            hi(Y0 + 5)
            for j in range(4):
                hi(Y0 + 6 + j)
                for m in (2 * j, 2 * j + 1):
                    act.wait_ge(m_raw, m + 1)
                    nc.scalar.activation(act_hi[:, m, :], ga[:, m, :], ACT.Copy).then_inc(a_hi, 1)
            for n in range(O0, W0):
                hi(n + 2)

            root(2)
            act.wait_ge(scale_r, 2)
            for t in (3, 2):
                scaled(outg, xres, t).then_inc(xa_r, 1)
            for half in range(2):
                root(3 + half, slice(2 * half, 2 * half + 2))
                act.wait_ge(scale_r, 3 + half)
                scaled(xn, xres, 2 * half + 1).then_inc(xa_r, 1)
            modulated(24, 32, KD, KD)
            act.wait_ge(x1_out, 16)
            for n in range(W0, NBLK):
                if n + 2 < NBLK:
                    hi(n + 2)
                act.wait_ge(blk_mm, n + 1)
                nc.scalar.activation(qT[:, n - W0, :], bank[(n - W0) % 2][:, :], ACT.Copy).then_inc(z_act, 1)

            def part_u(c, slot):
                act.wait_ge(u_in[slot % RAW], 16 * (c // RAW + 1) if isinstance(c, int) else 4 * c + 16 - 4 * (slot % RAW))
                need(act, u_mm, c - 1)
                nc.scalar.activation(whi[:, slot % 2, :], raw[:, slot % RAW, :], ACT.Copy).then_inc(u_hi, 1)

            def gelu(c, slot, buf=gel):
                act.wait_ge(u_mm, c + 1)
                if buf is gel:
                    act.wait_ge(w_mul, c - LEAD + 1)
                nc.scalar.activation(buf[:, slot, :], bank[slot % 2][:, :], ACT.Gelu_apprx_tanh).then_inc(gel_r, 1)

            def ahead(c, p, last=False):
                if not isinstance(c, int) or c:
                    if (p - 1) % 4 == 0:
                        act.wait_ge(gel_out, 4 * (c - 1) if not isinstance(c, int) else max(16, 4 * (c - 1)))
                    gelu(c - 1, (p - 1) % PS, gelz)
                if not last:
                    part_u(c + 1, (p + 1) % PS)

            def gates(t, b):
                s, t0 = b // (TB // TOK), b % (TB // TOK) * TOK
                if t0 == 0:
                    act.wait_ge(stage_out[s], 16 * t + 16)
                act.wait_ge(gt_mm, NBT * t + (b + 1 + OH))
                nc.scalar.activation(stage[:, s, :, t0:t0 + TOK].rearrange("p i t -> p t i"),
                                     bank[2 + b % 2][:, :].rearrange("p (t i) -> p t i", t=TOK),
                                     ACT.Copy).then_inc(gt_sb, 1)
                if t0 == TB - TOK:
                    act.wait_ge(gt_sb, NBT * t + (b + 1 + 2))
                    dst = gates_dram[2 * t + s] if isinstance(t, int) else \
                        gates_dram[bass.ds(2 * t + s, 1)].rearrange("o p i t -> (o p) i t")
                    act.dma_start(dst, stage[:, s]).then_inc(stage_out[s], 16)

            def selecting(t, c0, p0):
                for j in range(PRE_T):
                    ahead(c0 + j, p0 + j)
                    if j == 8:
                        act.wait_ge(gate_sub, t + 1)
                        nc.scalar.activation(sel[:, 1, :, :], cv[:], ACT.Exp).then_inc(gate_exp, 1)

            def laying(t, c0, p0):
                for b in range(NBT):
                    if b % 8 == 1:
                        ahead(c0 + b // 8, p0 + b // 8)
                    gates(t, b)

            act.sem_inc(gt_sb, 2)
            for i in range(2):
                act.sem_inc(stage_out[i], 16)
            part_u(0, 0)
            selecting(0, 0, 0)
            with act.Fori(0, TT - 1) as it:
                selecting(it + 1, PER * it + PRE_T, PRE_T)
                laying(it, PER * it + 2 * PRE_T, 2 * PRE_T)
            laying(TT - 1, PRE - FILL - PRE_G, PRE - FILL - PRE_G)

            def part_w(c, k):
                act.wait_ge(w_mul, c + 1)
                nc.scalar.activation(eh[:, k, :], wf[:, k % 2, :], ACT.Copy).then_inc(w_hi, 1)

            def part_v(g, n, last=False):
                act.wait_ge(v_in[n % VR], 16 * (4 * g + n // VR + 1))
                before = v_before(n, last)
                if before is not None:
                    need(act, v_mm, 16 * g + before + 1)
                hi_slot, _ = v_slot(n, last)
                nc.scalar.activation(hi_slot, vraw[:, n % VR, :], ACT.Copy).then_inc(v_hi, 1)

            for j in range(FILL):
                ahead(PRE - FILL + j, PRE - FILL + j, j == FILL - 1)
                if j >= 4:
                    if j == 4:
                        for i in range(2):
                            act.wait_ge(stage_out[i], 16 * (NTB // 2 + 1))
                    part_w(j - 4, j - 4)
                if j >= 5:
                    part_v(0, j - 5)
            gelu(PRE - 1, (PRE - 1) % PS, gelz)

            def group(g, par, with_u, next_u, last=False):
                for k in range(GR):
                    cu = GR * g + LEAD + k
                    if with_u and k + 1 < GR:
                        part_u(cu + 1, k + 1)
                    if k == 0:
                        part_w(GR * g + GR - 1, GR - 1)
                    part_v(g, k + 3, last)
                    if with_u and k:
                        gelu(cu - 1, par * GR + k - 1)
                if with_u:
                    gelu(GR * g + LEAD + GR - 1, par * GR + GR - 1)
                for k in range(GR):
                    if k + 11 < 16:
                        part_v(g, k + 11, last)
                    elif not last:
                        part_v(g + 1, k - 5)
                    if k == GR - 2 and next_u:
                        part_u(GR * g + GR + LEAD, 0)
                    if k and not last:
                        part_w(GR * g + GR + k - 1, k - 1)

            for k in range(4, GR - 1):
                part_w(k, k)
            for g in range(FIRST):
                group(g, g % 2, u_beside(g), u_beside(g + 1))
            with act.Fori(0, LOOP) as it:
                group(2 * it + FIRST, 1, True, True)
                group(2 * it + (FIRST + 1), 0, True, True)
            group(NG - 3, 1, True, False)
            group(NG - 2, 0, False, False)
            group(NG - 1, 1, False, False, True)
            for t in range(TT):
                root(5 + t, slice(t, t + 1))
                if t < 3:
                    act.wait_ge(scale_r, 5 + t)
                    nc.scalar.activation(acc[:, t, :], acc[:, t, :], ACT.Copy,
                                         scale=sq[:, 2, t:t + 1]).then_inc(xa_r, 1)

        @block.vector
        def _(dve):
            ch = Chain(dve, dch)
            link = ch.link
            done = [0]

            def until(n):
                while done[0] <= AT_STREAM[("w", n)]:
                    entry()

            def entry():
                s = done[0]
                kind, n = STREAM[s]
                dve.wait_ge(raw_in[s % RAW], 16 * (s // RAW + 1))
                if kind == "mod":
                    nc.vector.scalar_tensor_tensor(out=raw[:, s % RAW, :], in0=raw[:, s % RAW, :], scalar=1.0,
                                                   in1=cs[:], op0=ALU.mult, op1=ALU.mult,
                                                   accum_out=modc[:, n:n + 1]).then_inc(raw_free, 1)
                else:
                    dve.wait_ge(blk_hi, n + 1)
                    high, low = w_parts(n)
                    nc.vector.tensor_tensor(low[:, :], raw[:, s % RAW, :], high[:, :].bitcast(F32),
                                            ALU.subtract).then_inc(raw_free, 1)
                done[0] += 1

            def bn(src, t, i):
                return nc.vector.bn_stats(stats[:, t, i, :], src[:, t, i * HALF:(i + 1) * HALF])

            def scales(last, roots, between=lambda: None, shift=True, ts=slice(0, TT), meanwhile=None):
                link(last)
                between()
                for t in range(ts.start, ts.stop):
                    last = nc.vector.bn_aggr(mv[:, t, :], stats[:, t, :, :].rearrange("p a b -> p (a b)"))
                link(last)
                nc.vector.tensor_scalar(sq[:, 0, ts], mv[:, ts, 1], EPS, None, ALU.add).then_inc(var_r, 1)
                if meanwhile is not None:
                    link(meanwhile())
                between()
                dve.wait_ge(dev_r, roots)
                link(nc.vector.reciprocal(sq[:, 2, ts], sq[:, 1, ts]))
                link(nc.vector.tensor_tensor(sq[:, 3, ts], sq[:, 2, ts], sq[:, 2, ts], ALU.mult))
                link(nc.vector.tensor_tensor(sq[:, 3, ts], sq[:, 3, ts], sq[:, 0, ts], ALU.mult))
                link(nc.vector.tensor_scalar(sq[:, 3, ts], sq[:, 3, ts], -0.5, 1.5, ALU.mult, ALU.add))
                link(nc.vector.tensor_tensor(sq[:, 2, ts], sq[:, 2, ts], sq[:, 3, ts], ALU.mult))
                if shift:
                    nc.vector.scalar_tensor_tensor(out=sq[:, 3, ts], in0=mv[:, ts, 0], scalar=-1.0, in1=sq[:, 2, ts],
                                                   op0=ALU.mult, op1=ALU.mult).then_inc(scale_r, 1)

            def scaled(dst, src, t):
                return nc.vector.tensor_scalar(dst[:, t, :], src[:, t, :], mv[:, t, 0:1], sq[:, 2, t:t + 1],
                                               ALU.subtract, ALU.mult)

            def centred(dst, src, rows_of, t):
                return nc.vector.scalar_tensor_tensor(out=dst[:, t, :], in0=src[:, t, :], scalar=mv[:, t, 0:1],
                                                      in1=rows_of[:, 1, :], op0=ALU.subtract, op1=ALU.mult)

            def finished(dst, src, rows_of, t, cut=slice(0, D)):
                return nc.vector.scalar_tensor_tensor(out=dst[:, t, cut], in0=src[:, t, cut],
                                                      scalar=sq[:, 2, t:t + 1], in1=rows_of[:, 2, cut],
                                                      op0=ALU.mult, op1=ALU.add)

            def low_part(kd, before):
                dve.wait_ge(a_hi, before + kd + 1)
                nc.vector.tensor_tensor(act_lo[:, kd, :], uraw[:, kd, :], act_hi[:, kd, :].bitcast(F32),
                                        ALU.subtract).then_inc(a_lo, 1)

            def bias(m, n, one):
                link(nc.vector.tensor_tensor(modc[:, m:m + n], modc[:, m:m + n], bmod[:, m:m + n], ALU.add))
                if one:
                    link(nc.vector.tensor_scalar(modc[:, m:m + n], modc[:, m:m + n], 1.0, None, ALU.add))

            dve.wait_ge(cs_r, 1)
            for t in range(TT):
                entry()
                dve.wait_ge(x_in[t], 16)
                bn(xres, t, 0)
                last = bn(xres, t, 1)
            scales(last, 1, entry)
            scaled(xn, xres, 0)
            scaled(xn, xres, 1).then_inc(xn_r, 1)
            dve.wait_ge(small_in, 64)
            link(nc.vector.tensor_scalar(bmod[:, 8:16], bmod[:, 8:16], 1.0, None, ALU.add))
            until(2)
            for kd in range(KD + 1):
                if kd < KD:
                    while done[0] <= AT_STREAM[("mod", 8 + kd)]:
                        entry()
                    dve.wait_ge(raw_free, done[0])
                    both = modc[:, kd:kd + 9:8]
                    nc.vector.tensor_tensor(both, both, bmod[:, kd:kd + 9:8], ALU.add).then_inc(mod_r, 1)
                if kd:
                    low_part(kd - 1, 0)
            until(3)
            for n in range(G0):
                if n > 1:
                    until(n + 2)
                if n == F0:
                    dve.wait_ge(blk_mm, n + 1)
                    nc.vector.tensor_scalar(frow[:, 2, :], bank[z_bank[n]][0:HEADS, :], bf[:, 0:1], None,
                                            ALU.add).then_inc(f_log, 1)
                    dve.wait_ge(f_log, 1)
                    nc.vector.memset(frow[:, 1, :], 1.0).then_inc(z_dve, 1)
                elif n == V0 + 2:
                    dve.wait_ge(f_exp, 1)
                    link(nc.vector.tensor_scalar(frow[:, 2, :], frow[:, 2, :], 0.0, None, ALU.min))
                    link(nc.vector.tensor_tensor(frow[:, 2, :], frow[:, 2, :], frow[:, 3, :], ALU.subtract))
                    link(nc.vector.tensor_tensor_scan(frow[:, 0, :], frow[:, 1, :], frow[:, 2, :], 0.0,
                                                      ALU.mult, ALU.add))
                    nc.vector.tensor_scalar(frow[:, 1, :], frow[:, 0, :], -1.0, None, ALU.mult).then_inc(f_ready, 1)
                elif n == C0 - 1:
                    dve.wait_ge(v_mm1, 1)
                    for t in range(2, 4):
                        nc.vector.tensor_copy(vals[:, t, :], bank[4 + t][:, :]).then_inc(v_dve, 1)
                elif n >= C0 and (n - C0) % 2 == 1:
                    i = (n - C0) // 2
                    dve.wait_ge(const_r, 1)
                    dve.wait_ge(z_act, by_act.index(n) + 1)
                    nc.vector.tensor_tensor(hc[:, i, TAPS - 1:], bank[z_bank[n - 1]][:, :], sg[:, i % 2, :],
                                            ALU.mult).then_inc(hc_r, 1)
                    dve.wait_ge(hc_r, i + 1)
                    nc.vector.nop().then_inc(z_dve, 1)

            def score_max(h, q):
                dve.wait_ge(s_mm, 4 * h + q + 1)
                w = P * (q + 1)
                link(nc.vector.tensor_tensor_reduce(out=bank[4 + q % 2][:, 0:w], in0=bank[4 + q % 2][:, 0:w],
                                                    in1=mask[:, T - w:T], scale=1.0, scalar=NEG,
                                                    op0=ALU.add, op1=ALU.max, accum_out=att_s[:, 0, q:q + 1]))
                nc.vector.tensor_scalar(att_s[:, 1, q:q + 1], att_s[:, 0, q:q + 1], -1.0, None,
                                        ALU.mult).then_inc(nmax, 1)

            def prob_norm(h, q):
                dve.wait_ge(p_exp, 4 * h + q + 1)
                w = P * (q + 1)
                link(nc.vector.reciprocal(att_s[:, 3, q:q + 1], att_s[:, 2, q:q + 1]))
                nc.vector.tensor_scalar(prob[:, tri(q):tri(q) + w], prob[:, tri(q):tri(q) + w], att_s[:, 3, q:q + 1],
                                        None, ALU.mult).then_inc(p_norm, 1)

            DC = CT - 1
            taps = [(k, i) for k in range(TAPS) for i in range(DC)]

            def tap(j):
                k, i = taps[j]
                if k == 0:
                    nc.vector.tensor_scalar(conv[:, i, :], hc[:, i, 0:T], convw[:, i, 0:1], convv[:, 0, i:i + 1],
                                            ALU.mult, ALU.add).then_inc(conv_d, 1)
                else:
                    dve.wait_ge(conv_d, j - DC + 1)
                    nc.vector.scalar_tensor_tensor(out=conv[:, i, :], in0=hc[:, i, k:k + T],
                                                   scalar=convw[:, i, k:k + 1], in1=conv[:, i, :],
                                                   op0=ALU.mult, op1=ALU.add).then_inc(conv_d, 1)

            def att_part(i):
                dve.wait_ge(part_hi, i + 1)
                nc.vector.tensor_tensor(att_lo[:, i, :], attT[:, i, :], att_hi[:, i, :].bitcast(F32),
                                        ALU.subtract).then_inc(part_lo, 1)

            dve.wait_ge(mask_r, 1)
            dve.wait_ge(hc_r, CT)
            share = (len(taps) + 2 * HEADS - 1) // (2 * HEADS)
            for h in range(HEADS):
                n = G0 + 2 * h
                score_max(h, 0)
                score_max(h, 1)
                prob_norm(h, 0)
                prob_norm(h, 1)
                until(n + 2)
                score_max(h, 2)
                score_max(h, 3)
                for j in range(2 * h * share, min((2 * h + 1) * share, len(taps))):
                    tap(j)
                prob_norm(h, 2)
                prob_norm(h, 3)
                until(n + 3)
                for j in range((2 * h + 1) * share, min((2 * h + 2) * share, len(taps))):
                    tap(j)
                if h > 4:
                    att_part(h - 5)
            def diagonals(dst, m0):
                for m in range(KD):
                    last = nc.vector.tensor_scalar(dst[:, m, :], ident[:], modc[:, m0 + m:m0 + m + 1], None, ALU.mult)
                last.then_inc(g_dg, 1)

            att_part(AT - 1)
            until(Y0 + 2)

            def merge(j, g, n):
                dve.wait_ge(blk_mm, n + 1)
                for r in range(2):
                    last = nc.vector.tensor_tensor(g[:, 2 * j + r, :], g[:, 2 * j + r, :], bank[Y_BANK[j] + r][:, :],
                                                   ALU.mult)
                last.then_inc(y_free, 1)

            dve.wait_ge(conv_p, 1)
            dve.wait_ge(conv_d, len(taps))
            dve.wait_ge(conv_mm, 1)
            for i in range(CT):
                nc.vector.tensor_tensor(conv[:, i, :], conv[:, i, :], bank[4][:, :], ALU.subtract).then_inc(conv_c, 1)
            merge(0, ga, Y0)
            until(Y0 + 3)
            dve.wait_ge(conv_mm, 2)
            nc.vector.tensor_scalar(rbc[:, 0, :], bank[5][:, :], EPS, None, ALU.add).then_inc(conv_v, 1)
            merge(1, ga, Y0 + 1)
            dve.wait_ge(conv_s, 1)
            link(nc.vector.tensor_tensor(rbc[:, 3, :], rbc[:, 2, :], rbc[:, 2, :], ALU.mult))
            link(nc.vector.tensor_tensor(rbc[:, 3, :], rbc[:, 3, :], rbc[:, 0, :], ALU.mult))
            link(nc.vector.tensor_scalar(rbc[:, 3, :], rbc[:, 3, :], -0.5, 1.5, ALU.mult, ALU.add))
            link(nc.vector.tensor_tensor(rbc[:, 2, :], rbc[:, 2, :], rbc[:, 3, :], ALU.mult))
            for i in range(CT):
                nc.vector.tensor_tensor(conv[:, i, :], conv[:, i, :], rbc[:, 2, :], ALU.mult).then_inc(conv_y, 1)
            until(Y0 + 4)
            for i in range(CT):
                dve.wait_ge(part_hi, AT + i + 1)
                nc.vector.tensor_tensor(cvn_lo[:, i, :], conv[:, i, :], cvn_hi[:, i, :].bitcast(F32),
                                        ALU.subtract).then_inc(part_lo, 1)
            merge(2, ga, Y0 + 2)
            until(Y0 + 5)
            merge(3, ga, Y0 + 3)
            bias(16, 8, False)
            diagonals(dg1, 16)
            for j in range(4):
                until(Y0 + 6 + j)
                merge(j, gb, Y0 + 4 + j)
                dve.wait_ge(y_free, 4 + j + 1)
                for r in range(2):
                    nc.vector.tensor_tensor(ga[:, 2 * j + r, :], ga[:, 2 * j + r, :], gb[:, 2 * j + r, :],
                                            ALU.add).then_inc(m_raw, 1)
                for r in range(2):
                    m = 2 * j + r
                    dve.wait_ge(a_hi, KD + m + 1)
                    nc.vector.tensor_tensor(act_lo[:, m, :], ga[:, m, :], act_hi[:, m, :].bitcast(F32),
                                            ALU.subtract).then_inc(a_lo, 1)

            def gate_row(dst, banks, n):
                dve.wait_ge(g_mm, n)
                for half in range(2):
                    last = nc.vector.tensor_scalar(dst[:, half * HALF:(half + 1) * HALF], bank[banks + half][:, :],
                                                   float(CC), 1.0, ALU.mult, ALU.add)
                last.then_inc(g_row, 1)

            until(O0 + 2)
            gate_row(rows1[:, 0, :], 6, 1)
            dve.wait_ge(x_again, 16 * TT)
            dve.wait_ge(row_in, 32)
            dve.wait_ge(g_row, 1)

            def gate_bank(t, half):
                cut = slice(half * HALF, (half + 1) * HALF)
                if t < TT - 1:
                    dve.wait_ge(o1_mm, (TT - 1) * half + t + 1)
                else:
                    dve.wait_ge(blk_mm, O0 + 4 * half + 4)
                return nc.vector.tensor_tensor(outg[:, t, cut], bank[4 * half + t][:, :], rows1[:, 0, cut], ALU.mult)

            def plus_x(t, half):
                cut = slice(half * HALF, (half + 1) * HALF)
                return nc.vector.scalar_tensor_tensor(out=xres[:, t, cut], in0=xres[:, t, cut], scalar=ALPHA,
                                                      in1=outg[:, t, cut], op0=ALU.mult, op1=ALU.add)

            def gated(half):
                if half == 0:
                    for t in range(TT):
                        last = gate_bank(t, 0)
                    link(last)
                    until(O0 + 7)
                    for t in range(TT):
                        last = plus_x(t, 0)
                    link(last)
                    for t in range(TT):
                        bn(xres, t, 0)
                else:
                    for t in range(TT):
                        link(gate_bank(t, 1))
                        link(plus_x(t, 1))
                        last = bn(xres, t, 1)
                    return last

            for n in range(O0 + 3, O0 + 7):
                until(n)
            gated(0)
            until(W0)
            bias(24, 8, False)
            bias(32, 8, True)
            bias(40, 8, False)
            nc.vector.nop().then_inc(mod_r, 1)
            scales(gated(1), 2, meanwhile=lambda: centred(outg, xres, rows1, 0))
            finished(xres, outg, rows1, 0).then_inc(x1_r, 1)
            link(centred(outg, xres, rows1, 1))
            finished(xres, outg, rows1, 1).then_inc(x1_r, 1)
            for t in range(2):
                dve.wait_ge(x1_r, t + 1)
                bn(xres, t, 0)
                last = bn(xres, t, 1)
            scales(last, 3, ts=slice(0, 2))
            scaled(xn, xres, 0).then_inc(xn_r, 1)
            for i, t in enumerate((3, 2)):
                dve.wait_ge(x1_p, i + 1)
                bn(xres, t, 0)
                last = bn(xres, t, 1)
            scales(last, 4, ts=slice(2, 4))
            scaled(xn, xres, 2).then_inc(xn_r, 1)
            until(W0 + 1)
            for kd in range(KD):
                low_part(kd, 2 * KD)
            until(NBLK - 1)

            def low_u(c, slot):
                dve.wait_ge(u_hi, c + 1)
                nc.vector.tensor_tensor(wlo[:, slot % 2, :], raw[:, slot % RAW, :],
                                        whi[:, slot % 2, :].bitcast(F32), ALU.subtract).then_inc(u_lo, 1)

            def best(lists, top, idx, spare, between, free=None):
                for o, v in zip(top, lists):
                    last = nc.vector.max(o[:, 0:8], v)
                link(last)
                between()
                for o, v, i in zip(top, lists, idx):
                    nc.vector.max_index(i[:, 0:8], o[:, 0:8], v)
                between()
                for o, v, w in zip(top, lists, spare):
                    last = nc.vector.match_replace(w, o[:, 0:8], v, NEG)
                link(last)
                if free is not None:
                    nc.vector.nop().then_inc(free, 1)
                between()
                for o, w in zip(top, spare):
                    last = nc.vector.max(o[:, 8:16], w)
                link(last)
                for o, w, i in zip(top, spare, idx):
                    last = nc.vector.max_index(i[:, 8:16], o[:, 8:16], w)
                link(last)

            both = [(h, s) for h in range(PH) for s in range(2)]
            heads = range(PH)

            def select(t, c0, p0):
                split = [0]

                def ahead():
                    if split[0] < PRE_T:
                        split[0] += 1
                        low_u(c0 + split[0], (p0 + split[0]) % PS)

                ahead()
                dve.wait_ge(sc_mm, t + 1)
                dve.sem_inc(alone, 1)
                best([bank[4 + h // 2][:, (h % 2) * 256 + s * NK:(h % 2) * 256 + (s + 1) * NK] for h, s in both],
                     [sv[:, h, s, :] for h, s in both], [si[:, h, s, :] for h, s in both],
                     [sc2[:, 2 * h + s, :] for h, s in both], ahead, sc_read)
                ahead()
                link(nc.vector.tensor_copy(sif[:], si[:]))
                link(nc.vector.tensor_scalar(sif[:, :, 0, :], sif[:, :, 0, :], float(NK), None, ALU.mult))
                for src, dst in ((sv, cand), (sif, ecand)):
                    off = 0
                    for a, na, nb in RECTS:
                        shape = [P, PH, na, nb]
                        last = nc.vector.tensor_tensor(
                            dst[:, :, off:off + na * nb].rearrange("p h (a b) -> p h a b", b=nb),
                            src[:, :, 0, a:a + na].unsqueeze(3).broadcast_to(shape),
                            src[:, :, 1, 0:nb].unsqueeze(2).broadcast_to(shape), ALU.add)
                        off += na * nb
                link(last)
                best([cand[:, h, :] for h in heads], [cv[:, h, :] for h in heads],
                     [pos[:, h, :] for h in heads], [cand2[:, h, :] for h in heads],
                     lambda: split[0] < 6 and ahead())
                ahead()
                nc.vector.tensor_copy(posf[:], pos[:])
                link(nc.vector.tensor_copy(gsum[:, 1, :], cv[:, :, 0]))
                nc.vector.tensor_tensor(cv[:], cv[:], gsum[:, 1, :].unsqueeze(2).broadcast_to([P, PH, TOPK]),
                                        ALU.subtract).then_inc(gate_sub, 1)

                def compare(h):
                    shape = [P, TOPK, NCAND]
                    nc.vector.tensor_tensor(eq[:, h % 2], posf[:, h, :].unsqueeze(2).broadcast_to(shape),
                                            iota[:, 0:NCAND].unsqueeze(1).broadcast_to(shape),
                                            ALU.is_equal).then_inc(eq_r, 1)

                compare(0)
                compare(1)
                for h in heads:
                    if h % 2 == 1:
                        ahead()
                    dve.wait_ge(eqm_r, 8 * t + (h + 1))
                    link(nc.vector.tensor_reduce(sel[:, 0, h, :], eq[:, h % 2], AX, ALU.add))
                    if h + 2 < PH:
                        compare(h + 2)
                dve.wait_ge(gate_exp, t + 1)
                link(nc.vector.tensor_reduce(gsum[:, 0, :], sel[:, 1, :, :], AX, ALU.add))
                link(nc.vector.reciprocal(gsum[:, 1, :], gsum[:, 0, :]))
                nc.vector.tensor_tensor(sel[:, 1, :, :], sel[:, 1, :, :],
                                        gsum[:, 1, :].unsqueeze(2).broadcast_to([P, PH, TOPK]),
                                        ALU.mult).then_inc(sel_r, 1)
                while split[0] < PRE_T:
                    ahead()

            def transposed(t):
                dve.wait_ge(selT_mm, t + 1)
                nc.vector.tensor_copy(selT[:, 2, :], bank[2][:, P:2 * P])
                link(nc.vector.tensor_copy(selI[:, 0, :], bank[2][:, 0:P]))
                link(nc.vector.tensor_scalar(selI[:, 1, :], selI[:, 0, :], NK - 1, None, ALU.bitwise_and))
                link(nc.vector.tensor_scalar(selI[:, 0, :], selI[:, 0, :], NK.bit_length() - 1, None,
                                             ALU.logical_shift_right))
                link(nc.vector.tensor_copy(selT[:, 0:2, :], selI[:]))
                nc.vector.nop().then_inc(selT_sb, 1)

            def one_hots(t, c0, p0):
                for b in range(NBT):
                    if b % 8 == 6:
                        low_u(c0 + (b // 8 + 1), (p0 + b // 8 + 1) % PS)
                    dve.wait_ge(gt_mm, NBT * t + (b + 1))
                    row = one[b % OH]
                    shape = [P, TOK, NK]
                    for r in range(2):
                        ins = nc.vector.tensor_tensor(
                            row[:, r], iota[:].unsqueeze(1).broadcast_to(shape),
                            selT[:, 1 - r, b * TOK:(b + 1) * TOK].unsqueeze(2).broadcast_to(shape), ALU.is_equal)
                    ins.then_inc(one_r, 1)

            low_u(0, 0)
            n0 = ch.n
            select(0, 0, 0)
            transposed(0)
            per = ch.n - n0
            with dve.Fori(0, TT - 1) as it:
                ch.turn = it * per
                select(it + 1, PER * it + PRE_T, PRE_T)
                one_hots(it, PER * it + 2 * PRE_T, 2 * PRE_T)
                dve.wait_ge(onem_r, NBT * it + NBT)
                transposed(it + 1)
            ch.turn = 0
            ch.n = n0 + TT * per
            one_hots(TT - 1, PRE - FILL - PRE_G, PRE - FILL - PRE_G)

            def weigh(g, k, slot):
                c = GR * g + k
                if isinstance(c, int) and c < PRE:
                    dve.wait_ge(back_in[c // 2 % 4], 16 * (c // 8 + 1))
                    src = gback[:, c // 2 % 4, c % 2, :]
                else:
                    dve.wait_ge(gel_r, c + 1)
                    src = gel[:, slot, :]
                s = (k // 2) % 2
                dve.wait_ge(g_in[s], 16 * (2 * g + k // 4 + 1))
                need(dve, v_mm, 16 * g + k - 7)
                need(dve, w_lo, c - 1)
                nc.vector.tensor_tensor(wf[:, k % 2, :].rearrange("p (b t) -> p b t", t=TB),
                                        src.rearrange("p (b t) -> p b t", t=TB),
                                        gring[:, s, :, k % 2, :], ALU.mult).then_inc(w_mul, 1)

            def low_w(g, k):
                dve.wait_ge(w_hi, GR * g + k + 1)
                nc.vector.tensor_tensor(el[:, k, :], wf[:, k % 2, :], eh[:, k, :].bitcast(F32),
                                        ALU.subtract).then_inc(w_lo, 1)

            def low_v(g, n, last=False):
                dve.wait_ge(v_hi, 16 * g + n + 1)
                hi_slot, lo_slot = v_slot(n, last)
                nc.vector.tensor_tensor(lo_slot, vraw[:, n % VR, :], hi_slot.bitcast(F32),
                                        ALU.subtract).then_inc(v_lo, 1)

            def wait_sum(g, half, t):
                if t < TT - 1 or (isinstance(g, int) and g == NG - 1 and half == 1):
                    dve.wait_ge(pv_mm, 6 * g + 3 * half + t + 1)
                else:
                    dve.wait_ge(v_mm, 16 * g + GR * half + GR)

            def add(g, half, first):
                for t in range(TT):
                    wait_sum(g, half, t)
                    need(dve, pv_add, 8 * g + 4 * half + t - 7)
                    dst = acc[:, t, half * HALF:(half + 1) * HALF]
                    if first:
                        nc.vector.tensor_copy(dst, bank[2 + t][:, :]).then_inc(pv_add, 1)
                    else:
                        nc.vector.tensor_tensor(dst, dst, bank[2 + t][:, :], ALU.add).then_inc(pv_add, 1)

            def residual(t, half):
                cut = slice(half * HALF, (half + 1) * HALF)
                dve.wait_ge(pv_add, 8 * (NG - 1))
                link(nc.vector.tensor_tensor(acc[:, t, cut], acc[:, t, cut], rows2[:, 0, cut], ALU.mult))
                return nc.vector.scalar_tensor_tensor(out=xfin[:, t, cut], in0=xfin[:, t, cut], scalar=ALPHA,
                                                      in1=acc[:, t, cut], op0=ALU.mult, op1=ALU.add)

            def last_gated(t, half):
                cut = slice(half * HALF, (half + 1) * HALF)
                wait_sum(NG - 1, half, t)
                nc.vector.tensor_tensor(acc[:, t, cut], bank[2 + t][:, :], rows2[:, 0, cut],
                                        ALU.mult).then_inc(pv_add, 1)

            def last_sum(t, half):
                cut = slice(half * HALF, (half + 1) * HALF)
                dve.wait_ge(pv_add, 8 * (NG - 1) + 4 * half + t + 1)
                link(nc.vector.tensor_tensor(xfin[:, t, cut], xfin[:, t, cut], acc[:, t, cut], ALU.add))
                return bn(xfin, t, half)

            def group(g, par, with_u, next_u, first=False, last=False):
                for k in range(GR):
                    if with_u and k + 1 < GR:
                        low_u(GR * g + LEAD + k + 1, k + 1)
                    if k == 0:
                        if first is not True:
                            add(g - 1, 1, first == "second")
                            low_w(g, GR - 2)
                        weigh(g, GR - 1, par * GR + GR - 1)
                        low_w(g, GR - 1)
                    if last and k == 0:
                        dve.wait_ge(w_mul, CH)
                        diagonals(dg2, 40)
                    if last and k == 2:
                        gate_row(rows2[:, 0, :], 0, 2)
                        dve.wait_ge(x1_in, 16)
                        dve.wait_ge(g_row, 2)
                    if last and k > 2:
                        if k < 7:
                            link(residual(k - 3, 0))
                        if k in (3, 7):
                            link(residual(k // 4, 1))
                    low_v(g, k + 3, last)
                if last:
                    for t in range(TT):
                        last_gated(t, 0)
                else:
                    add(g, 0, first is True)
                for k in range(GR):
                    if k + 11 < 16:
                        low_v(g, k + 11, last)
                    elif not last:
                        low_v(g + 1, k - 5)
                    if k == GR - 2 and next_u:
                        low_u(GR * g + GR + LEAD, 0)
                    if k and not last:
                        weigh(g + 1, k - 1, (1 - par) * GR + k - 1)
                        if k < GR - 1:
                            low_w(g + 1, k - 1)
                if last:
                    for t in range(TT):
                        last_sum(t, 0)
                        if t > 1:
                            link(residual(t, 1))

            for j in range(FILL):
                if j < FILL - 1:
                    low_u(PRE - FILL + j + 1, (PRE - FILL + j + 1) % PS)
                if j == 4:
                    for i in range(2):
                        dve.wait_ge(stage_out[i], 16 * (NTB // 2 + 1))
                if j >= 4:
                    weigh(0, j - 4, j - 4)
                    low_w(0, j - 4)
                if j >= 5:
                    low_v(0, j - 5)
            for k in range(4, GR - 1):
                weigh(0, k, k)
                low_w(0, k)
            for g in range(FIRST):
                group(g, g % 2, u_beside(g), u_beside(g + 1), (True, "second", False)[min(g, 2)])
            with dve.Fori(0, LOOP) as it:
                group(2 * it + FIRST, 1, True, True)
                group(2 * it + (FIRST + 1), 0, True, True)
            group(NG - 3, 1, True, False)
            group(NG - 2, 0, False, False)
            group(NG - 1, 1, False, False, last=True)
            dve.wait_ge(fin_in, 32)
            for t in range(TT):
                last_gated(t, 1)
                scales(last_sum(t, 1), 5 + t, shift=t < 3, ts=slice(t, t + 1),
                       meanwhile=lambda: centred(acc, xfin, rows2, t))
            for half in range(2):
                finished(xfin, acc, rows2, 3, slice(half * HALF, (half + 1) * HALF)).then_inc(y_r, 1)

        @block.tensor
        def _(pe):
            mm = nc.tensor.matmul

            def three(o, wh, wl, mh, ml, start, stop):
                mm(o, wh, mh, start=start, stop=False)
                mm(o, wh, ml, start=False, stop=False)
                return mm(o, wl, mh, start=False, stop=stop)

            def transposes(again):
                for ts in ((0, 1), (2, 3)):
                    for t in ts:
                        if not again:
                            pe.wait_ge(*((xn_r, 1) if t < 2 else (xa_r, t - 1)))
                        elif t % 2 == 0:
                            pe.wait_ge(xn_r, t // 2 + 2)
                        else:
                            pe.wait_ge(xa_r, t // 2 + 5)
                    for kd in range(KD):
                        for t in ts:
                            last = nc.tensor.transpose(bank[kd][:, t * P:(t + 1) * P], xn[:, t, kd * P:(kd + 1) * P],
                                                       ident[:])
                        if ts[-1] == TT - 1:
                            last.then_inc(xT_mm, 1)

            def low_ready(n):
                pe.wait_ge(raw_free, AT_STREAM[("w", n)] + 1)

            def tile(n, o):
                low_ready(n)
                for kd in range(KD):
                    w = slice(kd * P, (kd + 1) * P)
                    last = three(o, whi[:, n % SPL, w], wlo[:, n % SPL, w], act_hi[:, kd, :], act_lo[:, kd, :],
                                 kd == 0, kd == KD - 1)
                last.then_inc(blk_mm, 1)

            def side_by_side(n, count, before, banks_read):
                low_ready(n)
                pe.wait_ge(u_raw, banks_read)
                for kd in range(KD):
                    pe.wait_ge(a_lo, before + kd + 1)
                    for i in range(count):
                        if kd == 0 and i:
                            low_ready(n + i)
                        w = slice(kd * P, (kd + 1) * P)
                        high, low = w_parts(n + i)
                        last = three(bank[i][:, :], high[:, w], low[:, w], act_hi[:, kd, :], act_lo[:, kd, :],
                                     kd == 0, kd == KD - 1)
                        if kd == KD - 1:
                            last.then_inc(blk_mm, 1)

            def rows_block(n, b, o0, blocks=1, tile_done=None):
                for i in range(blocks):
                    low_ready(n + i)
                for t in range(TT):
                    for kk in range(2 * blocks):
                        kd = 2 * b + kk
                        s = (n + kk // 2) % SPL
                        w = slice(kk % 2 * HALF, (kk % 2 + 1) * HALF)
                        c = slice(t * P, (t + 1) * P)
                        last = three(bank[o0 + t][:, :], act_hi[:, kd, c], act_lo[:, kd, c],
                                     whi[:, s, w], wlo[:, s, w], kd == 0, kd == KD - 1)
                    if t < TT - 1 and tile_done is not None:
                        last.then_inc(tile_done, 1)
                last.then_inc(blk_mm, blocks)

            pe.wait_ge(const_r, 1)
            transposes(False)
            side_by_side(0, 3, 0, 3)
            for n in range(3, G0):
                if V0 <= n < C0:
                    rows_block(n, n - V0, 4)
                    if n == C0 - 1:
                        pe.wait_ge(blk_mm, C0)
                        pe.nop().then_inc(v_mm1, 1)
                else:
                    z_wait(pe, n)
                    tile(n, bank[z_bank[n]][:, :])

            def scores(h, q):
                need(pe, p_exp, 4 * h + q - 1)
                w = P * (q + 1)
                mm(bank[4 + q % 2][:, 0:w], qa[:, h, q * P:(q + 1) * P], ka[:, h, 0:w],
                   start=True, stop=True).then_inc(s_mm, 1)

            def prob_T(h, q):
                pe.wait_ge(p_norm, 4 * h + q + 1)
                need(pe, pT_sb, 4 * h + q - 1)
                for k in range(q + 1):
                    last = nc.tensor.transpose(bank[6 + q % 2][:, k * P:(k + 1) * P],
                                               prob[:, tri(q) + k * P:tri(q) + (k + 1) * P], ident[:])
                last.then_inc(pT_mm, 1)

            def attend(h):
                pe.wait_ge(pT_sb, 4 * h + 4)
                need(pe, o_sb, h)
                for k in range(TT):
                    last = mm(bank[3][0:DH, k * P:T], vals[:, k, h * DH:(h + 1) * DH], probT[:, k, k * P:T],
                              start=(k == 0), stop=(k == TT - 1))
                last.then_inc(o_mm, 1)

            pe.wait_ge(aug_in, 16 * 2 * HEADS)
            pe.wait_ge(z_act, 8)
            pe.wait_ge(v_act, 2)
            pe.wait_ge(v_dve, 2)
            for h in range(HEADS):
                n = G0 + 2 * h
                scores(h, 0)
                scores(h, 1)
                if h:
                    attend(h - 1)
                z_wait(pe, n)
                tile(n, bank[z_bank[n]][:, :])
                scores(h, 2)
                scores(h, 3)
                prob_T(h, 0)
                prob_T(h, 1)
                z_wait(pe, n + 1)
                tile(n + 1, bank[z_bank[n + 1]][:, :])
                prob_T(h, 2)
                prob_T(h, 3)
            attend(HEADS - 1)
            def branch_block(n, j, src_hi, src_lo, first):
                low_ready(n)
                for r in range(2):
                    for k in range(AT):
                        pe.wait_ge(part_lo, first + k + 1)
                        w = slice((r * AT + k) * P, (r * AT + k + 1) * P)
                        last = three(bank[Y_BANK[j] + r][:, :], whi[:, n % SPL, w], wlo[:, n % SPL, w],
                                     src_hi[:, k, :], src_lo[:, k, :], k == 0, k == AT - 1)
                last.then_inc(blk_mm, 1)

            pe.wait_ge(z_act, len(by_act))
            branch_block(Y0, 0, att_hi, att_lo, 0)
            pe.wait_ge(conv_p, 1)
            pe.wait_ge(conv_d, (CT - 1) * TAPS)
            for i in range(CT):
                last = mm(bank[4][:, :], consts[:], conv[:, i, :], start=(i == 0), stop=(i == CT - 1))
            last.then_inc(conv_mm, 1)
            pe.wait_ge(o_sb, HEADS)
            branch_block(Y0 + 1, 1, att_hi, att_lo, 0)
            for i in range(CT):
                pe.wait_ge(conv_q, i + 1)
                last = mm(bank[5][:, :], consts[:], hc[:, i, 0:T], start=(i == 0), stop=(i == CT - 1))
            last.then_inc(conv_mm, 1)
            branch_block(Y0 + 2, 2, att_hi, att_lo, 0)
            pe.wait_ge(conv_v, 1)
            branch_block(Y0 + 3, 3, att_hi, att_lo, 0)
            for j in range(4):
                pe.wait_ge(y_free, j + 1)
                branch_block(Y0 + 4 + j, j, cvn_hi, cvn_lo, AT)

            def gate_row(dg, banks, n):
                pe.wait_ge(g_dg, n)
                for half in range(2):
                    last = mm(bank[banks + half][:, :], consts[:],
                              dg[:, 4 * half:4 * half + 4, :].rearrange("p m c -> p (m c)"), start=True, stop=True)
                last.then_inc(g_mm, 1)

            pe.wait_ge(y_free, 6)
            for half in range(2):
                for b in range(4):
                    if half == 0:
                        pe.wait_ge(a_lo, KD + 2 * b + 2)
                    if half == 0 or b < 2:
                        rows_block(O0 + 4 * half + b, b, 4 * half, 1, o1_mm if b == 3 else None)
                    elif b == 2:
                        rows_block(O0 + 4 * half + b, b, 4 * half, 2, o1_mm)
                    if half == 0 and b == 0:
                        pe.wait_ge(y_free, 8)
                        gate_row(dg1, 6, 1)
                if half == 0:
                    pe.wait_ge(g_row, 1)
            transposes(True)
            side_by_side(W0, 2, 2 * KD, KD + 2)
            for h in range(2, PH):
                pe.wait_ge(z_act, len(by_act) + h - 1)
                tile(W0 + h, bank[h % 2][:, :])
            pe.wait_ge(small_in, 96)
            pe.wait_ge(z_act, len(by_act) + PH)

            def first_product(c, slot, kds=range(KD)):
                if kds[0] == 0:
                    pe.wait_ge(u_lo, c + 1)
                    need(pe, gel_r, c - 1)
                for kd in kds:
                    w = slice(kd * P, (kd + 1) * P)
                    last = three(bank[slot % 2][:, :], whi[:, slot % 2, w], wlo[:, slot % 2, w],
                                 act_hi[:, kd, :], act_lo[:, kd, :], kd == 0, kd == KD - 1)
                if kds[-1] == KD - 1:
                    last.then_inc(u_mm, 1)

            def retrieval_scores(t):
                need(pe, sc_read, t)
                for h in range(PH):
                    last = mm(bank[4 + h // 2][:, (h % 2) * 256:(h % 2 + 1) * 256], qT[:, h, t * P:(t + 1) * P],
                              keys[:], start=True, stop=True)
                last.then_inc(sc_mm, 1)

            def sel_T(t):
                pe.wait_ge(sel_r, t + 1)
                pe.wait_ge(gt_sb, NBT * t + 2)
                for r in range(2):
                    last = nc.tensor.transpose(bank[2][:, r * P:(r + 1) * P],
                                               sel[:, r, :, :].rearrange("p h k -> p (h k)"), ident[:])
                last.then_inc(selT_mm, 1)

            def token_gates(t, b):
                n = NBT * t + b
                pe.wait_ge(onem_r, n + 1)
                pe.wait_ge(gt_sb, n + 1)
                if b == 0:
                    pe.wait_ge(selT_sb, t + 1)
                row = one[b % OH]
                for j in range(TOK):
                    last = mm(bank[2 + b % 2][:, j * NK:(j + 1) * NK], row[:, 0, j, :], row[:, 1, j, :],
                              start=True, stop=True)
                last.then_inc(gt_mm, 1)

            def selecting(t, c0, p0):
                for j in range(PRE_T):
                    first_product(c0 + j, (p0 + j) % PS)
                    if j == PRE_T // 2 - 1 and t + 1 < TT:
                        retrieval_scores(t + 1)

            def laying(t, c0, p0):
                if t == TT - 1:
                    first_product(c0, p0 % PS, range(KD // 2))
                for b in range(NBT):
                    token_gates(t, b)
                    if t == TT - 1 and b < 8:
                        if b % 4 == 3:
                            first_product(c0, p0 % PS, range(b // 4 * 2 + 4, b // 4 * 2 + 6))
                    elif b % 2 == 1:
                        first_product(c0 + b // 8, (p0 + b // 8) % PS, range(b % 8 - 1, b % 8 + 1))

            pe.sem_inc(gt_mm, OH)
            retrieval_scores(0)
            selecting(0, 0, 0)
            sel_T(0)
            for t in range(TT - 1):
                c0 = PRE_T + PER * t
                selecting(t + 1, c0, c0)
                laying(t, c0 + PRE_T, c0 + PRE_T)
                sel_T(t + 1)
            laying(TT - 1, PRE - FILL - PRE_G, PRE - FILL - PRE_G)
            for c in range(PRE - FILL, PRE):
                first_product(c, c % PS)
            pe.wait_ge(gt_sb, T // TOK + 2)

            def second_product(g, k, half):
                n = half * GR + k
                pe.wait_ge(v_lo, 16 * g + n + 1)
                pe.wait_ge(w_lo, GR * g + k + 1)
                for t in range(TT):
                    if k == 0:
                        need(pe, pv_add, 8 * g + 4 * half + t - 3)
                    c = slice(t * P, (t + 1) * P)
                    last = three(bank[2 + t][:, :], eh[:, k, c], el[:, k, c], vhi[:, n % VR, :], vlo[:, n % VR, :],
                                 k == 0, k == GR - 1)
                    if k == GR - 1 and t < TT - 1:
                        last.then_inc(pv_mm, 1)
                last.then_inc(v_mm, 1)

            def group(g, with_u, last=False):
                for k in range(GR):
                    if with_u:
                        first_product(GR * g + LEAD + k, k)
                    second_product(g, k, 0)
                    if last and k == 1:
                        gate_row(dg2, 0, 2)
                if not last:
                    for k in range(GR):
                        second_product(g, k, 1)

            for g in range(FIRST):
                group(g, u_beside(g))
            with pe.Fori(0, LOOP) as it:
                group(2 * it + FIRST, True)
                group(2 * it + (FIRST + 1), True)
            group(NG - 3, True)
            group(NG - 2, False)
            group(NG - 1, False, True)
            g = NG - 1
            for t in range(TT):
                c = slice(t * P, (t + 1) * P)
                need(pe, pv_add, 8 * g + 4 + t - 3)
                for k in range(GR):
                    if t == 0:
                        pe.wait_ge(v_lo, 16 * g + GR + k + 1)
                    h, l = v_slot(GR + k, True)
                    ins = three(bank[2 + t][:, :], eh[:, k, c], el[:, k, c], h, l, k == 0, k == GR - 1)
                ins.then_inc(pv_mm, 1)


def kernel(**inputs):
    import numpy as np
    import concourse.bacc as _bacc
    from concourse import mybir as _mybir
    from concourse.bass_utils import run_bass_kernel_spmd as _run

    a = {k: np.asarray(v) for k, v in inputs.items()}

    def tiles(w):
        return w.reshape(KD, P, -1, P).transpose(2, 1, 0, 3).reshape(-1, P, D)

    def branch(w):
        return w.reshape(AT, P, 4, 2, P).transpose(2, 1, 3, 0, 4).reshape(4, P, D)

    w_in = a["w_in"][0]
    o = [0, AW, 2 * AW, 3 * AW, 3 * AW + HEADS]
    ca, cbc = o[4], o[4] + CC
    gates = cbc + CC
    wv = w_in[:, o[2]:o[3]].reshape(4, 2, P, AW).transpose(0, 2, 1, 3).reshape(4, P, D)
    pairs = np.stack([tiles(w_in[:, ca:cbc]), tiles(w_in[:, cbc:gates])], 1).reshape(2 * CT, P, D)
    branches = np.concatenate([branch(a["w_attn_out"][0]), branch(a["w_conv_out"][0])])
    w_out = a["w_out"][0].reshape(4, 2, P, 2, HALF).transpose(3, 0, 2, 1, 4).reshape(8, P, D)
    wblk = np.concatenate([
        tiles(w_in[:, o[0]:o[1]]), tiles(w_in[:, o[1]:o[2]]), tiles(w_in[:, o[3]:o[3] + P]), wv, pairs,
        tiles(w_in[:, gates:]), branches, w_out, tiles(a["peer_wq"][0])])
    arrays = {
        "x": a["x"][0],
        "cb": a["c"],
        "b_modc": a["b_mod"][0].reshape(MODT, P).T,
        "w_modt": a["w_mod"][0].T.reshape(MODT, P, D),
        "wblk": wblk,
        "b_fc": a["b_f"][0][:, None],
        "conv_wc": a["conv_w"][0].reshape(TAPS, CT, P).transpose(2, 1, 0),
        "conv_vec": np.stack([a["conv_b"][0], a["conv_ln_g"][0], a["conv_ln_b"][0]]).reshape(3, CT, P).transpose(2, 0, 1),
        "keys_t": a["peer_sub_keys"][0].transpose(0, 2, 1),
        "u_t": a["peer_u"][0].reshape(CH, P, KD, P).transpose(0, 3, 2, 1).reshape(CH, P, D),
        "v_tab": a["peer_v"][0],
        "rows": np.stack([a["ln1_g"][0], a["ln1_b"][0], a["ln2_g"][0], a["ln2_b"][0]]),
    }
    nc = _bacc.Bacc("TRN2", target_bir_lowering=False, num_devices=1)
    feeds, args = {}, []
    for name, arr in arrays.items():
        arr = np.ascontiguousarray(arr)
        feeds[f"in_{name}_dram"] = arr
        args.append(nc.dram_tensor(f"in_{name}_dram", arr.shape, _mybir.dt.from_np(arr.dtype), kind="ExternalInput").ap())
    args.append(nc.dram_tensor("out_0_dram", (T, D), F32, kind="ExternalOutput").ap())
    build(nc, *args)
    r = _run(nc, [feeds], core_ids=[0])
    return r.results[0]["out_0_dram"].reshape(1, T, D)
```
